# Optimizing a Trainium2 kernel written in Bass

```python
import math
import jax, jax.numpy as jnp
from jax import lax
import numpy as np

D_MODEL = 1024
BATCH = 1
SEQ = 256
DEPTH = 1

N_MEM = 256
MAX_POS_OFFSET = 1024
BLOCK = 128
RMS_EPS = 1e-6
NEG_INF = -1e30

MLA_HEADS = 8
MLA_NOPE = 64
MLA_ROPE = 32
MLA_V = 64
MLA_QK_DIM = MLA_NOPE + MLA_ROPE
MLA_Q_RANK = 384
MLA_KV_RANK = 256
ROPE_THETA = 10000.0
MLA_WIDTH = MLA_HEADS * MLA_V

DIL_PAIRS = ((128, 1), (512, 4), (2048, 16))
DIL_GROUPS = 3
DIL_HEADS_PER_GROUP = 4
DIL_HEADS = DIL_GROUPS * DIL_HEADS_PER_GROUP
DIL_HEAD_DIM = 128
DIL_WIDTH = DIL_HEADS_PER_GROUP * DIL_HEAD_DIM

MEM_HEADS = 4
MEM_HEAD_DIM = 128
MEM_WIDTH = MEM_HEADS * MEM_HEAD_DIM

N_BRANCH = 3

D_FF = 2816
CONV_WIDTH = 3

OFF_Q = MLA_Q_RANK
OFF_KV = OFF_Q + MLA_KV_RANK
OFF_KR = OFF_KV + MLA_ROPE
OFF_DIL = OFF_KR + 3 * DIL_HEADS * DIL_HEAD_DIM
OFF_MEMQ = OFF_DIL + MEM_WIDTH
D_IN = OFF_MEMQ + N_BRANCH * D_MODEL


def _rms_norm(x, g):
    xf = x.astype(jnp.float32)
    y = xf * lax.rsqrt(jnp.mean(xf * xf, axis=-1, keepdims=True) + RMS_EPS)
    return (y * g.astype(jnp.float32)).astype(x.dtype)

def _rope(t, positions):
    half = t.shape[-1] // 2
    inv_freq = ROPE_THETA ** (-jnp.arange(half, dtype=jnp.float32) / half)
    ang = positions.astype(jnp.float32)[:, :, None, None] * inv_freq
    cos, sin = jnp.cos(ang), jnp.sin(ang)
    t1 = t[..., :half].astype(jnp.float32)
    t2 = t[..., half:].astype(jnp.float32)
    return jnp.concatenate([t1 * cos - t2 * sin, t2 * cos + t1 * sin], axis=-1).astype(t.dtype)

def _alibi_slopes(n):
    return jnp.exp2(-8.0 * jnp.arange(1, n + 1, dtype=jnp.float32) / n)

def _mla(c_q, c_kv, k_rope, positions, q_norm, w_uq, kv_norm, w_ukv):
    B, S, _ = c_q.shape
    q = (_rms_norm(c_q, q_norm) @ w_uq).reshape(B, S, MLA_HEADS, MLA_QK_DIM)
    q = jnp.concatenate([q[..., :MLA_NOPE], _rope(q[..., MLA_NOPE:], positions)], axis=-1)
    kv = (_rms_norm(c_kv, kv_norm) @ w_ukv).reshape(B, S, MLA_HEADS, MLA_NOPE + MLA_V)
    k_pe = jnp.broadcast_to(_rope(k_rope[:, :, None, :], positions), (B, S, MLA_HEADS, MLA_ROPE))
    k = jnp.concatenate([kv[..., :MLA_NOPE], k_pe], axis=-1)
    v = kv[..., MLA_NOPE:]
    n_blk = S // BLOCK
    q_blocks = (q * MLA_QK_DIM ** -0.5).reshape(B, n_blk, BLOCK, MLA_HEADS, MLA_QK_DIM).transpose(1, 0, 2, 3, 4)
    key_idx = jnp.arange(S)

    def attend(args):
        q_blk, blk = args
        s = jnp.einsum('bqhd,bkhd->bhqk', q_blk, k).astype(jnp.float32)
        q_idx = blk * BLOCK + jnp.arange(BLOCK)
        s = jnp.where(key_idx[None, :] <= q_idx[:, None], s, NEG_INF)
        p = jax.nn.softmax(s, axis=-1).astype(v.dtype)
        return jnp.einsum('bhqk,bkhd->bqhd', p, v)

    o = lax.map(attend, (q_blocks, jnp.arange(n_blk)))
    return o.transpose(1, 0, 2, 3, 4).reshape(B, S, MLA_WIDTH)

def _dilated_group(q, k, v, window, dilation, slopes):
    B, S, H, dh = q.shape
    span = window // dilation
    L = S // dilation
    n_blk = -(-L // BLOCK)
    Lp = n_blk * BLOCK

    def to_blocks(t):
        t = t.reshape(B, L, dilation, H, dh).transpose(0, 2, 3, 1, 4)
        t = jnp.pad(t, ((0, 0), (0, 0), (0, 0), (0, Lp - L), (0, 0)))
        return t.reshape(B, dilation, H, n_blk, BLOCK, dh)

    def band(t):
        prev = jnp.pad(t, ((0, 0), (0, 0), (0, 0), (1, 0), (0, 0), (0, 0)))[:, :, :, :-1]
        return jnp.concatenate([prev, t], axis=4)

    qb = to_blocks(q) * dh ** -0.5
    kb = band(to_blocks(k))
    vb = band(to_blocks(v))
    s = jnp.einsum('bdhnqe,bdhnke->bdhnqk', qb, kb).astype(jnp.float32)
    dist = jnp.arange(BLOCK)[:, None] + BLOCK - jnp.arange(2 * BLOCK)[None, :]
    key_sub = jnp.arange(n_blk)[:, None, None] * BLOCK - BLOCK + jnp.arange(2 * BLOCK)[None, None, :]
    valid = (dist >= 0) & (dist <= span) & (key_sub >= 0)
    alibi = -slopes.astype(jnp.float32)[:, None, None, None] * (dist * dilation).astype(jnp.float32)
    s = jnp.where(valid, s + alibi, NEG_INF)
    m = jnp.max(s, axis=-1, keepdims=True)
    e = jnp.exp(s - m)
    den = jnp.sum(e, axis=-1, keepdims=True)
    o = jnp.einsum('bdhnqk,bdhnke->bdhnqe', (e / den).astype(v.dtype), vb)
    lse = (m + jnp.log(den))[..., 0]
    o = o.reshape(B, dilation, H, Lp, dh)[:, :, :, :L].transpose(0, 3, 1, 2, 4).reshape(B, S, H, dh)
    lse = lse.reshape(B, dilation, H, Lp)[..., :L].transpose(0, 3, 1, 2).reshape(B, S, H)
    return o, lse

def _dilated_mixture(dil_qkv):
    B, S, _ = dil_qkv.shape
    qkv = dil_qkv.reshape(B, S, 3, DIL_GROUPS, DIL_HEADS_PER_GROUP, DIL_HEAD_DIM)
    slopes = _alibi_slopes(DIL_HEADS).reshape(DIL_HEADS_PER_GROUP, DIL_GROUPS).T
    outs, lses = [], []
    for g, (window, dilation) in enumerate(DIL_PAIRS):
        o, lse = _dilated_group(qkv[:, :, 0, g], qkv[:, :, 1, g], qkv[:, :, 2, g], window, dilation, slopes[g])
        outs.append(o)
        lses.append(lse)
    w = jax.nn.softmax(jnp.stack(lses, axis=0), axis=0)
    o_stack = jnp.stack(outs, axis=0)
    o = jnp.sum(w[..., None].astype(o_stack.dtype) * o_stack, axis=0)
    return o.reshape(B, S, DIL_WIDTH)

def _mem_attention(q, mem, g_mem, w_mem_kv):
    B, S, _ = q.shape
    M = mem.shape[1]
    kv = (_rms_norm(mem, g_mem) @ w_mem_kv).reshape(B, M, 2, MEM_HEADS, MEM_HEAD_DIM)
    qh = q.reshape(B, S, MEM_HEADS, MEM_HEAD_DIM) * MEM_HEAD_DIM ** -0.5
    s = jnp.einsum('bshd,bmhd->bhsm', qh, kv[:, :, 0]).astype(jnp.float32)
    p = jax.nn.softmax(s, axis=-1).astype(q.dtype)
    return jnp.einsum('bhsm,bmhd->bshd', p, kv[:, :, 1]).reshape(B, S, MEM_WIDTH)

def _conv_ffn(h, w_up, conv_w, conv_b, w_down):
    S = h.shape[1]
    u = h @ w_up
    u_pad = jnp.pad(u, ((0, 0), (CONV_WIDTH - 1, 0), (0, 0)))
    z = conv_b + conv_w[0] * u_pad[:, 0:S]
    for j in range(1, CONV_WIDTH):
        z = z + conv_w[j] * u_pad[:, j:j + S]
    gate, val = z[..., :D_FF], z[..., D_FF:]
    return (jax.nn.silu(gate) * val) @ w_down

def _layer(x, mem, positions, g_pre_mix, w_in, b_gate, mla_q_norm, w_uq, mla_kv_norm, w_ukv, g_mem, w_mem_kv,
           w_br_mla, w_br_dil, w_br_mem, w_o, g_post_mix, g_pre_ffn, w_ffn_up, conv_w, conv_b, w_ffn_down, g_post_ffn):
    B, S, _ = x.shape
    h = _rms_norm(x, g_pre_mix)
    proj = h @ w_in
    y_mla = _mla(proj[..., :OFF_Q], proj[..., OFF_Q:OFF_KV], proj[..., OFF_KV:OFF_KR], positions,
                 mla_q_norm, w_uq, mla_kv_norm, w_ukv)
    y_dil = _dilated_mixture(proj[..., OFF_KR:OFF_DIL])
    y_mem = _mem_attention(proj[..., OFF_DIL:OFF_MEMQ], mem, g_mem, w_mem_kv)
    gates = jax.nn.sigmoid((proj[..., OFF_MEMQ:] + b_gate).astype(jnp.float32)).astype(x.dtype)
    gates = gates.reshape(B, S, N_BRANCH, D_MODEL)
    merged = (gates[:, :, 0] * (y_mla @ w_br_mla)
              + gates[:, :, 1] * (y_dil @ w_br_dil)
              + gates[:, :, 2] * (y_mem @ w_br_mem))
    x = x + _rms_norm(merged @ w_o, g_post_mix)
    h2 = _rms_norm(x, g_pre_ffn)
    x = x + _rms_norm(_conv_ffn(h2, w_ffn_up, conv_w, conv_b, w_ffn_down), g_post_ffn)
    return x

def first_inputs(seed: int = 0) -> dict:
    key = jax.random.key(seed)
    ks = jax.random.split(key, 24)
    f32 = jnp.float32

    def dense(k, fan_in, fan_out):
        return jax.random.normal(k, (DEPTH, fan_in, fan_out), f32) * fan_in ** -0.5

    def gain(k, n):
        return 1.0 + 0.05 * jax.random.normal(k, (DEPTH, n), f32)

    x = jax.random.normal(ks[0], (BATCH, SEQ, D_MODEL), f32)
    mem = jax.random.normal(ks[1], (BATCH, N_MEM, D_MODEL), f32)
    offset = jax.random.randint(ks[2], (BATCH, 1), 0, MAX_POS_OFFSET, dtype=jnp.int32)
    positions = (offset + jnp.arange(SEQ, dtype=jnp.int32)[None, :]).astype(jnp.int32)
    return {
        "x": x,
        "mem": mem,
        "positions": positions,
        "g_pre_mix": gain(ks[3], D_MODEL),
        "w_in": dense(ks[4], D_MODEL, D_IN),
        "b_gate": 0.1 * jax.random.normal(ks[5], (DEPTH, N_BRANCH * D_MODEL), f32),
        "mla_q_norm": gain(ks[6], MLA_Q_RANK),
        "w_uq": dense(ks[7], MLA_Q_RANK, MLA_HEADS * MLA_QK_DIM),
        "mla_kv_norm": gain(ks[8], MLA_KV_RANK),
        "w_ukv": dense(ks[9], MLA_KV_RANK, MLA_HEADS * (MLA_NOPE + MLA_V)),
        "g_mem": gain(ks[10], D_MODEL),
        "w_mem_kv": dense(ks[11], D_MODEL, 2 * MEM_WIDTH),
        "w_br_mla": dense(ks[12], MLA_WIDTH, D_MODEL),
        "w_br_dil": dense(ks[13], DIL_WIDTH, D_MODEL),
        "w_br_mem": dense(ks[14], MEM_WIDTH, D_MODEL),
        "w_o": dense(ks[15], D_MODEL, D_MODEL),
        "g_post_mix": gain(ks[16], D_MODEL),
        "g_pre_ffn": gain(ks[17], D_MODEL),
        "w_ffn_up": dense(ks[18], D_MODEL, 2 * D_FF),
        "conv_w": jax.random.normal(ks[19], (DEPTH, CONV_WIDTH, 2 * D_FF), f32) * CONV_WIDTH ** -0.5,
        "conv_b": 0.01 * jax.random.normal(ks[20], (DEPTH, 2 * D_FF), f32),
        "w_ffn_down": dense(ks[21], D_FF, D_MODEL),
        "g_post_ffn": gain(ks[22], D_MODEL),
    }

def first_block(x, mem, positions, g_pre_mix, w_in, b_gate, mla_q_norm, w_uq, mla_kv_norm, w_ukv, g_mem, w_mem_kv,
              w_br_mla, w_br_dil, w_br_mem, w_o, g_post_mix, g_pre_ffn, w_ffn_up, conv_w, conv_b, w_ffn_down,
              g_post_ffn):
    for l in range(DEPTH):
        x = _layer(x, mem, positions, g_pre_mix[l], w_in[l], b_gate[l], mla_q_norm[l], w_uq[l], mla_kv_norm[l],
                   w_ukv[l], g_mem[l], w_mem_kv[l], w_br_mla[l], w_br_dil[l], w_br_mem[l], w_o[l], g_post_mix[l],
                   g_pre_ffn[l], w_ffn_up[l], conv_w[l], conv_b[l], w_ffn_down[l], g_post_ffn[l])
    return x


DEPTH_2 = 2

D_RG = D_MODEL
RG_HEADS = 8
RG_HEAD_DIM = D_RG // RG_HEADS
D_ML = D_MODEL
ML_HEADS = 4
ML_HEAD_DIM = D_ML // ML_HEADS
D_MIX = D_RG + D_ML
D_IN_2 = 2 * D_RG + 3 * D_ML
CONV_WIDTH_2 = 4
RG_C = 8.0
ML_CHUNK = 128
EPS = 1e-6


def rms_norm(x, g):
    x32 = x.astype(jnp.float32)
    y = x32 * lax.rsqrt(jnp.mean(x32 * x32, axis=-1, keepdims=True) + EPS)
    return (y * g.astype(jnp.float32)).astype(x.dtype)

def causal_depthwise_conv(x, w, b):
    ch = x.shape[-1]
    y = lax.conv_general_dilated(
        x, w[:, None, :].astype(x.dtype), window_strides=(1,),
        padding=[(CONV_WIDTH_2 - 1, 0)], dimension_numbers=("NWC", "WIO", "NWC"),
        feature_group_count=ch)
    return y + b.astype(x.dtype)

def block_diag(x, w):
    h, dh, dout = w.shape
    xb = x.reshape(x.shape[:-1] + (h, dh))
    return jnp.einsum("bshd,hde->bshe", xb, w).reshape(x.shape[:-1] + (h * dout,))

def rglru(x, w_a, b_a, w_x, b_x, lam):
    r = jax.nn.sigmoid(block_diag(x, w_a) + b_a).astype(jnp.float32)
    i = jax.nn.sigmoid(block_diag(x, w_x) + b_x).astype(jnp.float32)
    log_a = -RG_C * r * jax.nn.softplus(-lam.astype(jnp.float32))
    a = jnp.exp(log_a)
    u = jnp.sqrt(-jnp.expm1(2.0 * log_a)) * (i * x.astype(jnp.float32))

    def combine(lhs, rhs):
        a1, b1 = lhs
        a2, b2 = rhs
        return a1 * a2, a2 * b1 + b2

    _, h = lax.associative_scan(combine, (a, u), axis=1)
    return h.astype(x.dtype)

def mlstm_chunkwise(q, k, v, log_i, log_f):
    bsz, s_len, nh, dh = q.shape
    nc = s_len // ML_CHUNK

    def to_chunks(t):
        return t.reshape(bsz, nc, ML_CHUNK, nh, dh).transpose(1, 0, 3, 2, 4)

    def gate_chunks(t):
        return t.reshape(bsz, nc, ML_CHUNK, nh).transpose(1, 0, 3, 2)

    causal = jnp.tril(jnp.ones((ML_CHUNK, ML_CHUNK), dtype=bool))

    def step(carry, xs):
        c_st, n_st, m_st = carry
        qc, kc, vc, li, lf = xs
        b = jnp.cumsum(lf, axis=-1)
        b_last = b[..., -1]
        d = jnp.where(causal, b[..., :, None] - b[..., None, :] + li[..., None, :], -jnp.inf)
        m_inter = b + m_st[..., None]
        m_t = jnp.maximum(m_inter, jnp.max(d, axis=-1))
        w_intra = jnp.exp(d - m_t[..., None])
        w_inter = jnp.exp(m_inter - m_t)
        s = jnp.einsum("bhtk,bhsk->bhts", qc, kc) * w_intra
        num = (jnp.einsum("bhts,bhsv->bhtv", s, vc)
               + w_inter[..., None] * jnp.einsum("bhtk,bhkv->bhtv", qc, c_st))
        den = jnp.sum(s, axis=-1) + w_inter * jnp.einsum("bhtk,bhk->bht", qc, n_st)
        h = num / jnp.maximum(jnp.abs(den), jnp.exp(-m_t))[..., None]
        g = b_last[..., None] - b + li
        m_new = jnp.maximum(b_last + m_st, jnp.max(g, axis=-1))
        w_state = jnp.exp(g - m_new[..., None])
        decay = jnp.exp(b_last + m_st - m_new)
        kw = kc * w_state[..., None]
        c_new = decay[..., None, None] * c_st + jnp.einsum("bhsk,bhsv->bhkv", kw, vc)
        n_new = decay[..., None] * n_st + jnp.sum(kw, axis=2)
        return (c_new, n_new, m_new), h

    init = (jnp.zeros((bsz, nh, dh, dh), jnp.float32),
            jnp.zeros((bsz, nh, dh), jnp.float32),
            jnp.zeros((bsz, nh), jnp.float32))
    _, h = lax.scan(step, init, (to_chunks(q), to_chunks(k), to_chunks(v),
                                 gate_chunks(log_i), gate_chunks(log_f)))
    return h.transpose(1, 0, 3, 2, 4).reshape(bsz, s_len, nh, dh)

def mlstm_branch(xm, o_pre, conv_w, conv_b, w_q, w_k, w_v, w_if, b_if, head_g):
    bsz, s_len, _ = xm.shape
    xc = jax.nn.silu(causal_depthwise_conv(xm, conv_w, conv_b))
    q = block_diag(xc, w_q)
    k = block_diag(xc, w_k)
    v = block_diag(xm, w_v)
    gates = (jnp.concatenate([q, k, v], axis=-1) @ w_if + b_if).astype(jnp.float32)
    log_i = gates[..., :ML_HEADS]
    log_f = jax.nn.log_sigmoid(gates[..., ML_HEADS:])

    def heads(t):
        return t.reshape(bsz, s_len, ML_HEADS, ML_HEAD_DIM).astype(jnp.float32)

    cell = mlstm_chunkwise(heads(q), heads(k) * (ML_HEAD_DIM ** -0.5), heads(v), log_i, log_f)
    h = jax.nn.sigmoid(heads(o_pre)) * cell
    h = h * lax.rsqrt(jnp.mean(h * h, axis=-1, keepdims=True) + EPS)
    return (h.reshape(bsz, s_len, D_ML) * head_g.astype(jnp.float32)).astype(xm.dtype)

def second_inputs(seed: int = 0) -> dict:
    key = jax.random.key(seed)
    ks = jax.random.split(key, 24)
    f32 = jnp.float32

    def nrm(k, shape, scale):
        return jax.random.normal(k, shape, f32) * scale

    x = jax.random.normal(ks[0], (BATCH, SEQ, D_MODEL), f32)
    c = jax.random.normal(ks[1], (BATCH, D_MODEL), f32)
    norm_g = 1.0 + nrm(ks[2], (DEPTH_2, D_MODEL), 0.02)
    w_ada = nrm(ks[3], (DEPTH_2, D_MODEL, 3 * D_MODEL), 0.3 * D_MODEL ** -0.5)
    b_ada = nrm(ks[4], (DEPTH_2, 3 * D_MODEL), 0.02)
    w_in = nrm(ks[5], (DEPTH_2, D_MODEL, D_IN_2), D_MODEL ** -0.5)
    rg_conv_w = nrm(ks[6], (DEPTH_2, CONV_WIDTH_2, D_RG), CONV_WIDTH_2 ** -0.5)
    rg_conv_b = nrm(ks[7], (DEPTH_2, D_RG), 0.02)
    rg_w_a = nrm(ks[8], (DEPTH_2, RG_HEADS, RG_HEAD_DIM, RG_HEAD_DIM), RG_HEAD_DIM ** -0.5)
    rg_b_a = nrm(ks[9], (DEPTH_2, D_RG), 0.02)
    rg_w_x = nrm(ks[10], (DEPTH_2, RG_HEADS, RG_HEAD_DIM, RG_HEAD_DIM), RG_HEAD_DIM ** -0.5)
    rg_b_x = nrm(ks[11], (DEPTH_2, D_RG), 0.02)
    a_c = jax.random.uniform(ks[12], (DEPTH_2, D_RG), f32, 0.9, 0.999)
    a0 = a_c ** (1.0 / RG_C)
    rg_lambda = jnp.log(a0) - jnp.log1p(-a0)
    ml_conv_w = nrm(ks[13], (DEPTH_2, CONV_WIDTH_2, D_ML), CONV_WIDTH_2 ** -0.5)
    ml_conv_b = nrm(ks[14], (DEPTH_2, D_ML), 0.02)
    ml_w_q = nrm(ks[15], (DEPTH_2, ML_HEADS, ML_HEAD_DIM, ML_HEAD_DIM), ML_HEAD_DIM ** -0.5)
    ml_w_k = nrm(ks[16], (DEPTH_2, ML_HEADS, ML_HEAD_DIM, ML_HEAD_DIM), ML_HEAD_DIM ** -0.5)
    ml_w_v = nrm(ks[17], (DEPTH_2, ML_HEADS, ML_HEAD_DIM, ML_HEAD_DIM), ML_HEAD_DIM ** -0.5)
    ml_w_if = nrm(ks[18], (DEPTH_2, 3 * D_ML, 2 * ML_HEADS), 0.1 * (3 * D_ML) ** -0.5)
    b_i = nrm(ks[19], (DEPTH_2, ML_HEADS), 0.1) - 1.0
    b_f = jnp.linspace(3.0, 6.0, ML_HEADS, dtype=f32)[None, :] + nrm(ks[20], (DEPTH_2, ML_HEADS), 0.1)
    ml_b_if = jnp.concatenate([b_i, b_f], axis=-1)
    ml_norm_g = 1.0 + nrm(ks[21], (DEPTH_2, D_ML), 0.02)
    w_out = nrm(ks[22], (DEPTH_2, D_MIX, D_MODEL), D_MIX ** -0.5)
    final_g = 1.0 + nrm(ks[23], (D_MODEL,), 0.02)
    return {"x": x, "c": c, "norm_g": norm_g, "w_ada": w_ada, "b_ada": b_ada,
            "w_in": w_in, "rg_conv_w": rg_conv_w, "rg_conv_b": rg_conv_b,
            "rg_w_a": rg_w_a, "rg_b_a": rg_b_a, "rg_w_x": rg_w_x, "rg_b_x": rg_b_x,
            "rg_lambda": rg_lambda, "ml_conv_w": ml_conv_w, "ml_conv_b": ml_conv_b,
            "ml_w_q": ml_w_q, "ml_w_k": ml_w_k, "ml_w_v": ml_w_v, "ml_w_if": ml_w_if,
            "ml_b_if": ml_b_if, "ml_norm_g": ml_norm_g, "w_out": w_out, "final_g": final_g}

def second_block(x, c, norm_g, w_ada, b_ada, w_in, rg_conv_w, rg_conv_b, rg_w_a, rg_b_a,
              rg_w_x, rg_b_x, rg_lambda, ml_conv_w, ml_conv_b, ml_w_q, ml_w_k, ml_w_v,
              ml_w_if, ml_b_if, ml_norm_g, w_out, final_g):
    split_pts = [D_RG, 2 * D_RG, 2 * D_RG + D_ML, 2 * D_RG + 2 * D_ML]
    c_act = jax.nn.silu(c)
    for l in range(DEPTH_2):
        mod = c_act @ w_ada[l] + b_ada[l]
        shift, scale, gate = jnp.split(mod, 3, axis=-1)
        h = rms_norm(x, norm_g[l]) * (1.0 + scale[:, None, :]) + shift[:, None, :]
        u = h @ w_in[l]
        rg_x, rg_z, ml_x, ml_o, ml_z = jnp.split(u, split_pts, axis=-1)
        y_rg = rglru(causal_depthwise_conv(rg_x, rg_conv_w[l], rg_conv_b[l]),
                     rg_w_a[l], rg_b_a[l], rg_w_x[l], rg_b_x[l], rg_lambda[l]) * jax.nn.silu(rg_z)
        y_ml = mlstm_branch(ml_x, ml_o, ml_conv_w[l], ml_conv_b[l], ml_w_q[l], ml_w_k[l],
                            ml_w_v[l], ml_w_if[l], ml_b_if[l], ml_norm_g[l]) * jax.nn.silu(ml_z)
        y = jnp.concatenate([y_rg, y_ml], axis=-1) @ w_out[l]
        x = x + gate[:, None, :] * y
    return rms_norm(x, final_g)


def setup_inputs(seed=0):
    out = dict(first_inputs(seed))
    for name, value in second_inputs(seed + 1).items():
        if name != "x":
            out[name + "_2"] = value
    return out


def reference(
    x, mem, positions, g_pre_mix, w_in, b_gate, mla_q_norm, w_uq, mla_kv_norm, w_ukv, g_mem,
    w_mem_kv, w_br_mla, w_br_dil, w_br_mem, w_o, g_post_mix, g_pre_ffn, w_ffn_up, conv_w,
    conv_b, w_ffn_down, g_post_ffn, c_2, norm_g_2, w_ada_2, b_ada_2, w_in_2, rg_conv_w_2,
    rg_conv_b_2, rg_w_a_2, rg_b_a_2, rg_w_x_2, rg_b_x_2, rg_lambda_2, ml_conv_w_2, ml_conv_b_2,
    ml_w_q_2, ml_w_k_2, ml_w_v_2, ml_w_if_2, ml_b_if_2, ml_norm_g_2, w_out_2, final_g_2,
):
    x = first_block(
        x, mem, positions, g_pre_mix, w_in, b_gate, mla_q_norm, w_uq, mla_kv_norm, w_ukv, g_mem,
        w_mem_kv, w_br_mla, w_br_dil, w_br_mem, w_o, g_post_mix, g_pre_ffn, w_ffn_up, conv_w,
        conv_b, w_ffn_down, g_post_ffn,
    )
    return second_block(
        x, c_2, norm_g_2, w_ada_2, b_ada_2, w_in_2, rg_conv_w_2, rg_conv_b_2, rg_w_a_2,
        rg_b_a_2, rg_w_x_2, rg_b_x_2, rg_lambda_2, ml_conv_w_2, ml_conv_b_2, ml_w_q_2, ml_w_k_2,
        ml_w_v_2, ml_w_if_2, ml_b_if_2, ml_norm_g_2, w_out_2, final_g_2,
    )


_drawn_inputs = setup_inputs


def setup_inputs(seed=0):
    import zlib

    import numpy as np

    out = dict(_drawn_inputs(seed))
    spreads = {}
    factors = {'mla_q_norm': 2.956,
     'g_mem': 3.526,
     'conv_b': 6.75,
     'norm_g_2': 8.0,
     'b_ada_2': 4.279,
     'rg_conv_b_2': 55.853,
     'rg_w_a_2': 5.336,
     'rg_b_a_2': 64.0,
     'rg_w_x_2': 2.813,
     'rg_b_x_2': 64.0,
     'rg_lambda_2': 2.944,
     'ml_conv_b_2': 8.0,
     'ml_w_if_2': 8.0,
     'ml_norm_g_2': 8.0,
     'final_g_2': 8.349}
    for name, (base, spread) in spreads.items():
        noise = np.random.default_rng([zlib.crc32(name.encode()), seed]).standard_normal(out[name].shape)
        drawn = base * np.exp(spread * noise) if base else spread * noise
        out[name] = __import__('jax').numpy.asarray(drawn.astype(out[name].dtype))
    for name, factor in factors.items():
        out[name] = (out[name] * factor).astype(out[name].dtype)
    return out
```

```python
from contextlib import ExitStack, contextmanager

import concourse.bass as bass
import numpy as np
from concourse import mybir

F32 = mybir.dt.float32
F32R = mybir.dt.float32r
I32 = mybir.dt.int32
ACT = mybir.ActivationFunctionType
ALU = mybir.AluOpType
AX = mybir.AxisListType

P = 128
S = 256
D = 1024
KD = D // P
EPS = 1e-6
NEG = -1e30
UNIT = 1024
SLOTS = 4

HM, NOPE, ROPE, VM = 8, 64, 32, 64
KQ, KKV = 3, 2
GROUPS, HD, DH = 3, 4, 128
DILATION = (1, 4, 16)
SPAN = 128
FF = 2816
KF = FF // P
LAYERS = 2
HR = 8
HL = 4
RG_C = 8.0

_ORDER = (("memk", 4), ("memv", 4), ("latent", 6), ("qk", 24), ("v", 12), ("uq", 4), ("ukvk", 1), ("ukvv", 1),
          ("memq", 4), ("gates", 24), ("branch", 12), ("wo", 8), ("up", 2 * KF), ("down", KF))
_LAYER = (("in", 40), ("rg", 2), ("mlq", 2), ("mlk", 2), ("mlv", 2), ("out", 16))
U = {}
_at = 0
for _n, _c in _ORDER:
    U[_n] = _at
    _at += _c
LAYER0 = _at
for _n, _c in _LAYER:
    U[_n] = _at
    _at += _c
PER_LAYER = _at - LAYER0
NU = LAYER0 + LAYERS * PER_LAYER


def _owners():
    own = ["a"] * NU

    def put(first, what):
        own[first:first + len(what)] = list(what)

    put(U["memv"], ".a" * 2)
    put(U["latent"] + 5, "v")
    put(U["v"], ".a" * 6)
    put(U["uq"], "v" * 4)
    put(U["branch"], "v" * 12)
    put(U["wo"], "." * 7 + "a")
    put(U["up"], "v" * 2 * KF)
    put(U["down"], "." * (KF - 1) + "a")
    for lay in range(LAYERS):
        o = lay * PER_LAYER
        put(U["in"] + o, "v" * 16)
        put(U["mlk"] + o, "v" * 2)
        put(U["out"] + o, "." * 16)
    return own


OWNER = _owners()
TAKEN = {e: [sum(o == e for o in OWNER[:n + 1]) for n in range(NU)] for e in "av"}

LAYER_A = TAKEN["a"][LAYER0 + PER_LAYER] - TAKEN["a"][LAYER0]

_C1 = (("g_pre_mix", KD), ("g_mem", KD), ("q_norm", KQ), ("kv_norm", KKV), ("b_gate", 24), ("g_post_mix", KD),
       ("g_pre_ffn", KD), ("conv_w", 3 * 2 * KF), ("conv_b", 2 * KF), ("g_post_ffn", KD), ("c", KD),
       ("b_ada", 24 * LAYERS), ("freq", 1), ("sign", 1), ("final_g", KD))
_C2 = (("norm_g", KD), ("rg_w", 4 * KD), ("rg_b", KD), ("b_a", KD), ("b_x", KD), ("lam", KD), ("ml_w", 4 * KD),
       ("ml_b", KD), ("head_g", KD), ("b_if", 2 * HL), ("w_if", 24 * 2 * HL))


def _columns(spec):
    at, out = 0, {}
    for name, n in spec:
        out[name] = (at, n)
        at += n
    return out, at


C1, NP1 = _columns(_C1)
C2, NP2 = _columns(_C2)

NORMS = [(KD, True), (KD, True), (KQ, True), (KKV, True), (KD, False), (KD, True), (KD, False),
         (KD, True), (KD, True), (KD, False)]
N_MEM, N_X, N_CQ, N_CKV, N_MIX, N_FFN, N_FFN_OUT, N_LAYER, N_FINAL = 0, 1, 2, 3, 4, 5, 6, 7, 9
SPLIT_BEFORE = [sum(k for k, s in NORMS[:n] if s) for n in range(len(NORMS) + 1)]

FIRST_UNITS = [LAYER0 + lay * PER_LAYER + m for lay in range(LAYERS + 1) for m in range(3)]

JOBS_MLA, JOBS_DIL, JOBS_MEM = range(0, HM), range(HM, HM + HD), range(HM + HD, HM + 2 * HD)


def affine(need, limit):
    for d in {b - a for a, b in zip(need, need[1:])} | {0}:
        a = max(x - d * i for i, x in enumerate(need))
        if all(a + d * i <= y for i, y in enumerate(limit)):
            return a, d
    raise ValueError(f"no line between {need} and {limit}")


def program(nc, w_units, w_ada, x_in, mem_in, pos_in, par1_in, par2_in, out):
    ctx = ExitStack()
    with ctx:
        def sb(name, shape, dt=F32):
            return ctx.enter_context(nc.sbuf_tensor(name, shape, dt))

        def sem(name):
            return ctx.enter_context(nc.semaphore(name))

        raw = sb("raw", [P, SLOTS, UNIT])
        w_hi = sb("w_hi", [P, SLOTS, UNIT], F32R)
        w_lo = sb("w_lo", [P, SLOTS, UNIT], F32R)
        act = sb("act", [P, 24, 2, S], F32R)
        x = sb("x", [P, KD, S])
        ar_d = sb("ar_d", [P, 36, S])
        ar_g = sb("ar_g", [P, 24, S])
        ar_m = sb("ar_m", [P, 12, S])
        ar_p = sb("ar_p", [P, 3456])
        dist = sb("dist", [P, GROUPS, 384])
        causal = sb("causal", [P, 384])
        causal_t = sb("causal_t", [P, 384])
        ident = sb("ident", [P, P])
        ones = sb("ones", [P, P])
        std = sb("std", [P, S])
        rstd = sb("rstd", [P, S])
        par1 = sb("par1", [P, NP1])
        par2 = sb("par2", [P, NP2])
        mod = sb("mod", [P, 24 * LAYERS])
        cact = sb("cact", [P, KD])
        small = sb("small", [P, 64])
        tiny = sb("tiny", [P, 24])
        psum = ctx.enter_context(nc.psum_tensor("psum", [P, 8, 512], F32))
        eps = tiny[:, 0:1]
        halfpi = tiny[:, 1:2]

        def c1(name, j=0, n=1):
            at = C1[name][0]
            if isinstance(j, int):
                return par1[:, at + j:at + j + n]
            return par1[:, bass.ds(j + at, n)]

        def c2(name, j=0, n=1):
            at = C2[name][0]
            return par2[:, at + j:at + j + n]

        def flat(ap):
            return ap.rearrange("p a b -> p (a b)")

        memx = ar_d[:, 0:8, :]
        latent = ar_g[:, 0:5, :]
        qk_d = ar_d[:, 0:24, :]
        v_d = ar_d[:, 24:36, :].rearrange("p a b -> p (a b)").rearrange("p (s n) -> p s n", s=2)
        q_mla = ar_g[:, 0:8, :]
        k_mla = ar_g[:, 8:16, :]
        v_mla = flat(ar_g[:, 16:20, :]).rearrange("p (s n) -> p s n", s=2)
        cos_t = ar_g[:, 20, :]
        sin_t = ar_g[:, 21, :]
        rope_tmp = ar_g[:, 22:24, :]
        k_mem = ar_m[:, 0:4, :]
        v_mem = flat(ar_m[:, 4:8, :]).rearrange("p (s n) -> p s n", s=2)
        q_mem = ar_m[:, 8:12, :]
        ada = ar_p[:, 0:3072].rearrange("p (r n) -> p r n", r=3)
        s_sb = ar_p[:, 0:2304].rearrange("p (r n) -> p r n", r=2)
        pt_sb = ar_p[:, 2304:3456]
        gates = ar_g
        merged = ar_d[:, 0:8, :]
        y_f = ar_d[:, 8:16, :]
        sq = ar_d[:, 16:24, :]
        tn = ar_d[:, 24:32, :]
        late = ar_g[:, 0:6, :]
        z_up = ar_p[:, 0:1024].rearrange("p (r n) -> p r n", r=4)
        u_rg = ar_d[:, 0:8, :]
        xc = ar_d[:, 8:16, :]
        xm = ar_d[:, 16:24, :]
        so = ar_d[:, 24:32, :]
        zy = ar_g[:, 0:16, :]
        k_ml = ar_g[:, 16:24, :]
        q_ml = ar_m[:, 0:8, :]
        rg_r = xc
        rg_t = ar_p[:, 0:2048].rearrange("p (a b) -> p a b", b=S)
        rg_i = (ar_m[:, 8:12, :], ar_d[:, 32:36, :])
        v_ml = u_rg
        v_tok = flat(xm).rearrange("p (s n) -> p s n", s=2)
        sq_ml = xc
        row = [ar_p[0:HL, 2048 + S * i:2048 + S * (i + 1)] for i in range(5)]
        neg_row = flat(ar_m[0:HL, 8:10, :])
        gate_tok = small[:, 0:16].rearrange("p (s g) -> p s g", s=2)
        c_col = small[:, 16:24].rearrange("p (s h) -> p s h", s=2)
        w_ml = ar_p[:, 0:768].rearrange("p (r n) -> p r n", r=2)
        sw_ml = ar_p[:, 768:1536].rearrange("p (r n) -> p r n", r=2)
        floor_ml = ar_p[:, 1536:1792]
        den_ml = ar_p[:, 1792:2048]
        soft = tiny[:, 8:16]
        nsoft = tiny[:, 16:24]
        gain2 = small[:, 24:32]
        t8 = [small[:, 32 + 8 * i:40 + 8 * i] for i in range(4)]

        def bank(b):
            return psum[:, b, :]

        def half(b, m):
            return psum[:, b, m * S:(m + 1) * S]

        def stat(j, q, k):
            at = (j % 2) * 8 + k * 2
            return small[:, at:at + 2] if q is None else small[:, at + q:at + q + 1]

        def score_views(j):
            s = s_sb[:, j % 2, :]
            if j in JOBS_MLA:
                views = [s[:, 0:128], s[:, 128:384]]
            elif j in JOBS_DIL:
                s = s.rearrange("p (g n) -> p g n", g=3)
                views = [s[:, :, 0:128], s[:, :, 128:384]]
            else:
                return [(psum[:, j % 2, q * S:(q + 1) * S], s[:, q * S:(q + 1) * S]) for q in range(2)]
            return [(v, v) for v in views]

        def head_rows(j):
            if j in JOBS_MLA:
                return 64 * (j % 2), 64 * (j % 2) + 64, 8 + j // 2
            return 0, P, j - JOBS_DIL[0]

        raw_in = [sem(f"raw_in{r}") for r in range(SLOTS)]
        ada_in = [sem(f"ada_in{r}") for r in range(3)]
        x_in_s, mem_in_s, par_in, par2_in_s, pos_in_s, out_s = (sem(n) for n in (
            "x_landed", "mem_landed", "par1_landed", "par2_landed", "pos_landed", "out_landed"))
        hi_done, lo_done, unit_used = sem("hi_done"), sem("lo_done"), sem("unit_used")
        taken = {"a": sem("taken_act"), "v": sem("taken_dve")}
        ada_used, mod_done, cact_done = sem("ada_used"), sem("mod_done"), sem("cact_done")
        sq_done, ss_done, std_done, rstd_done = (sem(n) for n in ("sq_done", "ss_done", "std_done", "rstd_done"))
        tn_done, nh_done, nl_done, res_done = (sem(n) for n in ("tn_done", "nh_done", "nl_done", "res_done"))
        masks_done, tables_done, rope_done, k_pe_done = (sem(n) for n in (
            "masks_done", "tables_done", "rope_done", "k_pe_done"))
        angle_done, sine_done = sem("angle_done"), sem("sine_done")
        s_ready, m_ready, e_ready, p_ready, pt_ready, pt_copied, o_ready, oh_ready, ol_ready = (
            sem(n) for n in ("s_ready", "m_ready", "e_ready", "p_ready", "pt_ready", "pt_copied", "o_ready",
                             "oh_ready", "ol_ready"))
        merge_done, mh_done, merged_lo = sem("merge_done"), sem("mh_done"), sem("merged_lo")
        q_nope = sem("q_nope")
        z_init, z_free, silu_done, prod_done, ah_done, al_done = (sem(n) for n in (
            "z_init", "z_free", "silu_done", "prod_done", "ah_done", "al_done"))
        (xc_silu, xs_hi, xs_lo, rg_tanh, rg_exp, rg_arg, rg_sqrt, yr_done, yh_done, yl_done, sp_exp, sp_done,
         vt_ready, vt_copied, gt_ready, gt_done, gr_ready, f_abs, f_exp, rows_done, cc_ready, cc_done,
         mb_ready, wm_ready, we_ready, floor_ready, st_ready, sw_ready, num_ready, cell_done, hsq_done, hss_done,
         hstd_done) = (sem(n) for n in (
             "xc_silu", "xs_hi", "xs_lo", "rg_tanh", "rg_exp", "rg_arg", "rg_sqrt", "y_done", "yh_done",
             "yl_done", "sp_exp", "sp_done", "vt_ready", "vt_copied", "gt_ready", "gt_done", "gr_ready",
             "f_abs", "f_exp", "rows_done", "cc_ready", "cc_done", "mb_ready", "wm_ready", "we_ready",
             "floor_ready", "st_ready", "sw_ready", "num_ready", "cell_done", "hsq_done", "hss_done", "hstd_done"))
        dve_step, act_step, pool_step = sem("dve_step"), sem("act_step"), sem("pool_step")

        block = ctx.enter_context(nc.Block())

        class Step:

            def __init__(self, eng, semaphore):
                self.eng, self.sem, self.n, self.off, self.scratch = eng, semaphore, 0, 0, None

            def link(self, ins):
                self.n += 1
                ins.then_inc(self.sem, 1)
                self.eng.wait_ge(self.sem, self.off + self.n)

            @contextmanager
            def turns(self, reg, n, per):
                start, off = self.n, self.off
                self.off = reg * per + off
                yield
                assert self.n - start == per, (self.n - start, per)
                self.n, self.off = start + n * per, off

        def taken_at(eng, n, loops=(), limit=None):
            for e in "av":
                points = [0]
                for _, step, turns in loops:
                    points = [o + step * i for o in points for i in range(turns)]
                need = [TAKEN[e][n + o] for o in points]
                most = [TAKEN[e][(limit or n) + o] for o in points]
                if need[-1] == 0:
                    continue
                value = None
                if not loops:
                    value = need[0]
                elif len(loops) == 1:
                    a, d = affine(need, most)
                    value = loops[0][0] * d + a if d else a
                else:
                    (lay, step, n0), (reg, _, n1) = loops
                    delta = TAKEN[e][n + step + loops[1][1] * (n1 - 1)] - TAKEN[e][n + loops[1][1] * (n1 - 1)]
                    need = [max(need[i + n1 * j] - delta * j for j in range(n0)) for i in range(n1)]
                    most = [min(most[i + n1 * j] - delta * j for j in range(n0)) for i in range(n1)]
                    a, d = affine(need, most)
                    value = reg * d + lay * delta + a if d else lay * delta + a
                if isinstance(value, int) and value <= 0:
                    continue
                eng.wait_ge(taken[e], value)

        def ring_free(eng, n, loops, start):
            turns, step = loops[-1][2], loops[-1][1]
            for e in "av":
                need = [TAKEN[e][n - 3 + step * i] for i in range(1, turns)]
                if need[-1] <= TAKEN[e][start - 1]:
                    continue
                a, d = affine(need, [TAKEN[e][n - 1 + step * i] for i in range(1, turns)])
                assert 0 < a - d <= TAKEN[e][n - 1]
                value = loops[-1][0] * d + (a - d)
                if len(loops) == 2:
                    value = loops[0][0] * (TAKEN[e][n + loops[0][1]] - TAKEN[e][n]) + value
                eng.wait_ge(taken[e], value)

        def unit_of(n, loops=()):
            for reg, step, _ in loops:
                n = reg * step + n
            return n

        def landed(n, loops=()):
            v = 16 * (n // SLOTS + 1)
            for reg, step, _ in loops:
                v = reg * (16 * step // SLOTS) + v
            return v

        @block.sync
        def _(sp):
            sp.dma_start(x[:], x_in).then_inc(x_in_s, 16)
            sp.dma_start(raw[:, 0, :], w_units[0]).then_inc(raw_in[0], 16)
            sp.dma_start(raw[:, 1, :], w_units[1]).then_inc(raw_in[1], 16)
            sp.dma_start(raw[:, 2, :], w_units[2]).then_inc(raw_in[2], 16)
            sp.dma_start(raw[:, 3, :], w_units[3]).then_inc(raw_in[3], 16)
            with sp.Fori(0, NU // SLOTS - 1) as i:
                for r in range(SLOTS):
                    sp.wait_ge(lo_done, i * SLOTS + (r + 1))
                    sp.dma_start(raw[:, r, :], w_units[bass.ds(i * SLOTS + (SLOTS + r), 1)]
                                 .rearrange("a p n -> p (a n)")).then_inc(raw_in[r], 16)
            for n in range(NU // SLOTS * SLOTS, NU):
                sp.wait_ge(lo_done, n - SLOTS + 1)
                sp.dma_start(raw[:, n % SLOTS, :], w_units[n]).then_inc(raw_in[n % SLOTS], 16)
            sp.wait_ge(tn_done, SPLIT_BEFORE[-1] + KD)
            sp.dma_start(out, tn[:]).then_inc(out_s, 16)
            sp.wait_ge(out_s, 16)

        @block.gpsimd
        def _(pool):
            step = Step(pool, pool_step)
            link = step.link
            g = nc.gpsimd
            link(g.memset(ident[:], 0.0))
            link(g.affine_select(out=ident[:], in_=ident[:], compare_op=ALU.not_equal, fill=1.0, base=0,
                                 pattern=[[-1, P]], channel_multiplier=1))
            link(g.memset(causal[:], 0.0))
            link(g.memset(causal_t[:], 0.0))
            link(g.affine_select(out=causal[:, 0:128], in_=causal[:, 0:128], compare_op=ALU.is_ge, fill=NEG,
                                 base=0, pattern=[[-1, 128]], channel_multiplier=1))
            link(g.affine_select(out=causal[:, 128:384], in_=causal[:, 128:384], compare_op=ALU.is_ge, fill=NEG,
                                 base=128, pattern=[[-1, 256]], channel_multiplier=1))
            for a in (0, 256):
                link(g.affine_select(out=causal_t[:, a:a + 128], in_=causal_t[:, a:a + 128], compare_op=ALU.is_ge,
                                     fill=NEG, base=0, pattern=[[1, 128]], channel_multiplier=-1))
            di = dist[:, 0, :].bitcast(I32)
            link(g.iota(di[:, 0:128], pattern=[[-1, 128]], base=0, channel_multiplier=1))
            link(g.iota(di[:, 128:384], pattern=[[-1, 256]], base=128, channel_multiplier=1))
            g.memset(ones[:], 1.0).then_inc(masks_done, 1)
            for r in range(3):
                pool.dma_start(ada[:, r, :], w_ada[r]).then_inc(ada_in[r], 16)
            with pool.Fori(1, 24 * LAYERS // 3) as i:
                for r in range(3):
                    if r < 2:
                        pool.wait_ge(ada_used, (i - 1) * 3 + (r + 1))
                    else:
                        pool.wait_ge(ada_used, i * 3)
                    pool.dma_start(ada[:, r, :], w_ada[bass.ds(i * 3 + r, 1)].rearrange("a p n -> p (a n)"))\
                        .then_inc(ada_in[r], 16)
            for lay in range(LAYERS):
                if lay:
                    pool.wait_ge(res_done, 2 + lay)
                pool.dma_start(par2[:], par2_in[lay]).then_inc(par2_in_s, 16)

        @block.scalar
        def _(a):
            step = Step(a, act_step)
            link = step.link
            hold_reg = a.alloc_register("act_hold")
            a.reg_mov(hold_reg, 0)

            def wait(semaphore, value):
                a.wait_ge(semaphore, value)
                if not isinstance(value, int):
                    a.reg_add(hold_reg, hold_reg, 0)

            def hi(n, loops=()):
                a.wait_ge(raw_in[n % SLOTS], landed(n, loops))
                if n >= SLOTS:
                    a.wait_ge(unit_used, unit_of(n - SLOTS + 1, loops))
                a.activation(w_hi[:, n % SLOTS, :], raw[:, n % SLOTS, :], ACT.Copy).then_inc(hi_done, 1)

            def ahead(n, loops=()):
                if n + 3 not in FIRST_UNITS:
                    hi(n + 3, loops)

            def product(n, loops=()):
                wait(unit_used, unit_of(n + 1, loops))

            def norm_square(n, src, dst, k):
                if n:
                    a.wait_ge(ss_done, n)
                c = (k + 1) // 2
                for lo_, hi_ in ((0, c), (c, k)):
                    a.activation(dst[:, lo_:hi_, :], src[:, lo_:hi_, :], ACT.Square).then_inc(sq_done, 1)

            def norm_std(n, k, serial=None):
                v = n if serial is None else serial
                a.wait_ge(ss_done, v + 1)
                if n:
                    a.wait_ge(rstd_done, v)
                a.activation(std[:], half(4, 0), ACT.Sqrt, bias=eps, scale=1.0 / (k * P)).then_inc(std_done, 1)

            def norm_hi(n, k, slot, src):
                for j in range(k):
                    a.wait_ge(tn_done, SPLIT_BEFORE[n] + j + 1)
                    a.activation(act[:, slot + j, 0, :], src[:, j, :], ACT.Copy).then_inc(nh_done, 1)

            a.dma_start(memx, mem_in).then_inc(mem_in_s, 16)
            a.dma_start(par1[:], par1_in).then_inc(par_in, 16)
            a.dma_start(ar_g[:, 20, :].bitcast(I32), pos_in).then_inc(pos_in_s, 16)
            for n in range(3):
                hi(n)
            a.wait_ge(par_in, 16)
            a.activation(cact[:], c1("c", 0, KD), ACT.Silu).then_inc(cact_done, 1)
            a.wait_ge(mem_in_s, 16)
            norm_square(N_MEM, memx, sq, KD)
            a.wait_ge(x_in_s, 16)
            a.activation(ar_g[:, 0:4, :], x[:, 0:4, :], ACT.Square).then_inc(sq_done, 1)
            a.activation(ar_g[:, 4:8, :], x[:, 4:8, :], ACT.Square).then_inc(sq_done, 1)
            a.wait_ge(tables_done, 1)
            norm_std(N_MEM, KD)
            norm_std(N_X, KD)
            norm_hi(N_MEM, KD, 0, tn)
            norm_hi(N_X, KD, 16, ar_g[:, 8:16, :])
            a.wait_ge(angle_done, 1)
            a.activation(cos_t[64:96, :], rope_tmp[64:96, 0, :], ACT.Sin, scale=0.5).then_inc(sine_done, 1)
            a.activation(sin_t[96:128, :], rope_tmp[96:128, 0, :], ACT.Sin).then_inc(sine_done, 1)
            for m in range(4):
                n = U["memk"] + m
                ahead(n)
                product(n)
                a.activation(k_mem[:, m, :], half(n % 4, 0), ACT.Copy).then_inc(taken["a"], 1)
            for m in range(2):
                n = U["memv"] + 2 * m
                ahead(n)
                ahead(n + 1)
                product(n + 1)
                a.activation(v_mem[:, :, m * S:(m + 1) * S], bank(n % 4).rearrange("p (s n) -> p s n", s=2),
                             ACT.Copy).then_inc(taken["a"], 1)
            for m in range(5):
                n = U["latent"] + m
                ahead(n)
                product(n)
                if m == 0:
                    a.wait_ge(nl_done, 2 * KD)
                ins = a.activation(latent[:, m, :], half(n % 4, 0), ACT.Copy).then_inc(taken["a"], 1)
                if m == KQ - 1:
                    a.wait_ge(taken["a"], TAKEN["a"][n])
                    norm_square(N_CQ, latent[:, 0:KQ, :], ar_g[:, 5:8, :], KQ)
            a.wait_ge(taken["a"], TAKEN["a"][U["latent"] + 4])
            norm_square(N_CKV, latent[:, KQ:5, :], ar_g[:, 8:10, :], KKV)
            ahead(U["latent"] + 5)
            norm_std(N_CQ, KQ)
            norm_std(N_CKV, KKV)
            norm_hi(N_CQ, KQ, 8, ar_g[:, 10:13, :])
            norm_hi(N_CKV, KKV, 11, ar_g[:, 13:15, :])

            with a.Fori(0, 6) as i:
                loops = ((i, 4, 6),)
                for r in range(4):
                    n = U["qk"] + r
                    ahead(n, loops)
                    product(n, loops)
                    a.activation(qk_d[:, bass.ds(i * 4 + r, 1), :].rearrange("p a n -> p (a n)"), half(n % 4, 0),
                                 ACT.Copy).then_inc(taken["a"], 1)
            with a.Fori(0, 3) as i:
                loops = ((i, 4, 3),)
                for r in range(0, 4, 2):
                    n = U["v"] + r
                    ahead(n, loops)
                    ahead(n + 1, loops)
                    product(n + 1, loops)
                    a.activation(v_d[:, :, bass.ds(i * 2 * S + r // 2 * S, S)],
                                 bank(n % 4).rearrange("p (s n) -> p s n", s=2), ACT.Copy).then_inc(taken["a"], 1)

            a.wait_ge(nl_done, SPLIT_BEFORE[N_CKV + 1])
            for m in range(4):
                n = U["uq"] + m
                ahead(n)
                product(n)
                a.activation(q_mla[0:64, 2 * m:2 * m + 2, :], psum[0:64, n % 4, :].rearrange(
                    "p (h t) -> p h t", h=2), ACT.Copy).then_inc(q_nope, 1)
            n = U["ukvk"]
            ahead(n)
            product(n)
            for m in range(4):
                for hh in range(2):
                    ins = a.activation(k_mla[0:64, 2 * m + hh, :], psum[64 * hh:64 * hh + 64, 4 + m // 2,
                                                                      (m % 2) * S:(m % 2 + 1) * S], ACT.Copy)
            ins.then_inc(taken["a"], 1)
            n = U["ukvv"]
            ahead(n)
            product(n)
            a.wait_ge(k_pe_done, 1)
            for blk in range(2):
                ins = a.activation(v_mla[:, blk, :], bank(6 + blk), ACT.Copy)
            ins.then_inc(taken["a"], 1)
            for m in range(4):
                n = U["memq"] + m
                ahead(n)
                product(n)
                a.activation(q_mem[:, m, :], half(n % 4, 0), ACT.Copy).then_inc(taken["a"], 1)

            def exps(j):
                a.wait_ge(m_ready, j + 1)
                scale = (NOPE + ROPE) ** -0.5 if j in JOBS_MLA else DH ** -0.5
                for q, (src, dst) in enumerate(score_views(j)):
                    ins = a.activation(dst, src, ACT.Exp, bias=stat(j, q, 2), scale=scale, accum_out=stat(j, q, 3))
                ins.then_inc(e_ready, 1)

            def copy_pt(j):
                a.wait_ge(pt_ready, j + 1)
                if j in JOBS_DIL or j == JOBS_MEM[0]:
                    a.wait_ge(o_ready, j)
                elif j >= 2:
                    a.wait_ge(o_ready, j - 1)
                if j in JOBS_DIL:
                    a.activation(pt_sb.rearrange("p (g n) -> p g n", g=3), psum[:, 3:6, 0:384], ACT.Copy)\
                        .then_inc(pt_copied, 1)
                else:
                    n = 384 if j in JOBS_MLA else 512
                    a.activation(pt_sb[:, 512 * (j % 2):512 * (j % 2) + n], psum[:, 3 + j % 2, 0:n], ACT.Copy)\
                        .then_inc(pt_copied, 1)

            def out_hi(j):
                a.wait_ge(o_ready, j + 1)
                lo_p, hi_p, slot = head_rows(j)
                a.activation(act[lo_p:hi_p, slot, 0, :], psum[lo_p:hi_p, 6 + j % 2, 0:S], ACT.Copy)\
                    .then_inc(oh_ready, 1)

            def attend(jobs):
                exps(jobs[0])
                for j in jobs:
                    if j + 1 <= jobs[-1]:
                        exps(j + 1)
                    copy_pt(j)
                    out_hi(j)

            a.wait_ge(ada_used, 24 * LAYERS)
            attend(list(JOBS_MLA))

            with a.Fori(0, 6) as i:
                loops = ((i, 4, 6),)
                for r in range(4):
                    n = U["gates"] + r
                    ahead(n, loops)
                    product(n, loops)
                    a.activation(gates[:, bass.ds(i * 4 + r, 1), :].rearrange("p a n -> p (a n)"), half(n % 4, 0),
                                 ACT.Sigmoid, bias=c1("b_gate", i * 4 + r)).then_inc(taken["a"], 1)
            attend(list(JOBS_DIL) + list(JOBS_MEM))
            for m in range(12):
                ahead(U["branch"] + m)
                if m >= 8:
                    j = 2 * (m - 8)
                    a.wait_ge(merge_done, m - 7)
                    a.activation(act[:, 16 + j:18 + j, 0, :], merged[:, j:j + 2, :], ACT.Copy).then_inc(mh_done, 1)

            def k_major(name, count, norm):
                for m in range(count):
                    ahead(U[name] + m)
                product(U[name] + count - 1)
                for b in range(4):
                    ins = a.activation(y_f[:, 2 * b:2 * b + 2, :], bank(4 + b).rearrange("p (h t) -> p h t", h=2),
                                       ACT.Copy)
                ins.then_inc(taken["a"], 1)
                a.wait_ge(taken["a"], TAKEN["a"][U[name] + count - 1])
                norm_square(norm, y_f, sq, KD)
                norm_std(norm, KD)

            k_major("wo", 8, N_MIX)
            a.wait_ge(res_done, 1)
            norm_square(N_FFN, x, sq, KD)
            norm_std(N_FFN, KD)
            norm_hi(N_FFN, KD, 16, tn)

            def up_turn(i, turns, first, direct):
                loops = ((i, 4, turns),)
                for r in range(4):
                    n = U["up"] + 4 * first + r
                    ahead(n, loops)
                    product(n, loops)
                    if r == 0 and direct:
                        wait(z_free, i + 1)
                    elif r == 0:
                        wait(ah_done, i + first)
                    a.activation(z_up[:, r, :], half(n % 4, 0), ACT.Identity,
                                 bias=c1("conv_b", i * 4 + (4 * first + r)),
                                 scale=c1("conv_w", i * 4 + (4 * first + r + 2 * 2 * KF))).then_inc(z_init, 1)
                    if r % 2:
                        taken_at(a, n - 1, loops)
                        a.activation(z_up[:, r - 1, :], z_up[:, r - 1, :], ACT.Silu).then_inc(silu_done, 1)
                wait(prod_done, i + (first + 1))
                if direct:
                    a.activation(act[:, bass.ds(i * 2 + 2 * first, 2), 0, :], z_up[:, 1:4:2, :], ACT.Copy)\
                        .then_inc(ah_done, 1)
                else:
                    a.activation(late[:, bass.ds(i * 2 + (2 * first - 16), 2), :], z_up[:, 1:4:2, :], ACT.Copy)\
                        .then_inc(ah_done, 1)

            with a.Fori(0, 8) as i:
                up_turn(i, 8, 0, True)
            a.wait_ge(z_free, 9)
            with a.Fori(0, 3) as i:
                up_turn(i, 3, 8, False)
            a.wait_ge(unit_used, U["down"])
            a.wait_ge(ah_done, 11)
            for t in range(3):
                a.activation(act[:, 16 + 2 * t:18 + 2 * t, 0, :], late[:, 2 * t:2 * t + 2, :], ACT.Copy)\
                    .then_inc(ah_done, 1)
            k_major("down", KF, N_FFN_OUT)

            with a.Fori(0, LAYERS) as lay:
                L = (lay, PER_LAYER, LAYERS)
                for m in range(3):
                    hi(LAYER0 + m, (L,))
                a.wait_ge(par2_in_s, lay * 16 + 16)
                a.wait_ge(sp_done, lay * 2 + 1)
                a.activation(t8[0], t8[0], ACT.Exp, scale=-1.0).then_inc(sp_exp, 1)
                a.wait_ge(res_done, lay + 2)
                a.wait_ge(ss_done, lay + N_LAYER)
                for h in range(2):
                    a.activation(sq[:, 4 * h:4 * h + 4, :], x[:, 4 * h:4 * h + 4, :], ACT.Square)\
                        .then_inc(sq_done, 1)
                norm_std(N_LAYER, KD, lay + N_LAYER)
                for j in range(KD):
                    wait(tn_done, lay * KD + (SPLIT_BEFORE[N_LAYER] + j + 1))
                    a.activation(act[:, 16 + j, 0, :], tn[:, j, :], ACT.Identity,
                                 bias=mod[:, bass.ds(lay * 24 + j, 1)]).then_inc(nh_done, 1)
                with a.Fori(0, 2) as i:
                    loops = (L, (i, 4, 2))
                    for r in range(4):
                        n = U["in"] + r
                        ahead(n, loops)
                        product(n, loops)
                        a.activation(u_rg[:, bass.ds(i * 4 + r, 1), :].rearrange("p a n -> p (a n)"),
                                     half(n % 4, 0), ACT.Identity,
                                     bias=par2[:, bass.ds(i * 4 + (C2["rg_b"][0] + r), 1)],
                                     scale=par2[:, bass.ds(i * 4 + (C2["rg_w"][0] + 3 * KD + r), 1)])\
                            .then_inc(z_init, 1)
                a.wait_ge(nl_done, lay * KD + SPLIT_BEFORE[N_LAYER + 1])
                with a.Fori(0, 2) as i:
                    loops = (L, (i, 4, 2))
                    for r in range(4):
                        n = U["in"] + 8 + r
                        ahead(n, loops)
                        product(n, loops)
                        a.activation(xm[:, bass.ds(i * 4 + r, 1), :].rearrange("p a n -> p (a n)"),
                                     half(n % 4, 0), ACT.Copy)
                        a.activation(xc[:, bass.ds(i * 4 + r, 1), :].rearrange("p a n -> p (a n)"),
                                     half(n % 4, 0), ACT.Identity,
                                     bias=par2[:, bass.ds(i * 4 + (C2["ml_b"][0] + r), 1)],
                                     scale=par2[:, bass.ds(i * 4 + (C2["ml_w"][0] + 3 * KD + r), 1)])\
                            .then_inc(z_init, 1)
                taken_at(a, U["in"] + 15, (L,))
                a.activation(xc[:], xc[:], ACT.Silu).then_inc(xc_silu, 1)
                for h in range(2):
                    a.activation(act[:, 8 + 4 * h:12 + 4 * h, 0, :], u_rg[:, 4 * h:4 * h + 4, :], ACT.Copy)\
                        .then_inc(xs_hi, 1)
                with a.Fori(0, 4) as i:
                    loops = (L, (i, 4, 4))
                    for r in range(4):
                        n = U["in"] + 16 + r
                        ahead(n, loops)
                        product(n, loops)
                        a.activation(zy[:, bass.ds(i * 4 + r, 1), :].rearrange("p a n -> p (a n)"),
                                     half(n % 4, 0), ACT.Silu).then_inc(taken["a"], 1)
                for h in range(2):
                    a.activation(act[:, 4 * h:4 * h + 4, 0, :], xm[:, 4 * h:4 * h + 4, :], ACT.Copy)\
                        .then_inc(xs_hi, 1)
                with a.Fori(0, 2) as i:
                    loops = (L, (i, 4, 2))
                    for r in range(4):
                        n = U["in"] + 32 + r
                        ahead(n, loops)
                        product(n, loops)
                        a.activation(so[:, bass.ds(i * 4 + r, 1), :].rearrange("p a n -> p (a n)"),
                                     half(n % 4, 0), ACT.Sigmoid).then_inc(taken["a"], 1)
                a.wait_ge(xc_silu, lay + 1)
                for h in range(2):
                    a.activation(act[:, 16 + 4 * h:20 + 4 * h, 0, :], xc[:, 4 * h:4 * h + 4, :], ACT.Copy)\
                        .then_inc(xs_hi, 1)
                ahead(U["rg"], (L,))
                ahead(U["rg"] + 1, (L,))
                product(U["rg"], (L,))
                a.wait_ge(xs_lo, lay * 6 + 6)
                for h in range(HR):
                    ins = a.activation(rg_r[:, h, :], half(4 + h // 2, h % 2), ACT.Sigmoid, bias=c2("b_a", h))
                ins.then_inc(taken["a"], 1)
                product(U["rg"] + 1, (L,))
                for h in range(HR):
                    ins = a.activation(rg_i[h // 4][:, h % 4, :], half(h // 2, h % 2), ACT.Sigmoid, bias=c2("b_x", h))
                ins.then_inc(taken["a"], 1)
                a.wait_ge(taken["a"], lay * LAYER_A + (TAKEN["a"][U["rg"] + 1]))
                a.wait_ge(sp_done, lay * 2 + 2)
                for h in range(HR):
                    ins = a.activation(rg_t[:, h, :], rg_r[:, h, :], ACT.Tanh, scale=soft[:, h:h + 1])
                ins.then_inc(rg_tanh, 1)
                a.wait_ge(rg_tanh, lay + 1)
                for q in range(2):
                    n = U["mlq"] + q
                    ahead(n, (L,))
                    product(n, (L,))
                    for b in range(2):
                        ins = a.activation(q_ml[:, 4 * q + 2 * b:4 * q + 2 * b + 2, :],
                                           bank(4 + 2 * q + b).rearrange("p (h t) -> p h t", h=2), ACT.Copy)
                    ins.then_inc(taken["a"], 1)
                for h in range(HR):
                    ins = a.activation(rg_r[:, h, :], rg_r[:, h, :], ACT.Exp, scale=nsoft[:, h:h + 1])
                ins.then_inc(rg_exp, 1)
                for q in range(2):
                    ahead(U["mlk"] + q, (L,))
                for q in range(2):
                    n = U["mlv"] + q
                    ahead(n, (L,))
                    product(n, (L,))
                    if q == 0:
                        a.wait_ge(rg_arg, lay * 2 + 1)
                    for b in range(2):
                        ins = a.activation(v_ml[:, 4 * q + 2 * b:4 * q + 2 * b + 2, :],
                                           bank(4 + 2 * q + b).rearrange("p (h t) -> p h t", h=2), ACT.Copy)
                    ins.then_inc(taken["a"], 1)
                a.wait_ge(rg_arg, lay * 2 + 2)
                a.activation(rg_t[:], rg_t[:], ACT.Sqrt).then_inc(rg_sqrt, 1)
                for q in range(4):
                    a.wait_ge(vt_ready, lay * 4 + (q + 1))
                    a.activation(v_tok[:, q // 2, (q % 2) * 512:(q % 2 + 1) * 512], bank(q), ACT.Copy)\
                        .then_inc(vt_copied, 1)
                a.wait_ge(f_abs, lay + 1)
                a.activation(row[2], row[2], ACT.Exp, scale=-1.0).then_inc(f_exp, 1)
                a.wait_ge(yr_done, lay * 5 + 1)
                for h in range(2):
                    a.activation(act[:, 8 + 4 * h:12 + 4 * h, 0, :], zy[:, 4 * h:4 * h + 4, :], ACT.Copy)\
                        .then_inc(yh_done, 1)
                for h in range(HL):
                    a.wait_ge(wm_ready, lay * HL + (h + 1))
                    a.activation(w_ml[:, h % 2, 0:256], w_ml[:, h % 2, 0:256], ACT.Exp, bias=c_col[:, 0, h:h + 1])
                    a.activation(w_ml[:, h % 2, 256:384], w_ml[:, h % 2, 256:384], ACT.Exp,
                                 bias=c_col[:, 1, h:h + 1]).then_inc(we_ready, 1)
                    if h:
                        a.wait_ge(cell_done, lay * HL + h)
                    a.activation(floor_ml, half(2 + h % 2, 1), ACT.Exp).then_inc(floor_ready, 1)
                for h in range(HL):
                    a.wait_ge(cell_done, lay * HL + (h + 1))
                    a.activation(sq_ml[:, 2 * h:2 * h + 2, :], so[:, 2 * h:2 * h + 2, :], ACT.Square)\
                        .then_inc(hsq_done, 1)
                for h in range(HL):
                    a.wait_ge(hss_done, lay * HL + (h + 1))
                    ins = a.activation(sq_ml[:, 2 * h, :], half(4 + h, 0), ACT.Sqrt, bias=eps, scale=1.0 / 256)
                    ins.then_inc(hstd_done, 1)
                for m in range(2):
                    ahead(U["out"] + m, (L,))
                for h in range(HL):
                    a.wait_ge(yr_done, lay * 5 + (h + 2))
                    a.activation(act[:, 2 * h:2 * h + 2, 0, :], zy[:, 8 + 2 * h:10 + 2 * h, :], ACT.Copy)\
                        .then_inc(yh_done, 1)
                for m in range(2, 13):
                    ahead(U["out"] + m, (L,))
            a.wait_ge(res_done, LAYERS + 2)
            norm_square(N_FINAL, x, sq, KD)
            norm_std(N_FINAL, KD)

        @block.vector
        def _(v):
            step = Step(v, dve_step)
            link = step.link

            def lo(n, loops=()):
                v.wait_ge(hi_done, unit_of(n + 1, loops))
                r = n % SLOTS
                v.tensor_tensor(w_lo[:, r, :], raw[:, r, :], w_hi[:, r, :].bitcast(F32), ALU.subtract)\
                    .then_inc(lo_done, 1)

            def ahead(n, loops=()):
                if n + 3 not in FIRST_UNITS:
                    lo(n + 3, loops)

            def act_lo(slot, src, count=1):
                return v.tensor_tensor(act[:, slot:slot + count, 1, :], src,
                                       act[:, slot:slot + count, 0, :].bitcast(F32), ALU.subtract)

            def norm_rstd(n):
                v.wait_ge(std_done, n + 1)
                ins = v.reciprocal(rstd[:], std[:])
                ins.then_inc(rstd_done, 1)
                v.wait_ge(rstd_done, n + 1)

            def norm_split(n, k, src, gain, dst, slot):
                norm_rstd(n)
                for j in range(k + 1):
                    if j < k:
                        v.scalar_tensor_tensor(out=dst[:, j, :], in0=src[:, j, :], scalar=gain(j), in1=rstd[:],
                                               op0=ALU.mult, op1=ALU.mult).then_inc(tn_done, 1)
                    if j:
                        v.wait_ge(nh_done, SPLIT_BEFORE[n] + j)
                        act_lo(slot + j - 1, dst[:, j - 1:j, :]).then_inc(nl_done, 1)

            def norm_add(n, gain):
                norm_rstd(n)
                for j in range(KD):
                    ins = v.scalar_tensor_tensor(out=tn[:, j, :], in0=y_f[:, j, :], scalar=gain(j), in1=rstd[:],
                                                 op0=ALU.mult, op1=ALU.mult)
                link(ins)
                v.tensor_tensor(x[:], x[:], tn[:], ALU.add).then_inc(res_done, 1)

            link(v.memset(tiny[:], 0.0))
            v.memset(eps, EPS).then_inc(tables_done, 1)
            for n in range(3):
                lo(n)
            v.wait_ge(par_in, 16)
            norm_split(N_MEM, KD, memx, lambda j: c1("g_mem", j), tn, 0)
            norm_split(N_X, KD, x, lambda j: c1("g_pre_mix", j), ar_g[:, 8:16, :], 16)

            two_pi = 2 * np.pi
            part1 = 6.28125
            part2 = float(np.float32(round((two_pi - part1) * 2 ** 22) / 2 ** 22))
            part3 = two_pi - part1 - part2
            magic = 1.5 * 2 ** 23
            ang, turn = rope_tmp[:, 0, :], rope_tmp[:, 1, :]
            v.wait_ge(pos_in_s, 16)
            link(v.tensor_scalar(ang, ar_g[:, 20, :].bitcast(I32), c1("freq"), None, ALU.mult))
            link(v.tensor_scalar(turn, ang, 1.0 / two_pi, magic, ALU.mult, ALU.add))
            link(v.tensor_scalar(turn, turn, magic, None, ALU.subtract))
            for part in (part1, part2, part3):
                link(v.scalar_tensor_tensor(out=ang, in0=turn, scalar=-part, in1=ang, op0=ALU.mult, op1=ALU.add))
            v.tensor_scalar(ang, ang, 3.1415925, -3.1415925, ALU.min, ALU.max).then_inc(angle_done, 1)

            v.wait_ge(masks_done, 1)
            di = dist[:, 0, :].bitcast(I32)
            tmp = flat(ar_m[:, 8:10, :])[:, 0:384]
            for g in (1, 2):
                dg = dist[:, g, :]
                link(v.tensor_scalar(dg.bitcast(I32), di, DILATION[g] - 1, None, ALU.bitwise_and))
                link(v.tensor_scalar(dg, dg.bitcast(I32), 0.0, 1.0, ALU.is_equal, ALU.subtract))
                link(v.scalar_tensor_tensor(out=dg, in0=dg, scalar=-300 * NEG, in1=di, op0=ALU.mult,
                                            op1=ALU.subtract))
                link(v.tensor_tensor(dg, dg, causal[:], ALU.add))
            link(v.tensor_scalar(tmp, di, float(SPAN), 300 * NEG, ALU.is_gt, ALU.mult))
            link(v.scalar_tensor_tensor(out=tmp, in0=di, scalar=-1.0, in1=tmp, op0=ALU.mult, op1=ALU.add))
            link(v.tensor_tensor(dist[:, 0, :], tmp, causal[:], ALU.add))
            v.wait_ge(sine_done, 2)
            link(v.tensor_tensor(cos_t[64:96, :], cos_t[64:96, :], cos_t[64:96, :], ALU.mult))
            link(v.tensor_scalar(cos_t[64:96, :], cos_t[64:96, :], -2.0, 1.0, ALU.mult, ALU.add))
            link(v.tensor_scalar(sin_t[96:128, :], sin_t[96:128, :], par1[96:128, C1["sign"][0]:C1["sign"][0] + 1],
                                 None, ALU.mult))

            for n in range(U["memk"], U["latent"] + 6):
                ahead(n)

            def rotate(dst, src_bank, m):
                link(v.tensor_tensor(rope_tmp[64:96, m, :], psum[96:128, src_bank, m * S:(m + 1) * S],
                                     sin_t[96:128, :], ALU.mult))
                ins = v.tensor_tensor(dst, psum[64:96, src_bank, m * S:(m + 1) * S], cos_t[64:96, :], ALU.mult)
                return ins

            n = U["latent"] + 5
            v.wait_ge(unit_used, n + 1)
            k_rot = ar_g[64:96, 16, :]
            rotate(k_rot, n % 4, 0).then_inc(taken["v"], 1)
            v.wait_ge(taken["v"], TAKEN["v"][n])
            link(v.tensor_tensor(k_rot, k_rot, rope_tmp[64:96, 0, :], ALU.add))
            norm_split(N_CQ, KQ, latent[:, 0:KQ, :], lambda j: c1("q_norm", j), ar_g[:, 10:13, :], 8)
            norm_split(N_CKV, KKV, latent[:, KQ:5, :], lambda j: c1("kv_norm", j), ar_g[:, 13:15, :], 11)

            with v.Fori(0, 9) as i:
                for r in range(4):
                    ahead(U["qk"] + r, ((i, 4, 9),))
            v.wait_ge(ada_used, 24 * LAYERS)
            v.tensor_tensor(mod[:], psum[:, 7, 0:24 * LAYERS], c1("b_ada", 0, 24 * LAYERS), ALU.add)\
                .then_inc(mod_done, 1)
            v.tensor_copy(k_mla[64:96, :, :], k_rot.unsqueeze(1).to_broadcast([32, 8, S])).then_inc(k_pe_done, 1)
            for m in range(4):
                n = U["uq"] + m
                ahead(n)
                v.wait_ge(q_nope, m + 1)
                for h in range(2):
                    dst = q_mla[64:96, 2 * m + h, :]
                    ins = rotate(dst, n % 4, h)
                    if h:
                        ins.then_inc(taken["v"], 1)
                        v.wait_ge(taken["v"], TAKEN["v"][n])
                    else:
                        link(ins)
                    ins = v.tensor_tensor(dst, dst, rope_tmp[64:96, h, :], ALU.add)
                ins.then_inc(rope_done, 1)
            for n in range(U["ukvk"], U["memq"] + 4):
                ahead(n)

            def maxima(j):
                v.wait_ge(s_ready, j + 1)
                s = s_sb[:, j % 2, :]
                scale = (NOPE + ROPE) ** -0.5 if j in JOBS_MLA else DH ** -0.5
                if j in JOBS_MLA:
                    link(v.tensor_tensor(s[:, 0:384], psum[:, j % 2, 0:384], causal[:], ALU.add))
                elif j in JOBS_DIL:
                    for g in range(GROUPS):
                        slope = 2.0 ** (-8.0 * ((j - JOBS_DIL[0]) * GROUPS + g + 1) / (GROUPS * HD))
                        ins = v.scalar_tensor_tensor(out=s[:, 384 * g:384 * g + 384], in0=dist[:, g, :],
                                                     scalar=slope / scale, in1=psum[:, g, 0:384], op0=ALU.mult,
                                                     op1=ALU.add)
                    link(ins)
                for q, (src, _) in enumerate(score_views(j)):
                    ins = v.tensor_reduce(stat(j, q, 0), src, AX.XY if j in JOBS_DIL else AX.X, ALU.max,
                                          negate=True)
                link(ins)
                v.tensor_scalar(stat(j, None, 2), stat(j, None, 0), scale, None, ALU.mult).then_inc(m_ready, 1)

            def normalise(j):
                v.wait_ge(e_ready, j + 1)
                link(v.reciprocal(stat(j, None, 1), stat(j, None, 3)))
                for q, (_, p) in enumerate(score_views(j)):
                    ins = v.tensor_scalar(p, p, stat(j, q, 1), None, ALU.mult)
                ins.then_inc(p_ready, 1)

            def out_lo(j):
                v.wait_ge(oh_ready, j + 1)
                lo_p, hi_p, slot = head_rows(j)
                v.tensor_tensor(act[lo_p:hi_p, slot, 1, :], psum[lo_p:hi_p, 6 + j % 2, 0:S],
                                act[lo_p:hi_p, slot, 0, :].bitcast(F32), ALU.subtract).then_inc(ol_ready, 1)

            def attend(jobs):
                maxima(jobs[0])
                for j in jobs:
                    if j + 1 <= jobs[-1]:
                        maxima(j + 1)
                    normalise(j)
                    out_lo(j)

            attend(list(JOBS_MLA))
            with v.Fori(0, 6) as i:
                for r in range(4):
                    ahead(U["gates"] + r, ((i, 4, 6),))
            taken_at(v, U["gates"] + 23)
            attend(list(JOBS_DIL) + list(JOBS_MEM))

            for b in range(3):
                for q in range(4):
                    n = U["branch"] + 4 * b + q
                    ahead(n)
                    v.wait_ge(unit_used, n + 1)
                    y = bank(n % 4).rearrange("p (h t) -> p h t", h=2)
                    g = gates[:, 8 * b + 2 * q:8 * b + 2 * q + 2, :]
                    m = merged[:, 2 * q:2 * q + 2, :]
                    dst = m if b == 0 else y_f[:, 2 * (q % 2):2 * (q % 2) + 2, :]
                    v.tensor_tensor(dst, y, g, ALU.mult).then_inc(taken["v"], 1)
                    if b:
                        v.wait_ge(taken["v"], TAKEN["v"][n])
                        ins = v.tensor_tensor(m, m, dst, ALU.add)
                        if b == 1:
                            ins.then_inc(dve_step, 1)
                            step.n += 1
                        else:
                            ins.then_inc(merge_done, 1)
                            v.wait_ge(mh_done, q + 1)
                            act_lo(16 + 2 * q, m, 2).then_inc(merged_lo, 1)
                if b == 1:
                    v.wait_ge(dve_step, step.n)
            for m in range(8):
                ahead(U["wo"] + m)
            norm_add(N_MIX, lambda j: c1("g_post_mix", j))
            v.wait_ge(res_done, 1)
            norm_split(N_FFN, KD, x, lambda j: c1("g_pre_ffn", j), tn, 16)

            def up_turn(i, turns, first, direct):
                loops = ((i, 4, turns),)
                with step.turns(i, turns, 4):
                    for r in range(4):
                        n = U["up"] + 4 * first + r
                        ahead(n, loops)
                        v.wait_ge(z_init, i * 4 + (4 * first + r + 1))
                        for tap, shift in ((1, 1), (0, 2)):
                            ins = v.scalar_tensor_tensor(
                                out=z_up[:, r, shift:S], in0=psum[:, n % 4, 0:S - shift],
                                scalar=c1("conv_w", i * 4 + (4 * first + r + tap * 2 * KF)),
                                in1=z_up[:, r, shift:S], op0=ALU.mult, op1=ALU.add)
                            if tap:
                                link(ins)
                            else:
                                ins.then_inc(taken["v"], 1)
                v.wait_ge(silu_done, i * 2 + (2 * first + 2))
                taken_at(v, U["up"] + 4 * first + 3, loops)
                ins = v.tensor_tensor(z_up[:, 1:4:2, :], z_up[:, 0:4:2, :], z_up[:, 1:4:2, :], ALU.mult)
                ins.then_inc(prod_done, 1)
                v.wait_ge(ah_done, i + (first + 1))
                if direct:
                    slot = i * 2 + 2 * first
                    v.tensor_tensor(act[:, bass.ds(slot, 2), 1, :], z_up[:, 1:4:2, :],
                                    act[:, bass.ds(slot, 2), 0, :].bitcast(F32), ALU.subtract)\
                        .then_inc(z_free, 1)

            v.memset(tiny[:, 5:6], 0.0).then_inc(z_free, 1)
            with v.Fori(0, 8) as i:
                up_turn(i, 8, 0, True)
            with v.Fori(0, 3) as i:
                up_turn(i, 3, 8, False)
            for t in range(3):
                v.wait_ge(ah_done, 11 + t + 1)
                act_lo(16 + 2 * t, late[:, 2 * t:2 * t + 2, :], 2).then_inc(al_done, 1)
            for m in range(KF):
                ahead(U["down"] + m)
            norm_add(N_FFN_OUT, lambda j: c1("g_post_ffn", j))

            def log1p(dst, e, t, q, poly):
                link(v.tensor_scalar(t, e, 2.0, None, ALU.add))
                link(v.reciprocal(t, t))
                link(v.tensor_tensor(e, e, t, ALU.mult))
                link(v.tensor_tensor(q, e, e, ALU.mult))
                link(v.tensor_scalar(poly, q, 1.0 / 17, None, ALU.mult))
                for d in (15, 13, 11, 9, 7, 5, 3):
                    link(v.scalar_tensor_tensor(out=poly, in0=poly, scalar=1.0 / d, in1=q, op0=ALU.add,
                                                op1=ALU.mult))
                link(v.tensor_scalar(poly, poly, 1.0, 2.0, ALU.add, ALU.mult))
                link(v.tensor_tensor(dst, poly, e, ALU.mult))

            LINKS = 97
            with v.Fori(0, LAYERS) as lay, step.turns(lay, LAYERS, LINKS):
                L = (lay, PER_LAYER, LAYERS)
                for m in range(3):
                    lo(LAYER0 + m, (L,))
                v.wait_ge(par2_in_s, lay * 16 + 16)
                v.scalar_tensor_tensor(out=t8[0], in0=c2("lam", 0, KD), scalar=-1.0, in1=c2("lam", 0, KD),
                                       op0=ALU.mult, op1=ALU.max).then_inc(sp_done, 1)
                at = lay * 24 + KD
                v.wait_ge(res_done, lay + 2)
                v.scalar_tensor_tensor(out=gain2, in0=mod[:, bass.ds(at, KD)], scalar=1.0,
                                       in1=c2("norm_g", 0, KD), op0=ALU.add, op1=ALU.mult).then_inc(dve_step, 1)
                step.n += 1
                v.wait_ge(sp_exp, lay + 1)
                log1p(t8[1], t8[0], t8[2], t8[3], t8[1])
                link(v.tensor_scalar(t8[2], c2("lam", 0, KD), -1.0, 0.0, ALU.mult, ALU.max))
                link(v.tensor_tensor(t8[1], t8[1], t8[2], ALU.add))
                link(v.tensor_scalar(soft, t8[1], RG_C, None, ALU.mult))
                v.tensor_scalar(nsoft, t8[1], -RG_C, None, ALU.mult).then_inc(sp_done, 1)
                v.wait_ge(std_done, lay + (N_LAYER + 1))
                v.reciprocal(rstd[:], std[:]).then_inc(rstd_done, 1)
                v.wait_ge(rstd_done, lay + (N_LAYER + 1))
                for j in range(KD + 1):
                    if j < KD:
                        v.scalar_tensor_tensor(out=tn[:, j, :], in0=x[:, j, :], scalar=gain2[:, j:j + 1],
                                               in1=rstd[:], op0=ALU.mult, op1=ALU.mult).then_inc(tn_done, 1)
                    if j:
                        v.wait_ge(nh_done, lay * KD + (SPLIT_BEFORE[N_LAYER] + j))
                        v.scalar_tensor_tensor(out=act[:, 16 + j - 1, 1, :], in0=tn[:, j - 1, :],
                                               scalar=mod[:, bass.ds(lay * 24 + (j - 1), 1)],
                                               in1=act[:, 16 + j - 1, 0, :].bitcast(F32), op0=ALU.add,
                                               op1=ALU.subtract).then_inc(nl_done, 1)
                for part, (dst, w) in enumerate(((u_rg, "rg_w"), (xc, "ml_w"))):
                    with v.Fori(0, 2) as i, step.turns(i, 2, 8):
                        loops = (L, (i, 4, 2))
                        for r in range(4):
                            n = U["in"] + 8 * part + r
                            ahead(n, loops)
                            v.wait_ge(z_init, lay * 16 + (i * 4 + (2 * KF + 8 * part + r + 1)))
                            for shift in (1, 2, 3):
                                at = i * 4 + (C2[w][0] + (3 - shift) * KD + r)
                                tile = dst[:, bass.ds(i * 4 + r, 1), shift:S].rearrange("p a n -> p (a n)")
                                ins = v.scalar_tensor_tensor(out=tile, in0=psum[:, n % 4, 0:S - shift],
                                                             scalar=par2[:, bass.ds(at, 1)], in1=tile,
                                                             op0=ALU.mult, op1=ALU.add)
                                if shift < 3:
                                    link(ins)
                                else:
                                    ins.then_inc(taken["v"], 1)

                def split(which, slot, src):
                    for h in range(2):
                        v.wait_ge(xs_hi, lay * 6 + (2 * which + h + 1))
                        act_lo(slot + 4 * h, src[:, 4 * h:4 * h + 4, :], 4).then_inc(xs_lo, 1)

                split(0, 8, u_rg)
                with v.Fori(0, 4) as i:
                    for r in range(4):
                        ahead(U["in"] + 16 + r, (L, (i, 4, 4)))
                split(1, 0, xm)
                with v.Fori(0, 2) as i:
                    for r in range(4):
                        ahead(U["in"] + 32 + r, (L, (i, 4, 2)))
                split(2, 16, xc)
                ahead(U["rg"], (L,))
                ahead(U["rg"] + 1, (L,))
                v.wait_ge(taken["a"], lay * LAYER_A + TAKEN["a"][U["rg"] + 1])
                for h in range(2):
                    ins = v.tensor_tensor(rg_i[h], rg_i[h], u_rg[:, 4 * h:4 * h + 4, :], ALU.mult)
                ins.then_inc(rg_arg, 1)
                for q in range(2):
                    ahead(U["mlq"] + q, (L,))
                for q in range(2):
                    n = U["mlk"] + q
                    ahead(n, (L,))
                    v.wait_ge(unit_used, unit_of(n + 1, (L,)))
                    for b in range(2):
                        ins = v.tensor_copy(k_ml[:, 4 * q + 2 * b:4 * q + 2 * b + 2, :],
                                            bank(2 * q + b).rearrange("p (h t) -> p h t", h=2))
                    ins.then_inc(taken["v"], 1)
                for q in range(2):
                    ahead(U["mlv"] + q, (L,))
                v.wait_ge(rg_exp, lay + 1)
                link(v.tensor_tensor(xm[:], rg_r[:], rg_r[:], ALU.mult))
                v.scalar_tensor_tensor(out=flat(rg_t), in0=flat(xm), scalar=1.0, in1=flat(rg_t), op0=ALU.add,
                                       op1=ALU.mult).then_inc(rg_arg, 1)
                v.wait_ge(rg_sqrt, lay + 1)
                for h in range(2):
                    ins = v.tensor_tensor(rg_i[h], rg_i[h], rg_t[:, 4 * h:4 * h + 4, :], ALU.mult)
                link(ins)
                for h in range(HR):
                    ins = v.tensor_tensor_scan(rg_t[:, h, :], rg_r[:, h, :], rg_i[h // 4][:, h % 4, :], 0.0,
                                               ALU.mult, ALU.add)
                link(ins)
                v.tensor_tensor(zy[:, 0:8, :], zy[:, 0:8, :], rg_t[:], ALU.mult).then_inc(yr_done, 1)
                v.wait_ge(gt_ready, lay + 1)
                for blk in range(2):
                    ins = v.tensor_tensor(gate_tok[:, blk, :], psum[:, 6, 8 * blk:8 * blk + 8], c2("b_if", 0, 8),
                                          ALU.add)
                ins.then_inc(gt_done, 1)
                v.wait_ge(gr_ready, lay + 1)
                li, f, e, t, q = row
                v.tensor_copy(li, psum[0:HL, 7, 0:S])
                link(v.tensor_copy(f, psum[0:HL, 7, S:2 * S]))
                v.scalar_tensor_tensor(out=e, in0=f, scalar=-1.0, in1=f, op0=ALU.mult, op1=ALU.max)\
                    .then_inc(f_abs, 1)
                for h in range(2):
                    v.wait_ge(yh_done, lay * 6 + (h + 1))
                    act_lo(8 + 4 * h, zy[:, 4 * h:4 * h + 4, :], 4).then_inc(yl_done, 1)
                v.wait_ge(f_exp, lay + 1)
                poly = neg_row[:, 0:S]
                log1p(e, e, t, q, poly)
                link(v.scalar_tensor_tensor(out=f, in0=f, scalar=0.0, in1=e, op0=ALU.min, op1=ALU.subtract))
                link(v.memset(t, 1.0))
                link(v.tensor_tensor_scan(q, t, f, 0.0, ALU.mult, ALU.add))
                link(v.tensor_tensor(li, li, q, ALU.subtract))
                link(v.tensor_tensor_scan(f, t, li, 0.0, ALU.mult, ALU.max))
                v.tensor_scalar(neg_row[:, 0:S], f, -1.0, None, ALU.mult)
                v.scalar_tensor_tensor(out=neg_row[:, S:2 * S], in0=f, scalar=-1.0, in1=q, op0=ALU.mult,
                                       op1=ALU.subtract).then_inc(rows_done, 1)
                v.wait_ge(cc_ready, lay + 1)
                v.tensor_copy(small[:, 16:24], psum[:, 6, 0:8]).then_inc(cc_done, 1)

                def decay(h):
                    v.wait_ge(mb_ready, lay * HL + (h + 1))
                    v.tensor_tensor(w_ml[:, h % 2, 0:256], half(2 + h % 2, 0), causal_t[:, 0:256], ALU.add)
                    v.tensor_tensor(w_ml[:, h % 2, 256:384], psum[:, 2 + h % 2, 128:256], causal_t[:, 256:384],
                                    ALU.add).then_inc(wm_ready, 1)

                decay(0)
                for h in range(HL):
                    if h + 1 < HL:
                        decay(h + 1)
                    v.wait_ge(st_ready, lay * HL + (h + 1))
                    v.wait_ge(we_ready, lay * HL + (h + 1))
                    v.scalar_tensor_tensor(out=sw_ml[:, h % 2, :], in0=psum[:, h % 2, 0:384], scalar=256 ** -0.5,
                                           in1=w_ml[:, h % 2, :], op0=ALU.mult, op1=ALU.mult)\
                        .then_inc(sw_ready, 1)
                    v.wait_ge(num_ready, lay * HL + (h + 1))
                    v.wait_ge(floor_ready, lay * HL + (h + 1))
                    link(v.tensor_tensor(den_ml, half(6 + h % 2, 0), floor_ml, ALU.max))
                    link(v.scalar_tensor_tensor(out=den_ml, in0=half(6 + h % 2, 0), scalar=-1.0,
                                                in1=den_ml, op0=ALU.mult, op1=ALU.max))
                    link(v.reciprocal(den_ml, den_ml))
                    for dv in range(2):
                        ins = v.tensor_tensor(ar_m[:, 10 + dv, :], half(4 + h % 2, dv), den_ml, ALU.mult)
                    link(ins)
                    v.tensor_tensor(so[:, 2 * h:2 * h + 2, :], so[:, 2 * h:2 * h + 2, :], ar_m[:, 10:12, :],
                                    ALU.mult).then_inc(cell_done, 1)
                v.wait_ge(cell_done, lay * HL + HL)
                for h in range(HL):
                    v.wait_ge(hstd_done, lay * HL + (h + 1))
                    link(v.reciprocal(den_ml, sq_ml[:, 2 * h, :]))
                    for dv in range(2):
                        m = 2 * h + dv
                        ins = v.scalar_tensor_tensor(out=so[:, m, :], in0=so[:, m, :], scalar=c2("head_g", m),
                                                     in1=den_ml, op0=ALU.mult, op1=ALU.mult)
                    link(ins)
                    zh = zy[:, 8 + 2 * h:10 + 2 * h, :]
                    v.tensor_tensor(zh, zh, so[:, 2 * h:2 * h + 2, :], ALU.mult).then_inc(yr_done, 1)
                for m in range(2):
                    ahead(U["out"] + m, (L,))
                for h in range(HL):
                    v.wait_ge(yh_done, lay * 6 + (h + 3))
                    act_lo(2 * h, zy[:, 8 + 2 * h:10 + 2 * h, :], 2).then_inc(yl_done, 1)
                for m in range(2, 13):
                    ahead(U["out"] + m, (L,))
                v.wait_ge(unit_used, unit_of(U["out"] + 16, (L,)))
                for m in range(KD):
                    ins = v.scalar_tensor_tensor(out=x[:, m, :], in0=half(4 + m // 2, m % 2),
                                                 scalar=mod[:, bass.ds(lay * 24 + (16 + m), 1)], in1=x[:, m, :],
                                                 op0=ALU.mult, op1=ALU.add)
                ins.then_inc(res_done, 1)
            v.wait_ge(std_done, N_FINAL + 1)
            v.reciprocal(rstd[:], std[:]).then_inc(rstd_done, 1)
            v.wait_ge(rstd_done, N_FINAL + 1)
            for j in range(KD):
                v.scalar_tensor_tensor(out=tn[:, j, :], in0=x[:, j, :], scalar=c1("final_g", j), in1=rstd[:],
                                       op0=ALU.mult, op1=ALU.mult).then_inc(tn_done, 1)

        @block.tensor
        def _(t):
            def mm3(out_ap, wh, wl, rh, rl, start, stop):
                t.matmul(out_ap, wh, rh, start=start, stop=False, skip_group_check=True)
                t.matmul(out_ap, wh, rl, start=False, stop=False, skip_group_check=True)
                return t.matmul(out_ap, wl, rh, start=False, stop=stop, skip_group_check=True)

            def unit(n, loops=(), limit=True):
                t.wait_ge(lo_done, unit_of(n + 1, loops))

            def wide(n, loops=()):
                r = n % SLOTS
                return (w_hi[:, r, :].rearrange("p (k m) -> p k m", k=8),
                        w_lo[:, r, :].rearrange("p (k m) -> p k m", k=8))

            def tile_product(n, slot, loops=()):
                unit(n, loops)
                wh, wl = wide(n)
                for k in range(KD):
                    ins = mm3(half(n % 4, 0), wh[:, k, :], wl[:, k, :], act[:, slot + k, 0, :],
                              act[:, slot + k, 1, :], k == 0, k == KD - 1)
                ins.then_inc(unit_used, 1)

            def value_pair(n, slot, loops=(), between=None):
                for u in range(2):
                    unit(n + u, loops)
                    r = (n + u) % SLOTS
                    wh = w_hi[:, r, :].rearrange("p (k m) -> p k m", k=4)
                    wl = w_lo[:, r, :].rearrange("p (k m) -> p k m", k=4)
                    for k in range(4):
                        for blk in range(2):
                            cut = slice(blk * P, blk * P + P)
                            ins = mm3(half(n % 4, blk), act[:, slot + 4 * u + k, 0, cut],
                                      act[:, slot + 4 * u + k, 1, cut], wh[:, k, :], wl[:, k, :],
                                      u == 0 and k == 0 and blk == 0, u == 1 and k == 3)
                    ins.then_inc(unit_used, 1)
                    if between:
                        between(u)

            def k_product(name, first, count, slot, done, per, loops=(), total=None):
                for k in range(first, first + count):
                    n = U[name] + k
                    unit(n, loops)
                    done(k)
                    wh, wl = wide(n)
                    for m in range(KD):
                        ins = mm3(half(4 + m // 2, m % 2), wh[:, m, :], wl[:, m, :], act[:, slot(k), 0, :],
                                  act[:, slot(k), 1, :], k == 0 and m % 2 == 0, k == total - 1)
                    ins.then_inc(unit_used, 1)

            def norm_sum(n, tiles, k, value=None):
                v0 = n if value is None else value
                if n:
                    t.wait_ge(std_done, v0)
                c = (k + 1) // 2
                for j in range(k):
                    if j == 0:
                        t.wait_ge(sq_done, v0 * 2 + 1)
                    if j == c:
                        t.wait_ge(sq_done, v0 * 2 + 2)
                    ins = t.matmul(half(4, 0), ones[:], tiles[:, j, :], start=j == 0, stop=j == k - 1)
                ins.then_inc(ss_done, 1)

            t.wait_ge(masks_done, 1)
            norm_sum(N_MEM, sq, KD)
            norm_sum(N_X, ar_g[:, 0:8, :], KD)
            for m in range(4):
                if m == 0:
                    t.wait_ge(nl_done, KD)
                tile_product(U["memk"] + m, 0)
            for m in range(2):
                taken_at(t, U["memv"] + 2 * m - 4 + 1)
                value_pair(U["memv"] + 2 * m, 0)
            t.wait_ge(nl_done, 2 * KD)
            for m in range(6):
                taken_at(t, U["latent"] + m - 3)
                tile_product(U["latent"] + m, 16)
            norm_sum(N_CQ, ar_g[:, 5:8, :], KQ)
            norm_sum(N_CKV, ar_g[:, 8:10, :], KKV)

            t.wait_ge(cact_done, 1)

            def ada_unit(col, r, value):
                t.wait_ge(ada_in[r], value)
                w = ada[:, r, :].rearrange("p (k m) -> p k m", k=8)
                out_ap = psum[:, 7, col:col + 1] if isinstance(col, int) else psum[:, 7, bass.ds(col, 1)]
                for k in range(KD):
                    ins = t.matmul(out_ap, w[:, k, :], cact[:, k:k + 1], start=k == 0, stop=k == KD - 1,
                                   skip_group_check=True)
                ins.then_inc(ada_used, 1)

            taken_at(t, U["qk"] - 1)
            with t.Fori(0, 6) as i:
                loops = ((i, 4, 6),)
                for r in range(4):
                    n = U["qk"] + r
                    ring_free(t, n, loops, U["qk"])
                    tile_product(n, 16, loops)
                    for s in ((0, 1), (2,), (3, 4), (5,))[r]:
                        ada_unit(i * 6 + s, s % 3, i * 32 + 16 * (s // 3 + 1))
            taken_at(t, U["v"] - 1)
            with t.Fori(0, 3) as i:
                loops = ((i, 4, 3),)
                for r in range(0, 4, 2):
                    n = U["v"] + r
                    ring_free(t, n, loops, U["v"])

                    def between(u, i=i, r=r):
                        if r + u < 3:
                            ada_unit(i * 3 + (36 + r + u), (r + u), i * 16 + (12 * 16 + 16))

                    value_pair(n, 16, loops, between)
            for s in range(3):
                ada_unit(45 + s, s, 16 * 16)
            t.wait_ge(nl_done, SPLIT_BEFORE[N_CKV + 1])
            for q in range(4):
                n = U["uq"] + q
                taken_at(t, n - 3)
                unit(n)
                wh, wl = (w[:, n % SLOTS, 0:768].rearrange("p (k h m) -> p k h m", k=KQ, h=2) for w in (w_hi, w_lo))
                for h in range(2):
                    for k in range(KQ):
                        ins = mm3(half(n % 4, h), wh[:, k, h, :], wl[:, k, h, :], act[:, 8 + k, 0, :],
                                  act[:, 8 + k, 1, :], k == 0, k == KQ - 1)
                ins.then_inc(unit_used, 1)
            n = U["ukvk"]
            unit(n)
            wh, wl = (w[:, n % SLOTS, :].rearrange("p (k h m) -> p k h m", k=KKV, h=4) for w in (w_hi, w_lo))
            for m in range(4):
                for k in range(KKV):
                    ins = mm3(half(4 + m // 2, m % 2), wh[:, k, m, :], wl[:, k, m, :], act[:, 11 + k, 0, :],
                              act[:, 11 + k, 1, :], k == 0, k == KKV - 1)
            ins.then_inc(unit_used, 1)
            n = U["ukvv"]
            unit(n)
            t.wait_ge(mod_done, 1)
            wh, wl = (w[:, n % SLOTS, :].rearrange("p (k m) -> p k m", k=KKV) for w in (w_hi, w_lo))
            for blk in range(2):
                cut = slice(blk * P, blk * P + P)
                for k in range(KKV):
                    ins = mm3(bank(6 + blk), act[:, 11 + k, 0, cut], act[:, 11 + k, 1, cut], wh[:, k, :],
                              wl[:, k, :], k == 0, k == KKV - 1)
            ins.then_inc(unit_used, 1)
            for m in range(4):
                n = U["memq"] + m
                taken_at(t, n - 3)
                tile_product(n, 16)

            def scores(j):
                if j in JOBS_MLA or j in JOBS_MEM:
                    if j - 2 in JOBS_MLA or j == JOBS_MEM[0]:
                        t.wait_ge(m_ready, j - 1 if j in JOBS_MLA else j)
                    elif j == JOBS_MEM[1]:
                        t.wait_ge(m_ready, j - 1)
                    elif j in JOBS_MEM:
                        t.wait_ge(e_ready, j - 1)
                elif j > JOBS_DIL[0]:
                    t.wait_ge(m_ready, j)
                if j in JOBS_MLA:
                    q, k, b = q_mla[0:96, j, :], k_mla[0:96, j, :], j % 2
                    t.matmul(psum[:, b, 0:128], q[:, 0:128], k[:, 0:128], start=True, stop=True)
                    ins = t.matmul(psum[:, b, 128:384], q[:, 128:256], k, start=True, stop=True)
                elif j in JOBS_DIL:
                    for g in range(GROUPS):
                        h = g * HD + j - JOBS_DIL[0]
                        q, k = qk_d[:, h, :], qk_d[:, 12 + h, :]
                        t.matmul(psum[:, g, 0:128], q[:, 0:128], k[:, 0:128], start=True, stop=True)
                        ins = t.matmul(psum[:, g, 128:384], q[:, 128:256], k, start=True, stop=True)
                else:
                    h = j - JOBS_MEM[0]
                    for blk in range(2):
                        ins = t.matmul(half(j % 2, blk), q_mem[:, h, blk * P:blk * P + P], k_mem[:, h, :],
                                       start=True, stop=True)
                ins.then_inc(s_ready, 1)

            def transposes(j):
                t.wait_ge(p_ready, j + 1)
                if j in JOBS_DIL and j > JOBS_DIL[0] or j == JOBS_MEM[0]:
                    t.wait_ge(pt_copied, j)
                elif j >= 2:
                    t.wait_ge(pt_copied, j - 1)
                s = s_sb[:, j % 2, :]
                if j in JOBS_MEM:
                    for q in range(2):
                        for k in range(2):
                            ins = t.transpose(psum[:, 3 + j % 2, k * S + q * P:k * S + q * P + P],
                                              s[:, q * S + k * P:q * S + k * P + P], ident[:])
                else:
                    for g in range(GROUPS if j in JOBS_DIL else 1):
                        b = 3 + g if j in JOBS_DIL else 3 + j % 2
                        for c in range(3):
                            ins = t.transpose(psum[:, b, c * P:c * P + P],
                                              s[:, 384 * g + c * P:384 * g + c * P + P], ident[:])
                ins.then_inc(pt_ready, 1)

            def weighted(j):
                t.wait_ge(pt_copied, j + 1)
                if j >= 2:
                    t.wait_ge(ol_ready, j - 1)
                b = 6 + j % 2
                if j in JOBS_MLA:
                    p = pt_sb[:, 512 * (j % 2):512 * (j % 2) + 384]
                    rows = slice(64 * (j % 2), 64 * (j % 2) + 64)
                    t.matmul(psum[rows, b, 0:256], v_mla[:, 0, 64 * j:64 * j + 64], p[:, 0:256], start=True,
                             stop=False, skip_group_check=True)
                    ins = t.matmul(psum[rows, b, 128:256], v_mla[:, 1, 64 * j:64 * j + 64], p[:, 256:384],
                                   start=False, stop=True, skip_group_check=True)
                elif j in JOBS_DIL:
                    for g in range(GROUPS):
                        h = g * HD + j - JOBS_DIL[0]
                        p = pt_sb[:, 384 * g:384 * g + 384]
                        t.matmul(psum[:, b, 0:256], v_d[:, 0, P * h:P * h + P], p[:, 0:256], start=g == 0,
                                 stop=False, skip_group_check=True)
                        ins = t.matmul(psum[:, b, 128:256], v_d[:, 1, P * h:P * h + P], p[:, 256:384],
                                       start=False, stop=g == GROUPS - 1, skip_group_check=True)
                else:
                    h = j - JOBS_MEM[0]
                    for k in range(2):
                        ins = t.matmul(psum[:, b, 0:256], v_mem[:, k, P * h:P * h + P],
                                       pt_sb[:, 512 * (j % 2) + k * S:512 * (j % 2) + k * S + S], start=k == 0,
                                       stop=k == 1)
                ins.then_inc(o_ready, 1)

            def attend(jobs):
                scores(jobs[0])
                for j in jobs:
                    if j + 1 <= jobs[-1]:
                        scores(j + 1)
                    transposes(j)
                    weighted(j)

            taken_at(t, U["memq"] + 3)
            t.wait_ge(rope_done, 4)
            attend(list(JOBS_MLA))
            t.wait_ge(pt_copied, HM)
            with t.Fori(0, 6) as i:
                loops = ((i, 4, 6),)
                for r in range(4):
                    n = U["gates"] + r
                    ring_free(t, n, loops, U["gates"])
                    tile_product(n, 16, loops)
            taken_at(t, U["gates"] + 23)
            t.wait_ge(ol_ready, HM)
            attend(list(JOBS_DIL) + list(JOBS_MEM))
            t.wait_ge(ol_ready, JOBS_MEM[-1] + 1)
            for b in range(3):
                for q in range(4):
                    n = U["branch"] + 4 * b + q
                    taken_at(t, n - 3)
                    unit(n)
                    wh, wl = (w[:, n % SLOTS, :].rearrange("p (k h m) -> p k h m", k=4, h=2) for w in (w_hi, w_lo))
                    slot = (8, 0, 4)[b]
                    for h in range(2):
                        for k in range(4):
                            ins = mm3(half(n % 4, h), wh[:, k, h, :], wl[:, k, h, :], act[:, slot + k, 0, :],
                                      act[:, slot + k, 1, :], k == 0, k == 3)
                    ins.then_inc(unit_used, 1)
            k_product("wo", 0, 8, lambda k: 16 + k, lambda k: t.wait_ge(merged_lo, k // 2 + 1), 1, total=8)
            norm_sum(N_MIX, sq, KD)
            norm_sum(N_FFN, sq, KD)
            t.wait_ge(nl_done, SPLIT_BEFORE[N_FFN + 1])
            with t.Fori(0, 11) as i:
                loops = ((i, 4, 11),)
                for r in range(4):
                    n = U["up"] + r
                    ring_free(t, n, loops, U["up"])
                    tile_product(n, 16, loops)
            t.wait_ge(z_free, 9)
            k_product("down", 0, KF, lambda k: k, lambda k: k >= 16 and t.wait_ge(al_done, (k - 16) // 2 + 1),
                      1, total=KF)
            norm_sum(N_FFN_OUT, sq, KD)

            with t.Fori(0, LAYERS) as lay:
                L = (lay, PER_LAYER, LAYERS)
                norm_sum(N_LAYER, sq, KD, lay + N_LAYER)
                for first, turns in ((0, 4), (16, 6)):
                    with t.Fori(0, turns) as i:
                        loops = (L, (i, 4, turns))
                        for r in range(4):
                            n = U["in"] + first + r
                            if r == 0 and first:
                                taken_at(t, U["in"] + first - 1, (L,))
                            elif r == 0:
                                t.wait_ge(nl_done, lay * KD + SPLIT_BEFORE[N_LAYER + 1])
                            ring_free(t, n, loops, U["in"] + first)
                            tile_product(n, 16, loops)
                for u in range(2):
                    n = U["rg"] + u
                    unit(n, (L,))
                    if u == 0:
                        t.wait_ge(xs_lo, lay * 6 + 2)
                    else:
                        taken_at(t, U["in"] + 39, (L,))
                    wh, wl = wide(n)
                    for h in range(HR):
                        ins = mm3(half((4 if u == 0 else 0) + h // 2, h % 2), wh[:, h, :], wl[:, h, :],
                                  act[:, 8 + h, 0, :], act[:, 8 + h, 1, :], True, True)
                    ins.then_inc(unit_used, 1)
                for name, slot, first in (("mlq", 16, 4), ("mlk", 16, 0), ("mlv", 0, 4)):
                    for u in range(2):
                        n = U[name] + u
                        unit(n, (L,))
                        if name == "mlq":
                            taken_at(t, U["rg"], (L,))
                            t.wait_ge(xs_lo, lay * 6 + 6)
                        elif name == "mlk":
                            taken_at(t, U["rg"] + 1, (L,))
                        else:
                            taken_at(t, U["mlq"] + u, (L,))
                        wh, wl = (w[:, n % SLOTS, :].rearrange("p (h k m) -> p h k m", h=2, k=2)
                                  for w in (w_hi, w_lo))
                        for h in range(2):
                            for m in range(2):
                                for k in range(2):
                                    s = slot + 4 * u + 2 * h + k
                                    ins = mm3(half(first + 2 * u + h, m), wh[:, h, k, m * P:m * P + P],
                                              wl[:, h, k, m * P:m * P + P], act[:, s, 0, :], act[:, s, 1, :],
                                              k == 0, k == 1)
                        ins.then_inc(unit_used, 1)
                taken_at(t, U["mlv"] + 1, (L,))
                for q in range(4):
                    for c in range(4):
                        ins = t.transpose(psum[:, q, c * P:c * P + P],
                                          v_ml[:, 4 * (q % 2) + c, (q // 2) * P:(q // 2) * P + P], ident[:])
                    ins.then_inc(vt_ready, 1)
                for blk in range(2):
                    for c in range(24):
                        src = (q_ml, k_ml, v_ml)[c // 8]
                        ins = t.matmul(psum[:, 6, 8 * blk:8 * blk + 8], src[:, c % 8, blk * P:blk * P + P],
                                       c2("w_if", 8 * c, 8), start=c == 0, stop=c == 23, skip_group_check=True)
                ins.then_inc(gt_ready, 1)

                def ml_scores(h):
                    if h == 0:
                        t.wait_ge(vt_copied, lay * 4 + 4)
                    if h >= 2:
                        t.wait_ge(sw_ready, lay * HL + (h - 1))
                    for k in range(2):
                        m = 2 * h + k
                        t.matmul(psum[:, h % 2, 0:256], k_ml[:, m, 0:128], q_ml[:, m, :], start=k == 0,
                                 stop=False, skip_group_check=True)
                    for k in range(2):
                        m = 2 * h + k
                        ins = t.matmul(psum[:, h % 2, 256:384], k_ml[:, m, 128:256], q_ml[:, m, 128:256],
                                       start=False, stop=k == 1, skip_group_check=True)
                    ins.then_inc(st_ready, 1)

                ml_scores(0)
                ml_scores(1)
                t.wait_ge(gt_done, lay + 1)
                for blk in range(2):
                    for part in range(2):
                        ins = t.transpose(psum[0:HL, 7, part * S + blk * P:part * S + blk * P + P],
                                          gate_tok[:, blk, 4 * part:4 * part + 4], ident[:])
                ins.then_inc(gr_ready, 1)
                t.wait_ge(rows_done, lay + 1)
                for blk in range(2):
                    ins = t.matmul(psum[:, 6, 4 * blk:4 * blk + 4], row[0][:, blk * P:blk * P + P],
                                   ident[0:HL, 0:HL], start=True, stop=True, skip_group_check=True)
                ins.then_inc(cc_ready, 1)

                def spread(h):
                    if h >= 2:
                        t.wait_ge(floor_ready, lay * HL + (h - 1))
                    t.matmul(bank(2 + h % 2), ident[0:HL, h:h + 1].to_broadcast([HL, P]), neg_row, start=True,
                             stop=True).then_inc(mb_ready, 1)

                spread(0)
                t.wait_ge(cc_done, lay + 1)
                for h in range(HL):
                    if h + 1 < HL:
                        spread(h + 1)
                    if h + 1 < HL and h >= 1:
                        ml_scores(h + 1)
                    t.wait_ge(sw_ready, lay * HL + (h + 1))
                    if h >= 2:
                        t.wait_ge(cell_done, lay * HL + (h - 1))
                    sw = sw_ml[:, h % 2, :]
                    for dv in range(2):
                        c = 256 * h + 128 * dv
                        t.matmul(half(4 + h % 2, dv), v_tok[:, 0, c:c + P], sw[:, 0:256], start=dv == 0, stop=False,
                                 skip_group_check=True)
                        t.matmul(psum[:, 4 + h % 2, dv * S + 128:dv * S + 256], v_tok[:, 1, c:c + P],
                                 sw[:, 256:384], start=False, stop=True, skip_group_check=True)
                    t.matmul(psum[:, 6 + h % 2, 0:256], ones[:], sw[:, 0:256], start=True, stop=False,
                             skip_group_check=True)
                    t.matmul(psum[:, 6 + h % 2, 128:256], ones[:], sw[:, 256:384], start=False, stop=True,
                             skip_group_check=True).then_inc(num_ready, 1)
                t.wait_ge(cell_done, lay * HL + HL)
                for h in range(HL):
                    t.wait_ge(hsq_done, lay * HL + (h + 1))
                    for k in range(2):
                        ins = t.matmul(half(4 + h, 0), ones[:], sq_ml[:, 2 * h + k, :], start=k == 0, stop=k == 1)
                    ins.then_inc(hss_done, 1)
                t.wait_ge(hstd_done, lay * HL + HL)
                for k in range(16):
                    n = U["out"] + k
                    unit(n, (L,))
                    if k in (0, 4):
                        t.wait_ge(yl_done, lay * 6 + (k // 4 + 1))
                    elif k >= 8 and k % 2 == 0:
                        t.wait_ge(yl_done, lay * 6 + (2 + (k - 8) // 2 + 1))
                    slot = (k + 8) % 16
                    wh, wl = wide(n)
                    for m in range(KD):
                        ins = mm3(half(4 + m // 2, m % 2), wh[:, m, :], wl[:, m, :], act[:, slot, 0, :],
                                  act[:, slot, 1, :], k == 0 and m % 2 == 0, k == 15)
                    ins.then_inc(unit_used, 1)
            norm_sum(N_FINAL, sq, KD)


def _tile_columns(w):
    k, n = w.shape
    return w.reshape(k // P, P, n // P, P).transpose(2, 1, 0, 3).reshape(n // P, P, k)


def _pack_units(i):
    w_in = i["w_in"][0]
    off_kv, off_kr = 384, 640
    off_dil, off_memq, off_gate = 672, 5280, 5792
    units = []

    def put(a):
        units.append(np.ascontiguousarray(a, np.float32))

    def value_units(w):
        n = w.shape[1] // S
        put(w.reshape(2, 4, P, n, S).transpose(3, 0, 2, 1, 4).reshape(2 * n, P, UNIT))

    w_mem = i["w_mem_kv"][0]
    put(_tile_columns(w_mem[:, :512]))
    value_units(w_mem[:, 512:])
    put(_tile_columns(w_in[:, :off_kr]))
    kr = w_in[:, off_kr:off_dil]
    last = np.zeros((D, P), np.float32)
    last[:, 64:96] = kr
    last[:, 96:112] = kr[:, 16:]
    last[:, 112:128] = kr[:, :16]
    put(_tile_columns(last))
    dil = w_in[:, off_dil:off_memq]
    put(_tile_columns(dil[:, :3072]))
    value_units(dil[:, 3072:])
    uq = i["w_uq"][0].reshape(KQ, P, HM, NOPE + ROPE)
    full = np.zeros((KQ, P, HM, P), np.float32)
    full[..., :96] = uq
    full[..., 96:112] = uq[..., 80:96]
    full[..., 112:128] = uq[..., 64:80]
    uq_units = np.zeros((4, P, UNIT), np.float32)
    uq_units[:, :, :768] = full.reshape(KQ, P, 4, 2, P).transpose(2, 1, 0, 3, 4).reshape(4, P, 768)
    put(uq_units)
    ukv = i["w_ukv"][0].reshape(KKV, P, HM, NOPE + VM)
    put(ukv[..., :NOPE].transpose(1, 0, 2, 3).reshape(1, P, UNIT))
    put(ukv[..., NOPE:].transpose(1, 0, 2, 3).reshape(1, P, UNIT))
    put(_tile_columns(w_in[:, off_memq:off_gate]))
    put(_tile_columns(w_in[:, off_gate:]))
    for name in ("w_br_mla", "w_br_dil", "w_br_mem"):
        w = i[name][0]
        put(w.reshape(4, P, 4, 2, P).transpose(2, 1, 0, 3, 4).reshape(4, P, UNIT))
    put(i["w_o"][0].reshape(KD, P, D))
    up = i["w_ffn_up"][0]
    g, v = _tile_columns(up[:, :FF]), _tile_columns(up[:, FF:])
    put(np.stack([g, v], 1).reshape(2 * KF, P, UNIT))
    put(i["w_ffn_down"][0].reshape(KF, P, D))
    for lay in range(LAYERS):
        w = i["w_in_2"][lay]
        for a in (0, 2, 1, 4, 3):
            put(_tile_columns(w[:, a * D:(a + 1) * D]))
        for name in ("rg_w_a_2", "rg_w_x_2"):
            put(i[name][lay].transpose(1, 0, 2).reshape(1, P, UNIT))
        for name in ("ml_w_q_2", "ml_w_k_2", "ml_w_v_2"):
            put(i[name][lay].reshape(2, 2, 2, P, 256).transpose(0, 3, 1, 2, 4).reshape(2, P, UNIT))
        put(i["w_out_2"][lay].reshape(16, P, D))
    out = np.concatenate(units)
    assert out.shape == (NU, P, UNIT), out.shape
    return out


def _col(a):
    return np.ascontiguousarray(a.reshape(-1, P).T)


def _pack_params(i):
    par1 = np.zeros((P, NP1), np.float32)

    def put(par, cols, name, a):
        at, n = cols[name]
        assert a.shape == (P, n), (name, a.shape, n)
        par[:, at:at + n] = a

    for name, key in (("g_pre_mix", "g_pre_mix"), ("g_mem", "g_mem"), ("q_norm", "mla_q_norm"),
                      ("kv_norm", "mla_kv_norm"), ("b_gate", "b_gate"), ("g_post_mix", "g_post_mix"),
                      ("g_pre_ffn", "g_pre_ffn"), ("g_post_ffn", "g_post_ffn"), ("c", "c_2"),
                      ("b_ada", "b_ada_2"), ("final_g", "final_g_2")):
        put(par1, C1, name, _col(i[key]))
    w = i["conv_w"][0].reshape(3, 2, KF, P).transpose(0, 2, 1, 3)
    put(par1, C1, "conv_w", _col(w))
    put(par1, C1, "conv_b", _col(i["conv_b"][0].reshape(2, KF, P).transpose(1, 0, 2)))
    half_dim = ROPE // 2
    freq = np.float32(10000.0) ** (-np.arange(half_dim, dtype=np.float32) / np.float32(half_dim))
    put(par1, C1, "freq", np.tile(freq.astype(np.float32), P // half_dim)[:, None])
    put(par1, C1, "sign", np.tile(np.repeat([-1.0, 1.0], half_dim), P // ROPE)[:, None])
    par2 = np.zeros((LAYERS, P, NP2), np.float32)
    for lay in range(LAYERS):
        for name, key in (("norm_g", "norm_g_2"), ("rg_w", "rg_conv_w_2"), ("rg_b", "rg_conv_b_2"),
                          ("b_a", "rg_b_a_2"), ("b_x", "rg_b_x_2"), ("lam", "rg_lambda_2"),
                          ("ml_w", "ml_conv_w_2"), ("ml_b", "ml_conv_b_2"), ("head_g", "ml_norm_g_2")):
            put(par2[lay], C2, name, _col(i[key][lay]))
        put(par2[lay], C2, "b_if", np.broadcast_to(i["ml_b_if_2"][lay], (P, 2 * HL)))
        put(par2[lay], C2, "w_if", i["ml_w_if_2"][lay].reshape(24, P, 2 * HL).transpose(1, 0, 2).reshape(P, -1))
    return par1, par2


def kernel(**inputs):
    import concourse.bacc as bacc
    from concourse.bass_utils import run_bass_kernel_spmd

    i = {k: np.asarray(v) for k, v in inputs.items()}

    def features(a):
        return np.ascontiguousarray(a[0].T.reshape(KD, P, S).transpose(1, 0, 2))

    par1, par2 = _pack_params(i)
    arrays = {
        "w_units": _pack_units(i),
        "w_ada": np.concatenate([_tile_columns(i["w_ada_2"][lay]) for lay in range(LAYERS)]),
        "x_in": features(i["x"]),
        "mem_in": features(i["mem"]),
        "pos_in": np.ascontiguousarray(np.broadcast_to(i["positions"].astype(np.int32), (P, S))),
        "par1_in": par1,
        "par2_in": par2,
    }
    nc = bacc.Bacc("TRN2", target_bir_lowering=False, num_devices=1)
    args = {n: nc.dram_tensor(n, a.shape, mybir.dt.from_np(a.dtype), kind="ExternalInput").ap()
            for n, a in arrays.items()}
    out = nc.dram_tensor("out", (P, KD, S), F32, kind="ExternalOutput").ap()
    program(nc, out=out, **args)
    r = run_bass_kernel_spmd(nc, [arrays], core_ids=[0])
    y = r.results[0]["out"]
    return np.ascontiguousarray(y.transpose(1, 0, 2).reshape(D, S).T)[None]
```

```python
from contextlib import ExitStack, contextmanager

import concourse.bass as bass
import numpy as np
from concourse import mybir

F32 = mybir.dt.float32
F32R = mybir.dt.float32r
I32 = mybir.dt.int32
ACT = mybir.ActivationFunctionType
ALU = mybir.AluOpType
AX = mybir.AxisListType

P = 128
S = 256
D = 1024
KD = D // P
EPS = 1e-6
NEG = -1e30
UNIT = 1024
SLOTS = 4

HM, NOPE, ROPE, VM = 8, 64, 32, 64
KQ, KKV = 3, 2
GROUPS, HD, DH = 3, 4, 128
DILATION = (1, 4, 16)
SPAN = 128
FF = 2816
KF = FF // P
LAYERS = 2
HR = 8
HL = 4
RG_C = 8.0

_ORDER = (("memk", 4), ("memv", 4), ("latent", 6), ("qk", 24), ("v", 12), ("uq", 4), ("ukvk", 1), ("ukvv", 1),
          ("memq", 4), ("gates", 24), ("branch", 12), ("wo", 8), ("up", 2 * KF), ("down", KF))
_LAYER = (("conv", 16), ("rg", 2), ("z", 8), ("mlq", 2), ("mlk", 2), ("mlv", 2), ("late", 16), ("out", 16))
U = {}
_at = 0
for _n, _c in _ORDER:
    U[_n] = _at
    _at += _c
LAYER0 = _at
for _n, _c in _LAYER:
    U[_n] = _at
    _at += _c
PER_LAYER = _at - LAYER0
NU = LAYER0 + LAYERS * PER_LAYER


def _owners():
    own = ["a"] * NU

    def put(first, what):
        own[first:first + len(what)] = list(what)

    put(U["memv"], ".a" * 2)
    put(U["latent"] + 5, "v")
    put(U["v"], ".a" * 6)
    put(U["uq"], "v" * 4)
    put(U["branch"], "v" * 12)
    put(U["wo"], "." * 8)
    put(U["up"], "v" * 2 * KF)
    put(U["down"], "." * KF)
    for lay in range(LAYERS):
        o = lay * PER_LAYER
        put(U["conv"] + o, "v" * 16)
        put(U["mlk"] + o, "v" * 2)
        put(U["out"] + o, "." * 16)
    return own


OWNER = _owners()
TAKEN = {e: [sum(o == e for o in OWNER[:n + 1]) for n in range(NU)] for e in "av"}

LAYER_A = TAKEN["a"][LAYER0 + PER_LAYER] - TAKEN["a"][LAYER0]

_C1 = (("g_pre_mix", KD), ("g_mem", KD), ("q_norm", KQ), ("kv_norm", KKV), ("b_gate", 24), ("g_post_mix", KD),
       ("g_pre_ffn", KD), ("conv_w", 3 * 2 * KF), ("conv_b", 2 * KF), ("g_post_ffn", KD),
       ("b_ada", 24 * LAYERS), ("freq", 1), ("sign", 1), ("final_g", KD))
_C2 = (("norm_g", KD), ("rg_w", 4 * KD), ("rg_b", KD), ("b_a", KD), ("b_x", KD), ("lam", KD), ("ml_w", 4 * KD),
       ("ml_b", KD), ("head_g", KD), ("b_if", 2 * HL), ("w_if", 24 * 2 * HL))


def _columns(spec):
    at, out = 0, {}
    for name, n in spec:
        out[name] = (at, n)
        at += n
    return out, at


C1, NP1 = _columns(_C1)
C2, NP2 = _columns(_C2)

NORMS = [(KD, True), (KD, True), (KQ, True), (KKV, True), (KD, False), (KD, True), (KD, False),
         (KD, True), (KD, True), (KD, False)]
N_MEM, N_X, N_CQ, N_CKV, N_MIX, N_FFN, N_FFN_OUT, N_LAYER, N_FINAL = 0, 1, 2, 3, 4, 5, 6, 7, 9
SPLIT_BEFORE = [sum(k for k, s in NORMS[:n] if s) for n in range(len(NORMS) + 1)]
SQUARES_BEFORE = [sum((k + 1) // 2 for k, _ in NORMS[:n]) for n in range(len(NORMS) + 1)]
PAIRS = KD // 2

FIRST_UNITS = [LAYER0 + lay * PER_LAYER + m for lay in range(LAYERS + 1) for m in range(3)]

ADA_BETWEEN = ((0, 1), (2,), (3, 4), (5,))

JOBS_DIL, JOBS_MLA, JOBS_MEM = range(0, HD), range(HD, HD + HM), range(HD + HM, 2 * HD + HM)


def affine(need, limit):
    for d in {b - a for a, b in zip(need, need[1:])} | {0}:
        a = max(x - d * i for i, x in enumerate(need))
        if all(a + d * i <= y for i, y in enumerate(limit)):
            return a, d
    raise ValueError(f"no line between {need} and {limit}")


def program(nc, w_units, w_ada, x_in, mem_in, pos_in, c_in, par1_in, par2_in, out):
    ctx = ExitStack()
    with ctx:
        def sb(name, shape, dt=F32):
            return ctx.enter_context(nc.sbuf_tensor(name, shape, dt))

        def sem(name):
            return ctx.enter_context(nc.semaphore(name))

        raw = sb("raw", [P, SLOTS, UNIT])
        w_hi = sb("w_hi", [P, SLOTS, UNIT], F32R)
        w_lo = sb("w_lo", [P, SLOTS, UNIT], F32R)
        act = sb("act", [P, 24, 2, S], F32R)
        x = sb("x", [P, KD, S])
        ar_d = sb("ar_d", [P, 36, S])
        ar_g = sb("ar_g", [P, 24, S])
        ar_m = sb("ar_m", [P, 12, S])
        ar_p = sb("ar_p", [P, 3456])
        dist = sb("dist", [P, GROUPS, 384])
        causal = sb("causal", [P, 384])
        causal_t = sb("causal_t", [P, 384])
        ident = sb("ident", [P, P])
        ones = sb("ones", [P, P])
        std = sb("std", [P, S])
        rstd = sb("rstd", [P, S])
        par1 = sb("par1", [P, NP1])
        par2 = sb("par2", [P, NP2])
        mod = sb("mod", [P, 24 * LAYERS])
        small = sb("small", [P, 64])
        tiny = sb("tiny", [P, 24])
        psum = ctx.enter_context(nc.psum_tensor("psum", [P, 8, 512], F32))
        eps = tiny[:, 0:1]
        halfpi = tiny[:, 1:2]

        def c1(name, j=0, n=1):
            at = C1[name][0]
            if isinstance(j, int):
                return par1[:, at + j:at + j + n]
            return par1[:, bass.ds(j + at, n)]

        def c2(name, j=0, n=1):
            at = C2[name][0]
            return par2[:, at + j:at + j + n]

        def flat(ap):
            return ap.rearrange("p a b -> p (a b)")

        memx = ar_d[:, 0:8, :]
        latent = ar_g[:, 0:5, :]
        qk_d = ar_d[:, 0:24, :]
        v_d = ar_d[:, 24:36, :].rearrange("p a b -> p (a b)").rearrange("p (s n) -> p s n", s=2)
        q_mla = ar_g[:, 0:8, :]
        k_mla = ar_g[:, 8:16, :]
        v_mla = flat(ar_g[:, 16:20, :]).rearrange("p (s n) -> p s n", s=2)
        cos_t = ar_g[:, 20, :]
        sin_t = ar_g[:, 21, :]
        rope_tmp = ar_g[:, 22:24, :]
        k_mem = ar_m[:, 0:4, :]
        v_mem = flat(ar_m[:, 4:8, :]).rearrange("p (s n) -> p s n", s=2)
        q_mem = ar_m[:, 8:12, :]
        cact = flat(q_mem)
        ada = ar_p[:, 0:3072].rearrange("p (r n) -> p r n", r=3)
        s_sb = ar_p[:, 0:2304].rearrange("p (r n) -> p r n", r=2)
        pt_sb = ar_p[:, 2304:3456]
        gates = ar_d[:, 0:24, :]
        merged = ar_d[:, 24:32, :]
        branch_y = ar_d[:, 32:36, :]
        sq = ar_d[:, 16:24, :]
        tn = ar_d[:, 24:32, :]
        late = ar_g[:, 0:6, :]
        z_up = ar_p[:, 0:1024].rearrange("p (r n) -> p r n", r=4)
        u_rg = ar_d[:, 0:8, :]
        xc = ar_d[:, 8:16, :]
        xm = ar_d[:, 16:24, :]
        so = ar_d[:, 24:32, :]
        zy = ar_g[:, 0:16, :]
        k_ml = ar_g[:, 16:24, :]
        q_ml = ar_m[:, 0:8, :]
        rg_r = so
        rg_sq = xc
        rg_t = ar_p[:, 0:2048].rearrange("p (a b) -> p a b", b=S)
        rg_i = (ar_m[:, 8:12, :], ar_d[:, 32:36, :])
        v_ml = u_rg
        v_tok = flat(xm).rearrange("p (s n) -> p s n", s=2)
        sq_ml = xc
        row = [ar_p[0:HL, 2048 + S * i:2048 + S * (i + 1)] for i in range(5)]
        neg_row = flat(ar_m[0:HL, 8:10, :])
        gate_tok = small[:, 0:16].rearrange("p (s g) -> p s g", s=2)
        c_col = small[:, 16:24].rearrange("p (s h) -> p s h", s=2)
        w_ml = ar_p[:, 0:768].rearrange("p (r n) -> p r n", r=2)
        sw_ml = ar_p[:, 768:1536].rearrange("p (r n) -> p r n", r=2)
        floor_ml = ar_p[:, 1536:1792]
        den_ml = ar_p[:, 1792:2048]
        soft = tiny[:, 8:16]
        nsoft = tiny[:, 16:24]
        gain2 = small[:, 24:32]
        t8 = [small[:, 32 + 8 * i:40 + 8 * i] for i in range(4)]

        def bank(b):
            return psum[:, b, :]

        def half(b, m):
            return psum[:, b, m * S:(m + 1) * S]

        def stat(j, q, k):
            at = (j % 2) * 8 + k * 2
            return small[:, at:at + 2] if q is None else small[:, at + q:at + q + 1]

        def score_views(j):
            s = s_sb[:, j % 2, :]
            if j in JOBS_MLA:
                views = [s[:, 0:128], s[:, 128:384]]
            elif j in JOBS_DIL:
                s = s.rearrange("p (g n) -> p g n", g=3)
                views = [s[:, :, 0:128], s[:, :, 128:384]]
            else:
                return [(psum[:, j % 2, q * S:(q + 1) * S], s[:, q * S:(q + 1) * S]) for q in range(2)]
            return [(v, v) for v in views]

        def head_rows(j):
            if j in JOBS_MLA:
                h = j - JOBS_MLA[0]
                return 64 * (h % 2), 64 * (h % 2) + 64, 8 + h // 2
            return 0, P, j if j in JOBS_DIL else HD + j - JOBS_MEM[0]

        def gate_unit(j, second):
            return U["gates"] + 2 * (j - JOBS_MLA[0]) + second

        def gate_bank(n):
            return half((2, 5)[n % 2], 0)

        raw_in = [sem(f"raw_in{r}") for r in range(SLOTS)]
        ada_in = [sem(f"ada_in{r}") for r in range(3)]
        c_in_s, x_in_s, mem_in_s, par_in, par2_in_s, pos_in_s, out_s = (sem(n) for n in (
            "c_landed", "x_landed", "mem_landed", "par1_landed", "par2_landed", "pos_landed", "out_landed"))
        hi_done, lo_done, unit_used = sem("hi_done"), sem("lo_done"), sem("unit_used")
        taken = {"a": sem("taken_act"), "v": sem("taken_dve")}
        ada_used, mod_done, cact_done = sem("ada_used"), sem("mod_done"), sem("cact_done")
        sq_done, ss_done, std_done, rstd_done = (sem(n) for n in ("sq_done", "ss_done", "std_done", "rstd_done"))
        tn_done, nh_done, nl_done, res_done = (sem(n) for n in ("tn_done", "nh_done", "nl_done", "res_done"))
        masks_done, tables_done, rope_done, k_pe_done = (sem(n) for n in (
            "masks_done", "tables_done", "rope_done", "k_pe_done"))
        angle_done, sine_done = sem("angle_done"), sem("sine_done")
        s_ready, m_ready, e_ready, p_ready, pt_ready, pt_copied, o_ready, oh_ready, ol_ready = (
            sem(n) for n in ("s_ready", "m_ready", "e_ready", "p_ready", "pt_ready", "pt_copied", "o_ready",
                             "oh_ready", "ol_ready"))
        merge_done, mh_done, merged_lo = sem("merge_done"), sem("mh_done"), sem("merged_lo")
        gates_done = sem("gates_done")
        q_nope = sem("q_nope")
        z_init, z_free, silu_done, prod_done, ah_done, al_done = (sem(n) for n in (
            "z_init", "z_free", "silu_done", "prod_done", "ah_done", "al_done"))
        (xc_silu, xs_hi, xs_lo, rg_tanh, rg_exp, rg_arg, rg_sqrt, yr_done, yh_done, yl_done, sp_exp, sp_done,
         vt_ready, vt_copied, gt_ready, gt_done, gr_ready, f_abs, f_exp, rows_done, cc_ready, cc_done,
         mb_ready, wm_ready, we_ready, floor_ready, st_ready, sw_ready, num_ready, cell_done, hsq_done, hss_done,
         hstd_done) = (sem(n) for n in (
             "xc_silu", "xs_hi", "xs_lo", "rg_tanh", "rg_exp", "rg_arg", "rg_sqrt", "y_done", "yh_done",
             "yl_done", "sp_exp", "sp_done", "vt_ready", "vt_copied", "gt_ready", "gt_done", "gr_ready",
             "f_abs", "f_exp", "rows_done", "cc_ready", "cc_done", "mb_ready", "wm_ready", "we_ready",
             "floor_ready", "st_ready", "sw_ready", "num_ready", "cell_done", "hsq_done", "hss_done", "hstd_done"))
        dve_step, act_step, pool_step = sem("dve_step"), sem("act_step"), sem("pool_step")

        block = ctx.enter_context(nc.Block())

        class Step:

            def __init__(self, eng, semaphore):
                self.eng, self.sem, self.n, self.off, self.scratch = eng, semaphore, 0, 0, None

            def link(self, ins):
                self.n += 1
                ins.then_inc(self.sem, 1)
                self.eng.wait_ge(self.sem, self.off + self.n)

            @contextmanager
            def turns(self, reg, n, per):
                start, off = self.n, self.off
                self.off = reg * per + off
                yield
                assert self.n - start == per, (self.n - start, per)
                self.n, self.off = start + n * per, off

        def taken_at(eng, n, loops=(), limit=None):
            for e in "av":
                points = [0]
                for _, step, turns in loops:
                    points = [o + step * i for o in points for i in range(turns)]
                need = [TAKEN[e][n + o] for o in points]
                most = [TAKEN[e][(limit or n) + o] for o in points]
                if need[-1] == 0:
                    continue
                value = None
                if not loops:
                    value = need[0]
                elif len(loops) == 1:
                    a, d = affine(need, most)
                    value = loops[0][0] * d + a if d else a
                else:
                    (lay, step, n0), (reg, _, n1) = loops
                    delta = TAKEN[e][n + step + loops[1][1] * (n1 - 1)] - TAKEN[e][n + loops[1][1] * (n1 - 1)]
                    need = [max(need[i + n1 * j] - delta * j for j in range(n0)) for i in range(n1)]
                    most = [min(most[i + n1 * j] - delta * j for j in range(n0)) for i in range(n1)]
                    a, d = affine(need, most)
                    value = reg * d + lay * delta + a if d else lay * delta + a
                if isinstance(value, int) and value <= 0:
                    continue
                eng.wait_ge(taken[e], value)

        def ring_free(eng, n, loops, start):
            turns, step = loops[-1][2], loops[-1][1]
            for e in "av":
                need = [TAKEN[e][n - 3 + step * i] for i in range(1, turns)]
                if need[-1] <= TAKEN[e][start - 1]:
                    continue
                most = [TAKEN[e][n - 1 + step * i] for i in range(1, turns)]
                if turns == 2:
                    a, d = affine([TAKEN[e][n - 3]] + need, [TAKEN[e][n - 1]] + most)
                    a += d
                else:
                    a, d = affine(need, most)
                assert 0 < a - d <= TAKEN[e][n - 1]
                value = loops[-1][0] * d + (a - d)
                if len(loops) == 2:
                    value = loops[0][0] * (TAKEN[e][n + loops[0][1]] - TAKEN[e][n]) + value
                eng.wait_ge(taken[e], value)

        def unit_of(n, loops=()):
            for reg, step, _ in loops:
                n = reg * step + n
            return n

        def landed(n, loops=()):
            v = 16 * (n // SLOTS + 1)
            for reg, step, _ in loops:
                v = reg * (16 * step // SLOTS) + v
            return v

        @block.sync
        def _(sp):
            sp.dma_start(memx, mem_in).then_inc(mem_in_s, 16)
            sp.dma_start(x[:], x_in).then_inc(x_in_s, 16)
            sp.dma_start(raw[:, 0, :], w_units[0]).then_inc(raw_in[0], 16)
            sp.dma_start(raw[:, 1, :], w_units[1]).then_inc(raw_in[1], 16)
            sp.dma_start(raw[:, 2, :], w_units[2]).then_inc(raw_in[2], 16)
            sp.dma_start(raw[:, 3, :], w_units[3]).then_inc(raw_in[3], 16)
            for s in range(3):
                sp.dma_start(ada[:, s, :], w_ada[s]).then_inc(ada_in[s], 16)

            def weights(i, group, r):
                at = i * SLOTS + (group * SLOTS + r + 1)
                sp.wait_ge(lo_done, at)
                sp.dma_start(raw[:, r, :], w_units[bass.ds(at + (SLOTS - 1), 1)].rearrange("a p n -> p (a n)"))\
                    .then_inc(raw_in[r], 16)

            def modulation(k, slot):
                sp.wait_ge(ada_used, k + (-2))
                sp.dma_start(ada[:, slot, :], w_ada[bass.ds(k, 1)].rearrange("a p n -> p (a n)"))\
                    .then_inc(ada_in[slot], 16)

            with sp.Fori(0, 4) as i:
                for r in range(SLOTS):
                    weights(i, 0, r)
            for s in range(3):
                sp.wait_ge(ada_used, s + 1)
                sp.dma_start(ada[:, s, :], w_ada[3 + s]).then_inc(ada_in[s], 16)
            with sp.Fori(0, 6) as i:
                for r in range(SLOTS):
                    weights(i, 4, r)
                    for s in ADA_BETWEEN[r]:
                        modulation(i * 6 + (6 + s), s % 3)
            with sp.Fori(0, 2) as i:
                for r in range(SLOTS):
                    weights(i, 10, r)
                    if r < 3:
                        modulation(i * 3 + (42 + r), r)
            with sp.Fori(0, NU // SLOTS - 1 - 12) as i:
                for r in range(SLOTS):
                    weights(i, 12, r)
            for n in range(NU // SLOTS * SLOTS, NU):
                sp.wait_ge(lo_done, n - SLOTS + 1)
                sp.dma_start(raw[:, n % SLOTS, :], w_units[n]).then_inc(raw_in[n % SLOTS], 16)
            sp.wait_ge(tn_done, SPLIT_BEFORE[-1] + KD)
            sp.dma_start(out, tn[:]).then_inc(out_s, 16)
            sp.wait_ge(out_s, 16)

        @block.gpsimd
        def _(pool):
            step = Step(pool, pool_step)
            link = step.link
            g = nc.gpsimd
            link(g.memset(ident[:], 0.0))
            link(g.affine_select(out=ident[:], in_=ident[:], compare_op=ALU.not_equal, fill=1.0, base=0,
                                 pattern=[[-1, P]], channel_multiplier=1))
            link(g.memset(causal[:], 0.0))
            link(g.memset(causal_t[:], 0.0))
            link(g.affine_select(out=causal[:, 0:128], in_=causal[:, 0:128], compare_op=ALU.is_ge, fill=NEG,
                                 base=0, pattern=[[-1, 128]], channel_multiplier=1))
            link(g.affine_select(out=causal[:, 128:384], in_=causal[:, 128:384], compare_op=ALU.is_ge, fill=NEG,
                                 base=128, pattern=[[-1, 256]], channel_multiplier=1))
            for a in (0, 256):
                link(g.affine_select(out=causal_t[:, a:a + 128], in_=causal_t[:, a:a + 128], compare_op=ALU.is_ge,
                                     fill=NEG, base=0, pattern=[[1, 128]], channel_multiplier=-1))
            di = dist[:, 0, :].bitcast(I32)
            link(g.iota(di[:, 0:128], pattern=[[-1, 128]], base=0, channel_multiplier=1))
            link(g.iota(di[:, 128:384], pattern=[[-1, 256]], base=128, channel_multiplier=1))
            g.memset(ones[:], 1.0).then_inc(masks_done, 1)
            for lay in range(LAYERS):
                if lay:
                    pool.wait_ge(res_done, (2 + lay) * PAIRS)
                pool.dma_start(par2[:], par2_in[lay]).then_inc(par2_in_s, 16)

        @block.scalar
        def _(a):
            step = Step(a, act_step)
            link = step.link
            hold_reg = a.alloc_register("act_hold")
            a.reg_mov(hold_reg, 0)

            def wait(semaphore, value):
                a.wait_ge(semaphore, value)
                if not isinstance(value, int):
                    a.reg_add(hold_reg, hold_reg, 0)

            def hi(n, loops=()):
                a.wait_ge(raw_in[n % SLOTS], landed(n, loops))
                if n >= SLOTS:
                    a.wait_ge(unit_used, unit_of(n - SLOTS + 1, loops))
                a.activation(w_hi[:, n % SLOTS, :], raw[:, n % SLOTS, :], ACT.Copy).then_inc(hi_done, 1)

            def ahead(n, loops=()):
                if n + 3 not in FIRST_UNITS:
                    hi(n + 3, loops)

            def product(n, loops=()):
                wait(unit_used, unit_of(n + 1, loops))

            def norm_square(n, src, dst, k):
                if n:
                    a.wait_ge(ss_done, n)
                for j in range(0, k, 2):
                    a.activation(dst[:, j:min(j + 2, k), :], src[:, j:min(j + 2, k), :], ACT.Square)\
                        .then_inc(sq_done, 1)

            def residual_square(norms, residuals):
                a.wait_ge(ss_done, norms)
                for c in range(PAIRS):
                    a.wait_ge(res_done, residuals * PAIRS + (c + 1))
                    a.activation(sq[:, 2 * c:2 * c + 2, :], x[:, 2 * c:2 * c + 2, :], ACT.Square)\
                        .then_inc(sq_done, 1)

            def norm_std(n, k, lay=0, at=4):
                a.wait_ge(ss_done, lay + (n + 1))
                if n:
                    a.wait_ge(rstd_done, lay + n)
                a.activation(std[:], half(at, 0), ACT.Sqrt, bias=eps, scale=1.0 / (k * P)).then_inc(std_done, 1)

            def norm_hi(n, k, slot, src):
                for j in range(k):
                    a.wait_ge(tn_done, SPLIT_BEFORE[n] + j + 1)
                    a.activation(act[:, slot + j, 0, :], src[:, j, :], ACT.Copy).then_inc(nh_done, 1)

            a.dma_start(par1[:], par1_in).then_inc(par_in, 16)
            a.dma_start(cact, c_in).then_inc(c_in_s, 16)
            a.dma_start(ar_g[:, 20, :].bitcast(I32), pos_in).then_inc(pos_in_s, 16)
            a.wait_ge(mem_in_s, 16)
            norm_square(N_MEM, memx, sq, KD)
            hi(0)
            a.wait_ge(x_in_s, 16)
            for j in range(0, KD, 2):
                a.activation(ar_g[:, j:j + 2, :], x[:, j:j + 2, :], ACT.Square).then_inc(sq_done, 1)
            hi(1)
            hi(2)
            a.wait_ge(tables_done, 1)
            norm_std(N_MEM, KD)
            norm_std(N_X, KD)
            norm_hi(N_MEM, KD, 0, tn)
            ahead(U["memk"])
            norm_hi(N_X, KD, 16, ar_g[:, 8:16, :])
            ahead(U["memk"] + 1)
            ahead(U["memk"] + 2)
            for m in range(4):
                n = U["memk"] + m
                product(n)
                if m == 1:
                    ahead(U["memk"] + 3)
                elif m == 2:
                    a.wait_ge(angle_done, 1)
                    a.activation(cos_t[64:96, :], rope_tmp[64:96, 0, :], ACT.Sin, scale=0.5).then_inc(sine_done, 1)
                    a.activation(sin_t[96:128, :], rope_tmp[96:128, 0, :], ACT.Sin).then_inc(sine_done, 1)
                a.activation(k_mem[:, m, :], half(n % 4, 0), ACT.Copy).then_inc(taken["a"], 1)
            for m in range(2):
                n = U["memv"] + 2 * m
                ahead(n)
                ahead(n + 1)
                product(n + 1)
                a.activation(v_mem[:, :, m * S:(m + 1) * S], bank(n % 4).rearrange("p (s n) -> p s n", s=2),
                             ACT.Copy).then_inc(taken["a"], 1)
            a.wait_ge(c_in_s, 16)
            a.activation(cact, cact, ACT.Silu).then_inc(cact_done, 1)
            for m in range(5):
                n = U["latent"] + m
                ahead(n)
                product(n)
                if m == 0:
                    a.wait_ge(nl_done, 2 * KD)
                ins = a.activation(latent[:, m, :], half(n % 4, 0), ACT.Copy).then_inc(taken["a"], 1)
                if m == KQ - 1:
                    a.wait_ge(taken["a"], TAKEN["a"][n])
                    norm_square(N_CQ, latent[:, 0:KQ, :], ar_g[:, 5:8, :], KQ)
            a.wait_ge(taken["a"], TAKEN["a"][U["latent"] + 4])
            norm_square(N_CKV, latent[:, KQ:5, :], ar_g[:, 8:10, :], KKV)
            ahead(U["latent"] + 5)
            norm_std(N_CQ, KQ)
            norm_std(N_CKV, KKV)
            norm_hi(N_CQ, KQ, 8, ar_g[:, 10:13, :])
            norm_hi(N_CKV, KKV, 11, ar_g[:, 13:15, :])

            with a.Fori(0, 6) as i:
                loops = ((i, 4, 6),)
                for r in range(4):
                    n = U["qk"] + r
                    ahead(n, loops)
                    product(n, loops)
                    a.activation(qk_d[:, bass.ds(i * 4 + r, 1), :].rearrange("p a n -> p (a n)"), half(n % 4, 0),
                                 ACT.Copy).then_inc(taken["a"], 1)
            with a.Fori(0, 3) as i:
                loops = ((i, 4, 3),)
                for r in range(0, 4, 2):
                    n = U["v"] + r
                    ahead(n, loops)
                    ahead(n + 1, loops)
                    product(n + 1, loops)
                    a.activation(v_d[:, :, bass.ds(i * 2 * S + r // 2 * S, S)],
                                 bank(n % 4).rearrange("p (s n) -> p s n", s=2), ACT.Copy).then_inc(taken["a"], 1)

            a.wait_ge(nl_done, SPLIT_BEFORE[N_CKV + 1])
            for m in range(4):
                n = U["uq"] + m
                ahead(n)
                product(n)
                a.activation(q_mla[0:64, 2 * m:2 * m + 2, :], psum[0:64, n % 4, :].rearrange(
                    "p (h t) -> p h t", h=2), ACT.Copy).then_inc(q_nope, 1)
            n = U["ukvk"]
            ahead(n)
            product(n)
            for m in range(4):
                for hh in range(2):
                    ins = a.activation(k_mla[0:64, 2 * m + hh, :], psum[64 * hh:64 * hh + 64, 4 + m // 2,
                                                                      (m % 2) * S:(m % 2 + 1) * S], ACT.Copy)
            ins.then_inc(taken["a"], 1)
            n = U["ukvv"]
            ahead(n)
            product(n)
            a.wait_ge(k_pe_done, 1)
            for blk in range(2):
                ins = a.activation(v_mla[:, blk, :], bank(6 + blk), ACT.Copy)
            ins.then_inc(taken["a"], 1)
            a.wait_ge(mod_done, 1)
            for m in range(4):
                n = U["memq"] + m
                ahead(n)
                product(n)
                a.activation(q_mem[:, m, :], half(n % 4, 0), ACT.Copy).then_inc(taken["a"], 1)

            def exps(j):
                a.wait_ge(m_ready, j + 1)
                scale = (NOPE + ROPE) ** -0.5 if j in JOBS_MLA else DH ** -0.5
                for q, (src, dst) in enumerate(score_views(j)):
                    ins = a.activation(dst, src, ACT.Exp, bias=stat(j, q, 2), scale=scale, accum_out=stat(j, q, 3))
                ins.then_inc(e_ready, 1)

            def copy_pt(j):
                a.wait_ge(pt_ready, j + 1)
                if 0 < j <= JOBS_MLA[0]:
                    a.wait_ge(o_ready, j)
                elif j:
                    a.wait_ge(o_ready, j - 1)
                if j in JOBS_DIL:
                    a.activation(pt_sb.rearrange("p (g n) -> p g n", g=3), psum[:, 3:6, 0:384], ACT.Copy)\
                        .then_inc(pt_copied, 1)
                else:
                    n = 384 if j in JOBS_MLA else 512
                    a.activation(pt_sb[:, 512 * (j % 2):512 * (j % 2) + n], psum[:, 3 + j % 2, 0:n], ACT.Copy)\
                        .then_inc(pt_copied, 1)

            def out_hi(j):
                a.wait_ge(o_ready, j + 1)
                lo_p, hi_p, slot = head_rows(j)
                a.activation(act[lo_p:hi_p, slot, 0, :], psum[lo_p:hi_p, 6 + j % 2, 0:S], ACT.Copy)\
                    .then_inc(oh_ready, 1)

            def gate_out(j, second):
                n = gate_unit(j, second)
                ahead(n)
                product(n)
                m = n - U["gates"]
                a.activation(gates[:, m, :], gate_bank(n), ACT.Identity, bias=c1("b_gate", m))\
                    .then_inc(taken["a"], 1)
                if m % KD == KD - 1:
                    a.wait_ge(taken["a"], TAKEN["a"][n])
                    a.activation(gates[:, m - KD + 1:m + 1, :], gates[:, m - KD + 1:m + 1, :], ACT.Sigmoid)\
                        .then_inc(gates_done, 1)

            exps(0)
            for j in range(JOBS_MEM[-1] + 1):
                if j < JOBS_MEM[-1]:
                    exps(j + 1)
                if j in JOBS_DIL:
                    copy_pt(j)
                else:
                    gate_out(j, 0)
                    copy_pt(j)
                    gate_out(j, 1)
                out_hi(j)
            for m in range(12):
                ahead(U["branch"] + m)
                if m >= 8:
                    j = 2 * (m - 8)
                    a.wait_ge(merge_done, m - 7)
                    a.activation(act[:, 16 + j:18 + j, 0, :], merged[:, j:j + 2, :], ACT.Copy).then_inc(mh_done, 1)

            def k_major(name, count, norm):
                for m in range(count):
                    ahead(U[name] + m)
                product(U[name] + count - 1)
                for b in range(4):
                    a.activation(sq[:, 2 * b:2 * b + 2, :], bank(4 + b).rearrange("p (h t) -> p h t", h=2),
                                 ACT.Square).then_inc(sq_done, 1)
                norm_std(norm, KD, at=0)

            k_major("wo", 8, N_MIX)
            residual_square(N_FFN, 0)
            norm_std(N_FFN, KD)
            norm_hi(N_FFN, KD, 16, tn)

            def up_turn(i, turns, first, direct):
                loops = ((i, 4, turns),)
                for r in range(4):
                    n = U["up"] + 4 * first + r
                    ahead(n, loops)
                    product(n, loops)
                    if r == 0 and direct:
                        wait(z_free, i + 1)
                    elif r == 0:
                        wait(ah_done, i + first)
                    a.activation(z_up[:, r, :], half(n % 4, 0), ACT.Identity,
                                 bias=c1("conv_b", i * 4 + (4 * first + r)),
                                 scale=c1("conv_w", i * 4 + (4 * first + r + 2 * 2 * KF))).then_inc(z_init, 1)
                    if r % 2:
                        taken_at(a, n - 1, loops)
                        a.activation(z_up[:, r - 1, :], z_up[:, r - 1, :], ACT.Silu).then_inc(silu_done, 1)
                wait(prod_done, i + (first + 1))
                if direct:
                    a.activation(act[:, bass.ds(i * 2 + 2 * first, 2), 0, :], z_up[:, 1:4:2, :], ACT.Copy)\
                        .then_inc(ah_done, 1)
                else:
                    a.activation(late[:, bass.ds(i * 2 + (2 * first - 16), 2), :], z_up[:, 1:4:2, :], ACT.Copy)\
                        .then_inc(ah_done, 1)

            with a.Fori(0, 8) as i:
                up_turn(i, 8, 0, True)
            a.wait_ge(z_free, 9)
            with a.Fori(0, 3) as i:
                up_turn(i, 3, 8, False)
            a.wait_ge(unit_used, U["down"])
            a.wait_ge(ah_done, 11)
            for t in range(3):
                a.activation(act[:, 16 + 2 * t:18 + 2 * t, 0, :], late[:, 2 * t:2 * t + 2, :], ACT.Copy)\
                    .then_inc(ah_done, 1)
            k_major("down", KF, N_FFN_OUT)

            with a.Fori(0, LAYERS) as lay:
                L = (lay, PER_LAYER, LAYERS)
                for m in range(3):
                    hi(LAYER0 + m, (L,))
                residual_square(lay + N_LAYER, lay + 1)
                norm_std(N_LAYER, KD, lay)
                for j in range(KD):
                    wait(tn_done, lay * KD + (SPLIT_BEFORE[N_LAYER] + j + 1))
                    a.activation(act[:, 16 + j, 0, :], tn[:, j, :], ACT.Identity,
                                 bias=mod[:, bass.ds(lay * 24 + j, 1)]).then_inc(nh_done, 1)
                a.wait_ge(par2_in_s, lay * 16 + 16)
                a.wait_ge(sp_done, lay * 2 + 1)
                a.activation(t8[0], t8[0], ACT.Exp, scale=-1.0).then_inc(sp_exp, 1)
                with a.Fori(0, 2) as i:
                    loops = (L, (i, 4, 2))
                    for r in range(4):
                        n = U["conv"] + r
                        ahead(n, loops)
                        product(n, loops)
                        a.activation(u_rg[:, bass.ds(i * 4 + r, 1), :].rearrange("p a n -> p (a n)"),
                                     half(n % 4, 0), ACT.Identity,
                                     bias=par2[:, bass.ds(i * 4 + (C2["rg_b"][0] + r), 1)],
                                     scale=par2[:, bass.ds(i * 4 + (C2["rg_w"][0] + 3 * KD + r), 1)])\
                            .then_inc(z_init, 1)
                taken_at(a, U["conv"] + 7, (L,))
                for h in range(2):
                    a.activation(act[:, 8 + 4 * h:12 + 4 * h, 0, :], u_rg[:, 4 * h:4 * h + 4, :], ACT.Copy)\
                        .then_inc(xs_hi, 1)
                a.wait_ge(nl_done, lay * KD + SPLIT_BEFORE[N_LAYER + 1])
                with a.Fori(0, 2) as i:
                    loops = (L, (i, 4, 2))
                    for r in range(4):
                        n = U["conv"] + 8 + r
                        ahead(n, loops)
                        product(n, loops)
                        a.activation(xm[:, bass.ds(i * 4 + r, 1), :].rearrange("p a n -> p (a n)"),
                                     half(n % 4, 0), ACT.Copy)
                        a.activation(xc[:, bass.ds(i * 4 + r, 1), :].rearrange("p a n -> p (a n)"),
                                     half(n % 4, 0), ACT.Identity,
                                     bias=par2[:, bass.ds(i * 4 + (C2["ml_b"][0] + r), 1)],
                                     scale=par2[:, bass.ds(i * 4 + (C2["ml_w"][0] + 3 * KD + r), 1)])\
                            .then_inc(z_init, 1)
                ahead(U["rg"], (L,))
                ahead(U["rg"] + 1, (L,))
                product(U["rg"], (L,))
                for h in range(HR):
                    ins = a.activation(rg_i[h // 4][:, h % 4, :], half(h // 2, h % 2), ACT.Sigmoid, bias=c2("b_x", h))
                ins.then_inc(taken["a"], 1)
                product(U["rg"] + 1, (L,))
                for h in range(HR):
                    ins = a.activation(rg_r[:, h, :], half(4 + h // 2, h % 2), ACT.Sigmoid, bias=c2("b_a", h))
                ins.then_inc(taken["a"], 1)
                taken_at(a, U["conv"] + 15, (L,))
                def split_high(slot, src, h):
                    a.activation(act[:, slot + 4 * h:slot + 4 * h + 4, 0, :], src[:, 4 * h:4 * h + 4, :], ACT.Copy)\
                        .then_inc(xs_hi, 1)

                def z_tile(m):
                    n = U["z"] + m
                    product(n, (L,))
                    a.activation(zy[:, m, :], half(n % 4, 0), ACT.Silu).then_inc(taken["a"], 1)

                split_high(0, xm, 0)
                ahead(U["z"], (L,))
                split_high(0, xm, 1)
                a.activation(xc[:], xc[:], ACT.Silu).then_inc(xc_silu, 1)
                ahead(U["z"] + 1, (L,))
                z_tile(0)
                a.wait_ge(xc_silu, lay + 1)
                split_high(8, xc, 0)
                ahead(U["z"] + 2, (L,))
                z_tile(1)
                split_high(8, xc, 1)
                ahead(U["z"] + 3, (L,))
                z_tile(2)
                z_tile(3)
                for m in range(4, 8):
                    ahead(U["z"] + m, (L,))
                    z_tile(m)
                a.wait_ge(taken["a"], lay * LAYER_A + TAKEN["a"][U["rg"] + 1])
                a.wait_ge(sp_done, lay * 2 + 2)
                for h in range(HR):
                    ins = a.activation(rg_t[:, h, :], rg_r[:, h, :], ACT.Tanh, scale=soft[:, h:h + 1])
                ins.then_inc(rg_tanh, 1)
                a.wait_ge(rg_tanh, lay + 1)
                for q in range(2):
                    n = U["mlq"] + q
                    ahead(n, (L,))
                    product(n, (L,))
                    for b in range(2):
                        ins = a.activation(q_ml[:, 4 * q + 2 * b:4 * q + 2 * b + 2, :],
                                           bank(4 + 2 * q + b).rearrange("p (h t) -> p h t", h=2), ACT.Copy)
                    ins.then_inc(taken["a"], 1)
                for h in range(HR):
                    ins = a.activation(rg_r[:, h, :], rg_r[:, h, :], ACT.Exp, scale=nsoft[:, h:h + 1])
                ins.then_inc(rg_exp, 1)
                for q in range(2):
                    ahead(U["mlk"] + q, (L,))
                for q in range(2):
                    n = U["mlv"] + q
                    ahead(n, (L,))
                    product(n, (L,))
                    if q == 0:
                        a.wait_ge(rg_arg, lay * 2 + 1)
                    for b in range(2):
                        ins = a.activation(v_ml[:, 4 * q + 2 * b:4 * q + 2 * b + 2, :],
                                           bank(4 + 2 * q + b).rearrange("p (h t) -> p h t", h=2), ACT.Copy)
                    ins.then_inc(taken["a"], 1)

                def gate_tiles(*tiles):
                    for m in tiles:
                        n = U["late"] + m
                        ahead(n, (L,))
                        product(n, (L,))
                        if m < KD:
                            ins = a.activation(zy[:, KD + m, :], half(n % 4, 0), ACT.Silu)
                        else:
                            ins = a.activation(so[:, m - KD, :], half(n % 4, 0), ACT.Sigmoid)
                        ins.then_inc(taken["a"], 1)

                def v_tokens(*which):
                    for q in which:
                        a.wait_ge(vt_ready, lay * 4 + (q + 1))
                        a.activation(v_tok[:, q // 2, (q % 2) * 512:(q % 2 + 1) * 512], bank(4 + q % 2), ACT.Copy)\
                            .then_inc(vt_copied, 1)

                gate_tiles(0)
                a.wait_ge(rg_arg, lay * 2 + 2)
                a.activation(rg_t[:], rg_t[:], ACT.Sqrt).then_inc(rg_sqrt, 1)
                gate_tiles(1)
                v_tokens(0, 1)
                a.wait_ge(f_abs, lay + 1)
                a.activation(row[2], row[2], ACT.Exp, scale=-1.0).then_inc(f_exp, 1)
                gate_tiles(2)
                v_tokens(2, 3)
                gate_tiles(3, 4, 5, 6, 7)
                a.wait_ge(yr_done, lay * 5 + 1)
                for h in range(2):
                    a.activation(act[:, 8 + 4 * h:12 + 4 * h, 0, :], zy[:, 4 * h:4 * h + 4, :], ACT.Copy)\
                        .then_inc(yh_done, 1)
                for h in range(HL):
                    gate_tiles(8 + 2 * h)
                    a.wait_ge(wm_ready, lay * HL + (h + 1))
                    a.activation(w_ml[:, h % 2, 0:256], w_ml[:, h % 2, 0:256], ACT.Exp, bias=c_col[:, 0, h:h + 1])
                    a.activation(w_ml[:, h % 2, 256:384], w_ml[:, h % 2, 256:384], ACT.Exp,
                                 bias=c_col[:, 1, h:h + 1]).then_inc(we_ready, 1)
                    if h:
                        a.wait_ge(cell_done, lay * HL + h)
                    a.activation(floor_ml, half(5, 1), ACT.Exp).then_inc(floor_ready, 1)
                    gate_tiles(9 + 2 * h)
                for h in range(HL):
                    a.wait_ge(cell_done, lay * HL + (h + 1))
                    a.activation(sq_ml[:, 2 * h:2 * h + 2, :], so[:, 2 * h:2 * h + 2, :], ACT.Square)\
                        .then_inc(hsq_done, 1)
                for m in range(3):
                    ahead(U["out"] + m, (L,))
                for h in range(HL):
                    a.wait_ge(hss_done, lay * HL + (h + 1))
                    a.activation(sq_ml[:, 2 * h, :], half(4 + h, 0), ACT.Sqrt, bias=eps, scale=1.0 / 256)\
                        .then_inc(hstd_done, 1)
                for h in range(HL):
                    a.wait_ge(yr_done, lay * 5 + (h + 2))
                    a.activation(act[:, 2 * h:2 * h + 2, 0, :], zy[:, 8 + 2 * h:10 + 2 * h, :], ACT.Copy)\
                        .then_inc(yh_done, 1)
                    ahead(U["out"] + 3 + h, (L,))
                for m in range(7, 13):
                    ahead(U["out"] + m, (L,))
            residual_square(N_FINAL, LAYERS + 1)
            norm_std(N_FINAL, KD)

        @block.vector
        def _(v):
            step = Step(v, dve_step)
            link = step.link

            def lo(n, loops=()):
                v.wait_ge(hi_done, unit_of(n + 1, loops))
                r = n % SLOTS
                v.tensor_tensor(w_lo[:, r, :], raw[:, r, :], w_hi[:, r, :].bitcast(F32), ALU.subtract)\
                    .then_inc(lo_done, 1)

            def ahead(n, loops=()):
                if n + 3 not in FIRST_UNITS:
                    lo(n + 3, loops)

            def act_lo(slot, src, count=1):
                return v.tensor_tensor(act[:, slot:slot + count, 1, :], src,
                                       act[:, slot:slot + count, 0, :].bitcast(F32), ALU.subtract)

            def norm_rstd(n):
                v.wait_ge(std_done, n + 1)
                ins = v.reciprocal(rstd[:], std[:])
                ins.then_inc(rstd_done, 1)
                v.wait_ge(rstd_done, n + 1)

            def norm_split(n, k, src, gain, dst, slot):
                norm_rstd(n)
                for j in range(k + 1):
                    if j < k:
                        v.scalar_tensor_tensor(out=dst[:, j, :], in0=src[:, j, :], scalar=gain(j), in1=rstd[:],
                                               op0=ALU.mult, op1=ALU.mult).then_inc(tn_done, 1)
                    if j:
                        v.wait_ge(nh_done, SPLIT_BEFORE[n] + j)
                        act_lo(slot + j - 1, dst[:, j - 1:j, :]).then_inc(nl_done, 1)

            def norm_add(n, gain):
                norm_rstd(n)
                for c in range(PAIRS + 1):
                    if c < PAIRS:
                        for j in (2 * c, 2 * c + 1):
                            ins = v.scalar_tensor_tensor(out=tn[:, j, :], in0=half(4 + c, j % 2), scalar=gain(j),
                                                         in1=rstd[:], op0=ALU.mult, op1=ALU.mult)
                        ins.then_inc(dve_step, 1)
                        step.n += 1
                    if c:
                        v.wait_ge(dve_step, step.n - (c < PAIRS))
                        v.tensor_tensor(x[:, 2 * c - 2:2 * c, :], x[:, 2 * c - 2:2 * c, :], tn[:, 2 * c - 2:2 * c, :],
                                        ALU.add).then_inc(res_done, 1)

            link(v.memset(tiny[:], 0.0))
            v.memset(eps, EPS).then_inc(tables_done, 1)
            for n in range(3):
                lo(n)
            v.wait_ge(par_in, 16)
            norm_split(N_MEM, KD, memx, lambda j: c1("g_mem", j), tn, 0)
            ahead(U["memk"])
            norm_split(N_X, KD, x, lambda j: c1("g_pre_mix", j), ar_g[:, 8:16, :], 16)
            ahead(U["memk"] + 1)
            ahead(U["memk"] + 2)

            two_pi = 2 * np.pi
            part1 = 6.28125
            part2 = float(np.float32(round((two_pi - part1) * 2 ** 22) / 2 ** 22))
            part3 = two_pi - part1 - part2
            magic = 1.5 * 2 ** 23
            ang, turn = rope_tmp[:, 0, :], rope_tmp[:, 1, :]
            v.wait_ge(pos_in_s, 16)
            link(v.tensor_scalar(ang, ar_g[:, 20, :].bitcast(I32), c1("freq"), None, ALU.mult))
            link(v.tensor_scalar(turn, ang, 1.0 / two_pi, magic, ALU.mult, ALU.add))
            link(v.tensor_scalar(turn, turn, magic, None, ALU.subtract))
            for part in (part1, part2, part3):
                link(v.scalar_tensor_tensor(out=ang, in0=turn, scalar=-part, in1=ang, op0=ALU.mult, op1=ALU.add))
            v.tensor_scalar(ang, ang, 3.1415925, -3.1415925, ALU.min, ALU.max).then_inc(angle_done, 1)

            ahead(U["memk"] + 3)
            ahead(U["memv"])
            v.wait_ge(masks_done, 1)
            di = dist[:, 0, :].bitcast(I32)
            tmp = flat(ar_d[:, 32:34, :])[:, 0:384]
            for g in (1, 2):
                dg = dist[:, g, :]
                link(v.tensor_scalar(dg.bitcast(I32), di, DILATION[g] - 1, None, ALU.bitwise_and))
                link(v.tensor_scalar(dg, dg.bitcast(I32), 0.0, 1.0, ALU.is_equal, ALU.subtract))
                link(v.scalar_tensor_tensor(out=dg, in0=dg, scalar=-300 * NEG, in1=di, op0=ALU.mult,
                                            op1=ALU.subtract))
                link(v.tensor_tensor(dg, dg, causal[:], ALU.add))
                ahead(U["memv"] + g)
            link(v.tensor_scalar(tmp, di, float(SPAN), 300 * NEG, ALU.is_gt, ALU.mult))
            link(v.scalar_tensor_tensor(out=tmp, in0=di, scalar=-1.0, in1=tmp, op0=ALU.mult, op1=ALU.add))
            link(v.tensor_tensor(dist[:, 0, :], tmp, causal[:], ALU.add))
            v.wait_ge(sine_done, 2)
            link(v.tensor_tensor(cos_t[64:96, :], cos_t[64:96, :], cos_t[64:96, :], ALU.mult))
            link(v.tensor_scalar(cos_t[64:96, :], cos_t[64:96, :], -2.0, 1.0, ALU.mult, ALU.add))
            link(v.tensor_scalar(sin_t[96:128, :], sin_t[96:128, :], par1[96:128, C1["sign"][0]:C1["sign"][0] + 1],
                                 None, ALU.mult))

            def modulation(k, slot, value):
                v.wait_ge(ada_in[slot], value)
                v.scalar_tensor_tensor(out=ada[:, slot, :], in0=ada[:, slot, :], scalar=1.0, in1=cact,
                                       op0=ALU.mult, op1=ALU.mult,
                                       accum_out=mod[:, k:k + 1] if isinstance(k, int) else mod[:, bass.ds(k, 1)])\
                    .then_inc(ada_used, 1)

            ahead(U["memv"] + 3)
            v.wait_ge(cact_done, 1)
            for n in range(U["latent"], U["latent"] + 6):
                ahead(n)
                if n - U["latent"] in range(3):
                    modulation(n - U["latent"], n - U["latent"], 16)

            def rotate(dst, src_bank, m):
                link(v.tensor_tensor(rope_tmp[64:96, m, :], psum[96:128, src_bank, m * S:(m + 1) * S],
                                     sin_t[96:128, :], ALU.mult))
                ins = v.tensor_tensor(dst, psum[64:96, src_bank, m * S:(m + 1) * S], cos_t[64:96, :], ALU.mult)
                return ins

            n = U["latent"] + 5
            v.wait_ge(unit_used, n + 1)
            k_rot = ar_g[64:96, 16, :]
            rotate(k_rot, n % 4, 0).then_inc(taken["v"], 1)
            v.wait_ge(taken["v"], TAKEN["v"][n])
            link(v.tensor_tensor(k_rot, k_rot, rope_tmp[64:96, 0, :], ALU.add))
            norm_split(N_CQ, KQ, latent[:, 0:KQ, :], lambda j: c1("q_norm", j), ar_g[:, 10:13, :], 8)
            norm_split(N_CKV, KKV, latent[:, KQ:5, :], lambda j: c1("kv_norm", j), ar_g[:, 13:15, :], 11)

            with v.Fori(0, 6) as i:
                for r in range(4):
                    ahead(U["qk"] + r, ((i, 4, 6),))
                    for s in ADA_BETWEEN[r]:
                        modulation(i * 6 + (3 + s), s % 3, i * 32 + 16 * (s // 3 + 2))
            with v.Fori(0, 3) as i:
                for r in range(4):
                    ahead(U["v"] + r, ((i, 4, 3),))
                    if r < 3:
                        modulation(i * 3 + (39 + r), r, i * 16 + (13 * 16 + 16))
            v.wait_ge(ada_used, 24 * LAYERS)
            v.tensor_tensor(mod[:], mod[:], c1("b_ada", 0, 24 * LAYERS), ALU.add).then_inc(mod_done, 1)
            v.tensor_copy(k_mla[64:96, :, :], k_rot.unsqueeze(1).to_broadcast([32, 8, S])).then_inc(k_pe_done, 1)
            for m in range(4):
                n = U["uq"] + m
                ahead(n)
                v.wait_ge(q_nope, m + 1)
                for h in range(2):
                    dst = q_mla[64:96, 2 * m + h, :]
                    ins = rotate(dst, n % 4, h)
                    if h:
                        ins.then_inc(taken["v"], 1)
                        v.wait_ge(taken["v"], TAKEN["v"][n])
                    else:
                        link(ins)
                    ins = v.tensor_tensor(dst, dst, rope_tmp[64:96, h, :], ALU.add)
                ins.then_inc(rope_done, 1)
            for n in range(U["ukvk"], U["memq"] + 4):
                ahead(n)

            def maxima(j):
                v.wait_ge(s_ready, j + 1)
                s = s_sb[:, j % 2, :]
                scale = (NOPE + ROPE) ** -0.5 if j in JOBS_MLA else DH ** -0.5
                if j in JOBS_MLA:
                    link(v.tensor_tensor(s[:, 0:384], psum[:, j % 2, 0:384], causal[:], ALU.add))
                elif j in JOBS_DIL:
                    for g in range(GROUPS):
                        slope = 2.0 ** (-8.0 * (j * GROUPS + g + 1) / (GROUPS * HD))
                        ins = v.scalar_tensor_tensor(out=s[:, 384 * g:384 * g + 384], in0=dist[:, g, :],
                                                     scalar=slope / scale, in1=psum[:, g, 0:384], op0=ALU.mult,
                                                     op1=ALU.add)
                    link(ins)
                for q, (src, _) in enumerate(score_views(j)):
                    ins = v.tensor_reduce(stat(j, q, 0), src, AX.XY if j in JOBS_DIL else AX.X, ALU.max,
                                          negate=True)
                link(ins)
                v.tensor_scalar(stat(j, None, 2), stat(j, None, 0), scale, None, ALU.mult).then_inc(m_ready, 1)

            def normalise(j):
                v.wait_ge(e_ready, j + 1)
                link(v.reciprocal(stat(j, None, 1), stat(j, None, 3)))
                for q, (_, p) in enumerate(score_views(j)):
                    ins = v.tensor_scalar(p, p, stat(j, q, 1), None, ALU.mult)
                ins.then_inc(p_ready, 1)

            def out_lo(j):
                v.wait_ge(oh_ready, j + 1)
                lo_p, hi_p, slot = head_rows(j)
                v.tensor_tensor(act[lo_p:hi_p, slot, 1, :], psum[lo_p:hi_p, 6 + j % 2, 0:S],
                                act[lo_p:hi_p, slot, 0, :].bitcast(F32), ALU.subtract).then_inc(ol_ready, 1)

            maxima(0)
            for j in range(JOBS_MEM[-1] + 1):
                if j < JOBS_MEM[-1]:
                    maxima(j + 1)
                normalise(j)
                if j not in JOBS_DIL:
                    ahead(gate_unit(j, 0))
                    ahead(gate_unit(j, 1))
                out_lo(j)

            for b in range(3):
                for q in range(4):
                    n = U["branch"] + 4 * b + q
                    ahead(n)
                    v.wait_ge(unit_used, n + 1)
                    y = bank(n % 4).rearrange("p (h t) -> p h t", h=2)
                    g = gates[:, 8 * b + 2 * q:8 * b + 2 * q + 2, :]
                    m = merged[:, 2 * q:2 * q + 2, :]
                    dst = m if b == 0 else branch_y[:, 2 * (q % 2):2 * (q % 2) + 2, :]
                    if q == 0:
                        v.wait_ge(gates_done, b + 1)
                    v.tensor_tensor(dst, y, g, ALU.mult).then_inc(taken["v"], 1)
                    if b:
                        v.wait_ge(taken["v"], TAKEN["v"][n])
                        ins = v.tensor_tensor(m, m, dst, ALU.add)
                        if b == 1:
                            ins.then_inc(dve_step, 1)
                            step.n += 1
                        else:
                            ins.then_inc(merge_done, 1)
                            v.wait_ge(mh_done, q + 1)
                            act_lo(16 + 2 * q, m, 2).then_inc(merged_lo, 1)
                if b == 1:
                    v.wait_ge(dve_step, step.n)
            for m in range(8):
                ahead(U["wo"] + m)
            norm_add(N_MIX, lambda j: c1("g_post_mix", j))
            v.wait_ge(res_done, PAIRS)
            norm_split(N_FFN, KD, x, lambda j: c1("g_pre_ffn", j), tn, 16)

            def up_turn(i, turns, first, direct):
                loops = ((i, 4, turns),)
                with step.turns(i, turns, 4):
                    for r in range(4):
                        n = U["up"] + 4 * first + r
                        ahead(n, loops)
                        v.wait_ge(z_init, i * 4 + (4 * first + r + 1))
                        for tap, shift in ((1, 1), (0, 2)):
                            ins = v.scalar_tensor_tensor(
                                out=z_up[:, r, shift:S], in0=psum[:, n % 4, 0:S - shift],
                                scalar=c1("conv_w", i * 4 + (4 * first + r + tap * 2 * KF)),
                                in1=z_up[:, r, shift:S], op0=ALU.mult, op1=ALU.add)
                            if tap:
                                link(ins)
                            else:
                                ins.then_inc(taken["v"], 1)
                v.wait_ge(silu_done, i * 2 + (2 * first + 2))
                taken_at(v, U["up"] + 4 * first + 3, loops)
                ins = v.tensor_tensor(z_up[:, 1:4:2, :], z_up[:, 0:4:2, :], z_up[:, 1:4:2, :], ALU.mult)
                ins.then_inc(prod_done, 1)
                v.wait_ge(ah_done, i + (first + 1))
                if direct:
                    slot = i * 2 + 2 * first
                    v.tensor_tensor(act[:, bass.ds(slot, 2), 1, :], z_up[:, 1:4:2, :],
                                    act[:, bass.ds(slot, 2), 0, :].bitcast(F32), ALU.subtract)\
                        .then_inc(z_free, 1)

            v.memset(tiny[:, 5:6], 0.0).then_inc(z_free, 1)
            with v.Fori(0, 8) as i:
                up_turn(i, 8, 0, True)
            with v.Fori(0, 3) as i:
                up_turn(i, 3, 8, False)
            for t in range(3):
                v.wait_ge(ah_done, 11 + t + 1)
                act_lo(16 + 2 * t, late[:, 2 * t:2 * t + 2, :], 2).then_inc(al_done, 1)
            for m in range(KF):
                ahead(U["down"] + m)
            norm_add(N_FFN_OUT, lambda j: c1("g_post_ffn", j))

            def log1p(dst, e, t, q, poly):
                link(v.tensor_scalar(t, e, 2.0, None, ALU.add))
                link(v.reciprocal(t, t))
                link(v.tensor_tensor(e, e, t, ALU.mult))
                link(v.tensor_tensor(q, e, e, ALU.mult))
                link(v.tensor_scalar(poly, q, 1.0 / 17, None, ALU.mult))
                for d in (15, 13, 11, 9, 7, 5, 3):
                    link(v.scalar_tensor_tensor(out=poly, in0=poly, scalar=1.0 / d, in1=q, op0=ALU.add,
                                                op1=ALU.mult))
                link(v.tensor_scalar(poly, poly, 1.0, 2.0, ALU.add, ALU.mult))
                link(v.tensor_tensor(dst, poly, e, ALU.mult))

            LINKS = 97
            with v.Fori(0, LAYERS) as lay, step.turns(lay, LAYERS, LINKS):
                L = (lay, PER_LAYER, LAYERS)
                for m in range(3):
                    lo(LAYER0 + m, (L,))
                v.wait_ge(par2_in_s, lay * 16 + 16)
                v.scalar_tensor_tensor(out=t8[0], in0=c2("lam", 0, KD), scalar=-1.0, in1=c2("lam", 0, KD),
                                       op0=ALU.mult, op1=ALU.max).then_inc(sp_done, 1)
                at = lay * 24 + KD
                v.wait_ge(res_done, lay * PAIRS + 2 * PAIRS)
                v.scalar_tensor_tensor(out=gain2, in0=mod[:, bass.ds(at, KD)], scalar=1.0,
                                       in1=c2("norm_g", 0, KD), op0=ALU.add, op1=ALU.mult).then_inc(dve_step, 1)
                step.n += 1
                v.wait_ge(std_done, lay + (N_LAYER + 1))
                v.reciprocal(rstd[:], std[:]).then_inc(rstd_done, 1)
                v.wait_ge(rstd_done, lay + (N_LAYER + 1))
                for j in range(KD + 1):
                    if j < KD:
                        v.scalar_tensor_tensor(out=tn[:, j, :], in0=x[:, j, :], scalar=gain2[:, j:j + 1],
                                               in1=rstd[:], op0=ALU.mult, op1=ALU.mult).then_inc(tn_done, 1)
                    if j:
                        v.wait_ge(nh_done, lay * KD + (SPLIT_BEFORE[N_LAYER] + j))
                        v.scalar_tensor_tensor(out=act[:, 16 + j - 1, 1, :], in0=tn[:, j - 1, :],
                                               scalar=mod[:, bass.ds(lay * 24 + (j - 1), 1)],
                                               in1=act[:, 16 + j - 1, 0, :].bitcast(F32), op0=ALU.add,
                                               op1=ALU.subtract).then_inc(nl_done, 1)
                def split(which, slot, src, halves=(0, 1)):
                    for h in halves:
                        v.wait_ge(xs_hi, lay * 6 + (2 * which + h + 1))
                        act_lo(slot + 4 * h, src[:, 4 * h:4 * h + 4, :], 4).then_inc(xs_lo, 1)

                for part, (dst, w) in enumerate(((u_rg, "rg_w"), (xc, "ml_w"))):
                    if part:
                        split(0, 8, u_rg)
                    with v.Fori(0, 2) as i, step.turns(i, 2, 8):
                        loops = (L, (i, 4, 2))
                        for r in range(4):
                            n = U["conv"] + 8 * part + r
                            ahead(n, loops)
                            v.wait_ge(z_init, lay * 16 + (i * 4 + (2 * KF + 8 * part + r + 1)))
                            for shift in (1, 2, 3):
                                at = i * 4 + (C2[w][0] + (3 - shift) * KD + r)
                                tile = dst[:, bass.ds(i * 4 + r, 1), shift:S].rearrange("p a n -> p (a n)")
                                ins = v.scalar_tensor_tensor(out=tile, in0=psum[:, n % 4, 0:S - shift],
                                                             scalar=par2[:, bass.ds(at, 1)], in1=tile,
                                                             op0=ALU.mult, op1=ALU.add)
                                if shift < 3:
                                    link(ins)
                                else:
                                    ins.then_inc(taken["v"], 1)

                ahead(U["rg"], (L,))
                ahead(U["rg"] + 1, (L,))
                split(1, 0, xm, (0,))
                ahead(U["z"], (L,))
                split(1, 0, xm, (1,))
                ahead(U["z"] + 1, (L,))
                split(2, 8, xc, (0,))
                ahead(U["z"] + 2, (L,))
                split(2, 8, xc, (1,))
                ahead(U["z"] + 3, (L,))
                v.wait_ge(taken["a"], lay * LAYER_A + TAKEN["a"][U["rg"]])
                for h in range(2):
                    ins = v.tensor_tensor(rg_i[h], rg_i[h], u_rg[:, 4 * h:4 * h + 4, :], ALU.mult)
                ins.then_inc(rg_arg, 1)
                for m in (4, 5):
                    ahead(U["z"] + m, (L,))
                v.wait_ge(sp_exp, lay + 1)
                log1p(t8[1], t8[0], t8[2], t8[3], t8[1])
                link(v.tensor_scalar(t8[2], c2("lam", 0, KD), -1.0, 0.0, ALU.mult, ALU.max))
                link(v.tensor_tensor(t8[1], t8[1], t8[2], ALU.add))
                link(v.tensor_scalar(soft, t8[1], RG_C, None, ALU.mult))
                v.tensor_scalar(nsoft, t8[1], -RG_C, None, ALU.mult).then_inc(sp_done, 1)
                for m in (6, 7):
                    ahead(U["z"] + m, (L,))
                for q in range(2):
                    ahead(U["mlq"] + q, (L,))
                for q in range(2):
                    n = U["mlk"] + q
                    ahead(n, (L,))
                    v.wait_ge(unit_used, unit_of(n + 1, (L,)))
                    for b in range(2):
                        ins = v.tensor_copy(k_ml[:, 4 * q + 2 * b:4 * q + 2 * b + 2, :],
                                            bank(2 * q + b).rearrange("p (h t) -> p h t", h=2))
                    ins.then_inc(taken["v"], 1)
                for q in range(2):
                    ahead(U["mlv"] + q, (L,))
                v.wait_ge(rg_exp, lay + 1)
                link(v.tensor_tensor(rg_sq[:], rg_r[:], rg_r[:], ALU.mult))
                v.scalar_tensor_tensor(out=flat(rg_t), in0=flat(rg_sq), scalar=1.0, in1=flat(rg_t), op0=ALU.add,
                                       op1=ALU.mult).then_inc(rg_arg, 1)
                ahead(U["late"], (L,))
                v.wait_ge(gt_ready, lay + 1)
                for blk in range(2):
                    ins = v.tensor_tensor(gate_tok[:, blk, :], psum[:, 7, 8 * blk:8 * blk + 8], c2("b_if", 0, 8),
                                          ALU.add)
                ins.then_inc(gt_done, 1)
                ahead(U["late"] + 1, (L,))
                v.wait_ge(gr_ready, lay + 1)
                li, f, e, t, q = row
                v.tensor_copy(li, psum[0:HL, 6, 0:S])
                link(v.tensor_copy(f, psum[0:HL, 6, S:2 * S]))
                v.scalar_tensor_tensor(out=e, in0=f, scalar=-1.0, in1=f, op0=ALU.mult, op1=ALU.max)\
                    .then_inc(f_abs, 1)
                ahead(U["late"] + 2, (L,))
                v.wait_ge(rg_sqrt, lay + 1)
                for h in range(2):
                    ins = v.tensor_tensor(rg_i[h], rg_i[h], rg_t[:, 4 * h:4 * h + 4, :], ALU.mult)
                link(ins)
                ahead(U["late"] + 3, (L,))
                for h in range(HR):
                    ins = v.tensor_tensor_scan(rg_t[:, h, :], rg_r[:, h, :], rg_i[h // 4][:, h % 4, :], 0.0,
                                               ALU.mult, ALU.add)
                link(ins)
                v.tensor_tensor(zy[:, 0:8, :], zy[:, 0:8, :], rg_t[:], ALU.mult).then_inc(yr_done, 1)
                for m in (4, 5):
                    ahead(U["late"] + m, (L,))
                v.wait_ge(f_exp, lay + 1)
                poly = neg_row[:, 0:S]
                log1p(e, e, t, q, poly)
                link(v.scalar_tensor_tensor(out=f, in0=f, scalar=0.0, in1=e, op0=ALU.min, op1=ALU.subtract))
                link(v.memset(t, 1.0))
                link(v.tensor_tensor_scan(q, t, f, 0.0, ALU.mult, ALU.add))
                link(v.tensor_tensor(li, li, q, ALU.subtract))
                link(v.tensor_tensor_scan(f, t, li, 0.0, ALU.mult, ALU.max))
                v.tensor_scalar(neg_row[:, 0:S], f, -1.0, None, ALU.mult)
                v.scalar_tensor_tensor(out=neg_row[:, S:2 * S], in0=f, scalar=-1.0, in1=q, op0=ALU.mult,
                                       op1=ALU.subtract).then_inc(rows_done, 1)
                for m in (6, 7):
                    ahead(U["late"] + m, (L,))
                v.wait_ge(cc_ready, lay + 1)
                v.tensor_copy(small[:, 16:24], psum[:, 7, 0:8]).then_inc(cc_done, 1)

                def decay(h):
                    v.wait_ge(mb_ready, lay * HL + (h + 1))
                    v.tensor_tensor(w_ml[:, h % 2, 0:256], half(5, 0), causal_t[:, 0:256], ALU.add)
                    v.tensor_tensor(w_ml[:, h % 2, 256:384], psum[:, 5, 128:256], causal_t[:, 256:384],
                                    ALU.add).then_inc(wm_ready, 1)

                decay(0)
                for h in range(2):
                    v.wait_ge(yh_done, lay * 6 + (h + 1))
                    act_lo(8 + 4 * h, zy[:, 4 * h:4 * h + 4, :], 4).then_inc(yl_done, 1)
                for h in range(HL):
                    ahead(U["late"] + 8 + 2 * h, (L,))
                    ahead(U["late"] + 9 + 2 * h, (L,))
                    v.wait_ge(st_ready, lay * HL + (h + 1))
                    v.wait_ge(we_ready, lay * HL + (h + 1))
                    v.scalar_tensor_tensor(out=sw_ml[:, h % 2, :], in0=psum[:, 4, 0:384], scalar=256 ** -0.5,
                                           in1=w_ml[:, h % 2, :], op0=ALU.mult, op1=ALU.mult)\
                        .then_inc(sw_ready, 1)
                    if h + 1 < HL:
                        decay(h + 1)
                    v.wait_ge(num_ready, lay * HL + (h + 1))
                    v.wait_ge(floor_ready, lay * HL + (h + 1))
                    link(v.tensor_tensor(den_ml, half(7, 0), floor_ml, ALU.max))
                    link(v.scalar_tensor_tensor(out=den_ml, in0=half(7, 0), scalar=-1.0,
                                                in1=den_ml, op0=ALU.mult, op1=ALU.max))
                    link(v.reciprocal(den_ml, den_ml))
                    for dv in range(2):
                        ins = v.tensor_tensor(ar_m[:, 10 + dv, :], half(6, dv), den_ml, ALU.mult)
                    link(ins)
                    taken_at(v, U["late"] + 9 + 2 * h, (L,))
                    v.tensor_tensor(so[:, 2 * h:2 * h + 2, :], so[:, 2 * h:2 * h + 2, :], ar_m[:, 10:12, :],
                                    ALU.mult).then_inc(cell_done, 1)
                for m in range(3):
                    ahead(U["out"] + m, (L,))
                v.wait_ge(cell_done, lay * HL + HL)
                for h in range(HL + 1):
                    if h < HL:
                        v.wait_ge(hstd_done, lay * HL + (h + 1))
                        link(v.reciprocal(den_ml, sq_ml[:, 2 * h, :]))
                        for dv in range(2):
                            m = 2 * h + dv
                            ins = v.scalar_tensor_tensor(out=so[:, m, :], in0=so[:, m, :], scalar=c2("head_g", m),
                                                         in1=den_ml, op0=ALU.mult, op1=ALU.mult)
                        link(ins)
                        zh = zy[:, 8 + 2 * h:10 + 2 * h, :]
                        v.tensor_tensor(zh, zh, so[:, 2 * h:2 * h + 2, :], ALU.mult).then_inc(yr_done, 1)
                    if h:
                        v.wait_ge(yh_done, lay * 6 + (h + 2))
                        act_lo(2 * h - 2, zy[:, 6 + 2 * h:8 + 2 * h, :], 2).then_inc(yl_done, 1)
                        ahead(U["out"] + 2 + h, (L,))
                for m in range(7, 13):
                    ahead(U["out"] + m, (L,))
                v.wait_ge(unit_used, unit_of(U["out"] + 16, (L,)))
                for m in range(KD):
                    ins = v.scalar_tensor_tensor(out=x[:, m, :], in0=half(m // 2, m % 2),
                                                 scalar=mod[:, bass.ds(lay * 24 + (16 + m), 1)], in1=x[:, m, :],
                                                 op0=ALU.mult, op1=ALU.add)
                    if m % 2:
                        ins.then_inc(res_done, 1)
            v.wait_ge(std_done, N_FINAL + 1)
            v.reciprocal(rstd[:], std[:]).then_inc(rstd_done, 1)
            v.wait_ge(rstd_done, N_FINAL + 1)
            for j in range(KD):
                v.scalar_tensor_tensor(out=tn[:, j, :], in0=x[:, j, :], scalar=c1("final_g", j), in1=rstd[:],
                                       op0=ALU.mult, op1=ALU.mult).then_inc(tn_done, 1)

        @block.tensor
        def _(t):
            def mm3(out_ap, wh, wl, rh, rl, start, stop):
                t.matmul(out_ap, wh, rh, start=start, stop=False, skip_group_check=True)
                t.matmul(out_ap, wh, rl, start=False, stop=False, skip_group_check=True)
                return t.matmul(out_ap, wl, rh, start=False, stop=stop, skip_group_check=True)

            def unit(n, loops=(), limit=True):
                t.wait_ge(lo_done, unit_of(n + 1, loops))

            def wide(n, loops=()):
                r = n % SLOTS
                return (w_hi[:, r, :].rearrange("p (k m) -> p k m", k=8),
                        w_lo[:, r, :].rearrange("p (k m) -> p k m", k=8))

            def tile_product(n, slot, loops=(), ready=None, out_ap=None):
                unit(n, loops)
                wh, wl = wide(n)
                for k in range(KD):
                    if ready:
                        ready(k)
                    ins = mm3(out_ap or half(n % 4, 0), wh[:, k, :], wl[:, k, :], act[:, slot + k, 0, :],
                              act[:, slot + k, 1, :], k == 0, k == KD - 1)
                ins.then_inc(unit_used, 1)

            def value_pair(n, slot, loops=()):
                for u in range(2):
                    unit(n + u, loops)
                    r = (n + u) % SLOTS
                    wh = w_hi[:, r, :].rearrange("p (k m) -> p k m", k=4)
                    wl = w_lo[:, r, :].rearrange("p (k m) -> p k m", k=4)
                    for k in range(4):
                        for blk in range(2):
                            cut = slice(blk * P, blk * P + P)
                            ins = mm3(half(n % 4, blk), act[:, slot + 4 * u + k, 0, cut],
                                      act[:, slot + 4 * u + k, 1, cut], wh[:, k, :], wl[:, k, :],
                                      u == 0 and k == 0 and blk == 0, u == 1 and k == 3)
                    ins.then_inc(unit_used, 1)

            def k_product(name, first, count, slot, done, per, loops=(), total=None):
                for k in range(first, first + count):
                    n = U[name] + k
                    unit(n, loops)
                    done(k)
                    wh, wl = wide(n)
                    for m in range(KD):
                        ins = mm3(half(4 + m // 2, m % 2), wh[:, m, :], wl[:, m, :], act[:, slot(k), 0, :],
                                  act[:, slot(k), 1, :], k == 0 and m % 2 == 0, k == total - 1)
                    ins.then_inc(unit_used, 1)

            def norm_sum(n, tiles, k, lay=0, at=4):
                if n:
                    t.wait_ge(std_done, lay + n)
                for j in range(k):
                    if j % 2 == 0:
                        t.wait_ge(sq_done, lay * PAIRS + (SQUARES_BEFORE[n] + j // 2 + 1))
                    ins = t.matmul(half(at, 0), ones[:], tiles[:, j, :], start=j == 0, stop=j == k - 1)
                ins.then_inc(ss_done, 1)

            def split_tile(n, lay=0):
                return lambda k: t.wait_ge(nl_done, lay * KD + (SPLIT_BEFORE[n] + k + 1))

            t.wait_ge(masks_done, 1)
            norm_sum(N_MEM, sq, KD)
            norm_sum(N_X, ar_g[:, 0:8, :], KD)
            for m in range(4):
                tile_product(U["memk"] + m, 0, ready=split_tile(N_MEM) if m == 0 else None)
            for m in range(2):
                taken_at(t, U["memv"] + 2 * m - 4 + 1)
                value_pair(U["memv"] + 2 * m, 0)
            t.wait_ge(nl_done, 2 * KD)
            for m in range(6):
                taken_at(t, U["latent"] + m - 3)
                tile_product(U["latent"] + m, 16)
            norm_sum(N_CQ, ar_g[:, 5:8, :], KQ)
            norm_sum(N_CKV, ar_g[:, 8:10, :], KKV)

            taken_at(t, U["qk"] - 1)
            with t.Fori(0, 6) as i:
                loops = ((i, 4, 6),)
                for r in range(4):
                    n = U["qk"] + r
                    ring_free(t, n, loops, U["qk"])
                    tile_product(n, 16, loops)
            taken_at(t, U["v"] - 1)
            with t.Fori(0, 3) as i:
                loops = ((i, 4, 3),)
                for r in range(0, 4, 2):
                    n = U["v"] + r
                    ring_free(t, n, loops, U["v"])
                    value_pair(n, 16, loops)
            t.wait_ge(nl_done, SPLIT_BEFORE[N_CKV + 1])
            for q in range(4):
                n = U["uq"] + q
                taken_at(t, n - 3)
                unit(n)
                wh, wl = (w[:, n % SLOTS, 0:768].rearrange("p (k h m) -> p k h m", k=KQ, h=2) for w in (w_hi, w_lo))
                for h in range(2):
                    for k in range(KQ):
                        ins = mm3(half(n % 4, h), wh[:, k, h, :], wl[:, k, h, :], act[:, 8 + k, 0, :],
                                  act[:, 8 + k, 1, :], k == 0, k == KQ - 1)
                ins.then_inc(unit_used, 1)
            n = U["ukvk"]
            unit(n)
            wh, wl = (w[:, n % SLOTS, :].rearrange("p (k h m) -> p k h m", k=KKV, h=4) for w in (w_hi, w_lo))
            for m in range(4):
                for k in range(KKV):
                    ins = mm3(half(4 + m // 2, m % 2), wh[:, k, m, :], wl[:, k, m, :], act[:, 11 + k, 0, :],
                              act[:, 11 + k, 1, :], k == 0, k == KKV - 1)
            ins.then_inc(unit_used, 1)
            n = U["ukvv"]
            unit(n)
            wh, wl = (w[:, n % SLOTS, :].rearrange("p (k m) -> p k m", k=KKV) for w in (w_hi, w_lo))
            for blk in range(2):
                cut = slice(blk * P, blk * P + P)
                for k in range(KKV):
                    ins = mm3(bank(6 + blk), act[:, 11 + k, 0, cut], act[:, 11 + k, 1, cut], wh[:, k, :],
                              wl[:, k, :], k == 0, k == KKV - 1)
            ins.then_inc(unit_used, 1)
            for m in range(4):
                n = U["memq"] + m
                taken_at(t, n - 3)
                tile_product(n, 16)

            def scores(j):
                if j in JOBS_MEM[2:]:
                    t.wait_ge(e_ready, j - 1)
                elif 0 < j <= JOBS_MLA[0]:
                    t.wait_ge(m_ready, j)
                elif j:
                    t.wait_ge(m_ready, j - 1)
                if j in JOBS_MLA:
                    h = j - JOBS_MLA[0]
                    q, k, b = q_mla[0:96, h, :], k_mla[0:96, h, :], j % 2
                    t.matmul(psum[:, b, 0:128], q[:, 0:128], k[:, 0:128], start=True, stop=True)
                    ins = t.matmul(psum[:, b, 128:384], q[:, 128:256], k, start=True, stop=True)
                elif j in JOBS_DIL:
                    for g in range(GROUPS):
                        h = g * HD + j
                        q, k = qk_d[:, h, :], qk_d[:, 12 + h, :]
                        t.matmul(psum[:, g, 0:128], q[:, 0:128], k[:, 0:128], start=True, stop=True)
                        ins = t.matmul(psum[:, g, 128:384], q[:, 128:256], k, start=True, stop=True)
                else:
                    h = j - JOBS_MEM[0]
                    for blk in range(2):
                        ins = t.matmul(half(j % 2, blk), q_mem[:, h, blk * P:blk * P + P], k_mem[:, h, :],
                                       start=True, stop=True)
                ins.then_inc(s_ready, 1)

            def transposes(j):
                t.wait_ge(p_ready, j + 1)
                if 0 < j <= JOBS_MLA[0]:
                    t.wait_ge(pt_copied, j)
                elif j:
                    t.wait_ge(pt_copied, j - 1)
                s = s_sb[:, j % 2, :]
                if j in JOBS_MEM:
                    for q in range(2):
                        for k in range(2):
                            ins = t.transpose(psum[:, 3 + j % 2, k * S + q * P:k * S + q * P + P],
                                              s[:, q * S + k * P:q * S + k * P + P], ident[:])
                else:
                    for g in range(GROUPS if j in JOBS_DIL else 1):
                        b = 3 + g if j in JOBS_DIL else 3 + j % 2
                        for c in range(3):
                            ins = t.transpose(psum[:, b, c * P:c * P + P],
                                              s[:, 384 * g + c * P:384 * g + c * P + P], ident[:])
                ins.then_inc(pt_ready, 1)

            def weighted(j):
                t.wait_ge(pt_copied, j + 1)
                if j >= 2:
                    t.wait_ge(ol_ready, j - 1)
                b = 6 + j % 2
                if j in JOBS_MLA:
                    p = pt_sb[:, 512 * (j % 2):512 * (j % 2) + 384]
                    h = j - JOBS_MLA[0]
                    rows = slice(64 * (h % 2), 64 * (h % 2) + 64)
                    t.matmul(psum[rows, b, 0:256], v_mla[:, 0, 64 * h:64 * h + 64], p[:, 0:256], start=True,
                             stop=False, skip_group_check=True)
                    ins = t.matmul(psum[rows, b, 128:256], v_mla[:, 1, 64 * h:64 * h + 64], p[:, 256:384],
                                   start=False, stop=True, skip_group_check=True)
                elif j in JOBS_DIL:
                    for g in range(GROUPS):
                        h = g * HD + j
                        p = pt_sb[:, 384 * g:384 * g + 384]
                        t.matmul(psum[:, b, 0:256], v_d[:, 0, P * h:P * h + P], p[:, 0:256], start=g == 0,
                                 stop=False, skip_group_check=True)
                        ins = t.matmul(psum[:, b, 128:256], v_d[:, 1, P * h:P * h + P], p[:, 256:384],
                                       start=False, stop=g == GROUPS - 1, skip_group_check=True)
                else:
                    h = j - JOBS_MEM[0]
                    for k in range(2):
                        ins = t.matmul(psum[:, b, 0:256], v_mem[:, k, P * h:P * h + P],
                                       pt_sb[:, 512 * (j % 2) + k * S:512 * (j % 2) + k * S + S], start=k == 0,
                                       stop=k == 1)
                ins.then_inc(o_ready, 1)

            def gate_product(j, second):
                n = gate_unit(j, second)
                if j == JOBS_MLA[0]:
                    t.wait_ge(pt_copied if second else m_ready, HD)
                taken_at(t, n - 2)
                tile_product(n, 16, out_ap=gate_bank(n))

            taken_at(t, U["memq"] + 3)
            scores(0)
            for j in range(JOBS_MEM[-1] + 1):
                if j + 1 == JOBS_MLA[0]:
                    t.wait_ge(rope_done, 4)
                if j < JOBS_MEM[-1]:
                    scores(j + 1)
                if j in JOBS_DIL:
                    transposes(j)
                else:
                    gate_product(j, 0)
                    transposes(j)
                    gate_product(j, 1)
                weighted(j)
            taken_at(t, U["gates"] + 23)
            t.wait_ge(ol_ready, JOBS_MEM[-1] + 1)
            for b in range(3):
                for q in range(4):
                    n = U["branch"] + 4 * b + q
                    taken_at(t, n - 3)
                    unit(n)
                    wh, wl = (w[:, n % SLOTS, :].rearrange("p (k h m) -> p k h m", k=4, h=2) for w in (w_hi, w_lo))
                    slot = (8, 0, 4)[b]
                    for h in range(2):
                        for k in range(4):
                            ins = mm3(half(n % 4, h), wh[:, k, h, :], wl[:, k, h, :], act[:, slot + k, 0, :],
                                      act[:, slot + k, 1, :], k == 0, k == 3)
                    ins.then_inc(unit_used, 1)
            k_product("wo", 0, 8, lambda k: 16 + k, lambda k: t.wait_ge(merged_lo, k // 2 + 1), 1, total=8)
            norm_sum(N_MIX, sq, KD, at=0)
            norm_sum(N_FFN, sq, KD)
            with t.Fori(0, 11) as i:
                loops = ((i, 4, 11),)
                for r in range(4):
                    n = U["up"] + r
                    ring_free(t, n, loops, U["up"])
                    tile_product(n, 16, loops, split_tile(N_FFN) if r == 0 else None)
            t.wait_ge(z_free, 9)
            k_product("down", 0, KF, lambda k: k, lambda k: k >= 16 and t.wait_ge(al_done, (k - 16) // 2 + 1),
                      1, total=KF)
            norm_sum(N_FFN_OUT, sq, KD, at=0)

            with t.Fori(0, LAYERS) as lay:
                L = (lay, PER_LAYER, LAYERS)
                norm_sum(N_LAYER, sq, KD, lay)
                with t.Fori(0, 4) as i:
                    loops = (L, (i, 4, 4))
                    for r in range(4):
                        n = U["conv"] + r
                        ring_free(t, n, loops, U["conv"])
                        tile_product(n, 16, loops, split_tile(N_LAYER, lay) if r == 0 else None)
                for u in range(2):
                    n = U["rg"] + u
                    unit(n, (L,))
                    if u == 0:
                        t.wait_ge(xs_lo, lay * 6 + 2)
                        taken_at(t, U["conv"] + 15, (L,))
                    wh, wl = wide(n)
                    for h in range(HR):
                        ins = mm3(half(4 * u + h // 2, h % 2), wh[:, h, :], wl[:, h, :], act[:, 8 + h, 0, :],
                                  act[:, 8 + h, 1, :], True, True)
                    ins.then_inc(unit_used, 1)

                def tiles(name, *which):
                    for m in which:
                        n = U[name] + m
                        taken_at(t, U["rg"] if name == "z" and m < 3 else n - 3, (L,))
                        tile_product(n, 16, (L,))

                tiles("z", *range(8))
                for name, slot, first in (("mlq", 8, 4), ("mlk", 8, 0), ("mlv", 0, 4)):
                    for u in range(2):
                        n = U[name] + u
                        unit(n, (L,))
                        if name == "mlq":
                            taken_at(t, U["rg"] + 1, (L,))
                            t.wait_ge(xs_lo, lay * 6 + 6)
                        elif name == "mlk":
                            taken_at(t, U["z"] + 7, (L,))
                        else:
                            taken_at(t, U["mlq"] + u, (L,))
                        wh, wl = (w[:, n % SLOTS, :].rearrange("p (h k m) -> p h k m", h=2, k=2)
                                  for w in (w_hi, w_lo))
                        for h in range(2):
                            for m in range(2):
                                for k in range(2):
                                    s = slot + 4 * u + 2 * h + k
                                    ins = mm3(half(first + 2 * u + h, m), wh[:, h, k, m * P:m * P + P],
                                              wl[:, h, k, m * P:m * P + P], act[:, s, 0, :], act[:, s, 1, :],
                                              k == 0, k == 1)
                        ins.then_inc(unit_used, 1)

                tiles("late", 0)
                taken_at(t, U["mlv"] + 1, (L,))
                for blk in range(2):
                    for c in range(24):
                        src = (q_ml, k_ml, v_ml)[c // 8]
                        ins = t.matmul(psum[:, 7, 8 * blk:8 * blk + 8], src[:, c % 8, blk * P:blk * P + P],
                                       c2("w_if", 8 * c, 8), start=c == 0, stop=c == 23, skip_group_check=True)
                ins.then_inc(gt_ready, 1)
                tiles("late", 1)
                t.wait_ge(gt_done, lay + 1)
                for blk in range(2):
                    for part in range(2):
                        ins = t.transpose(psum[0:HL, 6, part * S + blk * P:part * S + blk * P + P],
                                          gate_tok[:, blk, 4 * part:4 * part + 4], ident[:])
                ins.then_inc(gr_ready, 1)
                for q in range(4):
                    if q == 2:
                        tiles("late", 2)
                    if q >= 2:
                        t.wait_ge(vt_copied, lay * 4 + (q - 1))
                    for c in range(4):
                        ins = t.transpose(psum[:, 4 + q % 2, c * P:c * P + P],
                                          v_ml[:, 4 * (q % 2) + c, (q // 2) * P:(q // 2) * P + P], ident[:])
                    ins.then_inc(vt_ready, 1)

                def ml_scores(h):
                    if h:
                        t.wait_ge(sw_ready, lay * HL + h)
                    for k in range(2):
                        m = 2 * h + k
                        t.matmul(psum[:, 4, 0:256], k_ml[:, m, 0:128], q_ml[:, m, :], start=k == 0,
                                 stop=False, skip_group_check=True)
                    for k in range(2):
                        m = 2 * h + k
                        ins = t.matmul(psum[:, 4, 256:384], k_ml[:, m, 128:256], q_ml[:, m, 128:256],
                                       start=False, stop=k == 1, skip_group_check=True)
                    ins.then_inc(st_ready, 1)

                def spread(h):
                    if h:
                        t.wait_ge(floor_ready, lay * HL + h)
                    t.matmul(bank(5), ident[0:HL, h:h + 1].to_broadcast([HL, P]), neg_row, start=True,
                             stop=True).then_inc(mb_ready, 1)

                tiles("late", 3)
                t.wait_ge(vt_copied, lay * 4 + 4)
                ml_scores(0)
                tiles("late", 4, 5, 6, 7)
                t.wait_ge(rows_done, lay + 1)
                for blk in range(2):
                    ins = t.matmul(psum[:, 7, 4 * blk:4 * blk + 4], row[0][:, blk * P:blk * P + P],
                                   ident[0:HL, 0:HL], start=True, stop=True, skip_group_check=True)
                ins.then_inc(cc_ready, 1)
                spread(0)
                for h in range(HL):
                    tiles("late", 8 + 2 * h, 9 + 2 * h)
                    if h + 1 < HL:
                        spread(h + 1)
                    t.wait_ge(sw_ready, lay * HL + (h + 1))
                    if h:
                        t.wait_ge(cell_done, lay * HL + h)
                    else:
                        t.wait_ge(cc_done, lay + 1)
                    sw = sw_ml[:, h % 2, :]
                    for dv in range(2):
                        c = 256 * h + 128 * dv
                        t.matmul(half(6, dv), v_tok[:, 0, c:c + P], sw[:, 0:256], start=dv == 0, stop=False,
                                 skip_group_check=True)
                        t.matmul(psum[:, 6, dv * S + 128:dv * S + 256], v_tok[:, 1, c:c + P],
                                 sw[:, 256:384], start=False, stop=True, skip_group_check=True)
                    t.matmul(psum[:, 7, 0:256], ones[:], sw[:, 0:256], start=True, stop=False,
                             skip_group_check=True)
                    t.matmul(psum[:, 7, 128:256], ones[:], sw[:, 256:384], start=False, stop=True,
                             skip_group_check=True).then_inc(num_ready, 1)
                    if h + 1 < HL:
                        ml_scores(h + 1)
                for k in range(16):
                    n = U["out"] + k
                    if k == 0:
                        taken_at(t, U["late"] + 15, (L,))
                    if k == 2:
                        t.wait_ge(cell_done, lay * HL + HL)
                        for h in range(HL):
                            t.wait_ge(hsq_done, lay * HL + (h + 1))
                            for kk in range(2):
                                ins = t.matmul(half(4 + h, 0), ones[:], sq_ml[:, 2 * h + kk, :], start=kk == 0,
                                               stop=kk == 1)
                            ins.then_inc(hss_done, 1)
                    unit(n, (L,))
                    if k in (0, 4):
                        t.wait_ge(yl_done, lay * 6 + (k // 4 + 1))
                    elif k >= 8 and k % 2 == 0:
                        t.wait_ge(yl_done, lay * 6 + (2 + (k - 8) // 2 + 1))
                    slot = (k + 8) % 16
                    wh, wl = wide(n)
                    for m in range(KD):
                        ins = mm3(half(m // 2, m % 2), wh[:, m, :], wl[:, m, :], act[:, slot, 0, :],
                                  act[:, slot, 1, :], k == 0 and m % 2 == 0, k == 15)
                    ins.then_inc(unit_used, 1)
            norm_sum(N_FINAL, sq, KD)


def _tile_columns(w):
    k, n = w.shape
    return w.reshape(k // P, P, n // P, P).transpose(2, 1, 0, 3).reshape(n // P, P, k)


def _pack_units(i):
    w_in = i["w_in"][0]
    off_kv, off_kr = 384, 640
    off_dil, off_memq, off_gate = 672, 5280, 5792
    units = []

    def put(a):
        units.append(np.ascontiguousarray(a, np.float32))

    def value_units(w):
        n = w.shape[1] // S
        put(w.reshape(2, 4, P, n, S).transpose(3, 0, 2, 1, 4).reshape(2 * n, P, UNIT))

    w_mem = i["w_mem_kv"][0]
    put(_tile_columns(w_mem[:, :512]))
    value_units(w_mem[:, 512:])
    put(_tile_columns(w_in[:, :off_kr]))
    kr = w_in[:, off_kr:off_dil]
    last = np.zeros((D, P), np.float32)
    last[:, 64:96] = kr
    last[:, 96:112] = kr[:, 16:]
    last[:, 112:128] = kr[:, :16]
    put(_tile_columns(last))
    dil = w_in[:, off_dil:off_memq]
    put(_tile_columns(dil[:, :3072]))
    value_units(dil[:, 3072:])
    uq = i["w_uq"][0].reshape(KQ, P, HM, NOPE + ROPE)
    full = np.zeros((KQ, P, HM, P), np.float32)
    full[..., :96] = uq
    full[..., 96:112] = uq[..., 80:96]
    full[..., 112:128] = uq[..., 64:80]
    uq_units = np.zeros((4, P, UNIT), np.float32)
    uq_units[:, :, :768] = full.reshape(KQ, P, 4, 2, P).transpose(2, 1, 0, 3, 4).reshape(4, P, 768)
    put(uq_units)
    ukv = i["w_ukv"][0].reshape(KKV, P, HM, NOPE + VM)
    put(ukv[..., :NOPE].transpose(1, 0, 2, 3).reshape(1, P, UNIT))
    put(ukv[..., NOPE:].transpose(1, 0, 2, 3).reshape(1, P, UNIT))
    put(_tile_columns(w_in[:, off_memq:off_gate]))
    put(_tile_columns(w_in[:, off_gate:]))
    for name in ("w_br_mla", "w_br_dil", "w_br_mem"):
        w = i[name][0]
        put(w.reshape(4, P, 4, 2, P).transpose(2, 1, 0, 3, 4).reshape(4, P, UNIT))
    put(i["w_o"][0].reshape(KD, P, D))
    up = i["w_ffn_up"][0]
    g, v = _tile_columns(up[:, :FF]), _tile_columns(up[:, FF:])
    put(np.stack([g, v], 1).reshape(2 * KF, P, UNIT))
    put(i["w_ffn_down"][0].reshape(KF, P, D))
    for lay in range(LAYERS):
        w = i["w_in_2"][lay]
        def inputs_of(*parts):
            for part in parts:
                put(_tile_columns(w[:, part * D:(part + 1) * D]))

        inputs_of(0, 2)
        for name in ("rg_w_x_2", "rg_w_a_2"):
            put(i[name][lay].transpose(1, 0, 2).reshape(1, P, UNIT))
        inputs_of(1)
        for name in ("ml_w_q_2", "ml_w_k_2", "ml_w_v_2"):
            put(i[name][lay].reshape(2, 2, 2, P, 256).transpose(0, 3, 1, 2, 4).reshape(2, P, UNIT))
        inputs_of(4, 3)
        put(i["w_out_2"][lay].reshape(16, P, D))
    out = np.concatenate(units)
    assert out.shape == (NU, P, UNIT), out.shape
    return out


def _col(a):
    return np.ascontiguousarray(a.reshape(-1, P).T)


def _pack_params(i):
    par1 = np.zeros((P, NP1), np.float32)

    def put(par, cols, name, a):
        at, n = cols[name]
        assert a.shape == (P, n), (name, a.shape, n)
        par[:, at:at + n] = a

    for name, key in (("g_pre_mix", "g_pre_mix"), ("g_mem", "g_mem"), ("q_norm", "mla_q_norm"),
                      ("kv_norm", "mla_kv_norm"), ("b_gate", "b_gate"), ("g_post_mix", "g_post_mix"),
                      ("g_pre_ffn", "g_pre_ffn"), ("g_post_ffn", "g_post_ffn"),
                      ("b_ada", "b_ada_2"), ("final_g", "final_g_2")):
        put(par1, C1, name, _col(i[key]))
    w = i["conv_w"][0].reshape(3, 2, KF, P).transpose(0, 2, 1, 3)
    put(par1, C1, "conv_w", _col(w))
    put(par1, C1, "conv_b", _col(i["conv_b"][0].reshape(2, KF, P).transpose(1, 0, 2)))
    half_dim = ROPE // 2
    freq = np.float32(10000.0) ** (-np.arange(half_dim, dtype=np.float32) / np.float32(half_dim))
    put(par1, C1, "freq", np.tile(freq.astype(np.float32), P // half_dim)[:, None])
    put(par1, C1, "sign", np.tile(np.repeat([-1.0, 1.0], half_dim), P // ROPE)[:, None])
    par2 = np.zeros((LAYERS, P, NP2), np.float32)
    for lay in range(LAYERS):
        for name, key in (("norm_g", "norm_g_2"), ("rg_w", "rg_conv_w_2"), ("rg_b", "rg_conv_b_2"),
                          ("b_a", "rg_b_a_2"), ("b_x", "rg_b_x_2"), ("lam", "rg_lambda_2"),
                          ("ml_w", "ml_conv_w_2"), ("ml_b", "ml_conv_b_2"), ("head_g", "ml_norm_g_2")):
            put(par2[lay], C2, name, _col(i[key][lay]))
        put(par2[lay], C2, "b_if", np.broadcast_to(i["ml_b_if_2"][lay], (P, 2 * HL)))
        put(par2[lay], C2, "w_if", i["ml_w_if_2"][lay].reshape(24, P, 2 * HL).transpose(1, 0, 2).reshape(P, -1))
    return par1, par2


def kernel(**inputs):
    import concourse.bacc as bacc
    from concourse.bass_utils import run_bass_kernel_spmd

    i = {k: np.asarray(v) for k, v in inputs.items()}

    def features(a):
        return np.ascontiguousarray(a[0].T.reshape(KD, P, S).transpose(1, 0, 2))

    par1, par2 = _pack_params(i)
    arrays = {
        "w_units": _pack_units(i),
        "w_ada": np.ascontiguousarray(i["w_ada_2"].transpose(0, 2, 1).reshape(24 * LAYERS, P, D)),
        "x_in": features(i["x"]),
        "mem_in": features(i["mem"]),
        "pos_in": np.ascontiguousarray(np.broadcast_to(i["positions"].astype(np.int32), (P, S))),
        "c_in": np.ascontiguousarray(np.broadcast_to(i["c_2"], (P, D))),
        "par1_in": par1,
        "par2_in": par2,
    }
    nc = bacc.Bacc("TRN2", target_bir_lowering=False, num_devices=1)
    args = {n: nc.dram_tensor(n, a.shape, mybir.dt.from_np(a.dtype), kind="ExternalInput").ap()
            for n, a in arrays.items()}
    out = nc.dram_tensor("out", (P, KD, S), F32, kind="ExternalOutput").ap()
    program(nc, out=out, **args)
    r = run_bass_kernel_spmd(nc, [arrays], core_ids=[0])
    y = r.results[0]["out"]
    return np.ascontiguousarray(y.transpose(1, 0, 2).reshape(D, S).T)[None]
```

```python
from contextlib import ExitStack, contextmanager

import concourse.bass as bass
import numpy as np
from concourse import mybir

F32 = mybir.dt.float32
F32R = mybir.dt.float32r
I32 = mybir.dt.int32
ACT = mybir.ActivationFunctionType
ALU = mybir.AluOpType
AX = mybir.AxisListType

P = 128
S = 256
D = 1024
KD = D // P
EPS = 1e-6
NEG = -1e30
UNIT = 1024
SLOTS = 4

HM, NOPE, ROPE, VM = 8, 64, 32, 64
KQ, KKV = 3, 2
GROUPS, HD, DH = 3, 4, 128
DILATION = (1, 4, 16)
SPAN = 128
FF = 2816
KF = FF // P
LAYERS = 2
HR = 8
HL = 4
RG_C = 8.0

_ORDER = (("memk", 4), ("memv", 4), ("latent", 6), ("qk", 24), ("v", 12), ("ukvk", 1), ("ukvv", 1),
          ("uq", 4), ("memq", 4), ("gates", 24), ("branch", 12), ("wo", 8), ("up", 2 * KF), ("down", KF))
_LAYER = (("conv", 16), ("z0", 4), ("rg_i", 1), ("z4", 1), ("rg_r", 1), ("z5", 3), ("mlq", 2), ("mlk", 2),
          ("mlv", 2), ("late", 16), ("out", 16))
U = {}
_at = 0
for _n, _c in _ORDER:
    U[_n] = _at
    _at += _c
LAYER0 = _at
for _n, _c in _LAYER:
    U[_n] = _at
    _at += _c
PER_LAYER = _at - LAYER0
Z_UNITS = [U["z0"] + m for m in range(4)] + [U["z4"]] + [U["z5"] + m for m in range(3)]
GATE_ROWS_BANK = (U["late"] + 3) % 4
LATE_TILES = [0, 1, 2, 3, 4, 8, 9, 5, 10, 11, 6, 12, 13, 7, 14, 15]
NU = LAYER0 + LAYERS * PER_LAYER


def _owners():
    own = ["a"] * NU

    def put(first, what):
        own[first:first + len(what)] = list(what)

    put(U["memv"], ".a" * 2)
    put(U["latent"] + 5, "v")
    put(U["v"], ".a" * 6)
    put(U["uq"], "v" * 4)
    put(U["branch"], "v" * 12)
    put(U["wo"], "." * 8)
    put(U["up"], "v" * 2 * KF)
    put(U["down"], "." * KF)
    for lay in range(LAYERS):
        o = lay * PER_LAYER
        put(U["conv"] + o, "v" * 16)
        put(U["mlk"] + o, "v" * 2)
        put(U["out"] + o, "." * 16)
    return own


OWNER = _owners()
TAKEN = {e: [sum(o == e for o in OWNER[:n + 1]) for n in range(NU)] for e in "av"}

LAYER_A = TAKEN["a"][LAYER0 + PER_LAYER] - TAKEN["a"][LAYER0]

_C1 = (("g_pre_mix", KD), ("g_mem", KD), ("q_norm", KQ), ("kv_norm", KKV), ("b_gate", 24), ("g_post_mix", KD),
       ("g_pre_ffn", KD), ("conv_w", 3 * 2 * KF), ("conv_b", 2 * KF), ("g_post_ffn", KD),
       ("b_ada", 24 * LAYERS), ("freq", 1), ("sign", 1), ("final_g", KD))
_C2 = (("norm_g", KD), ("rg_w", 4 * KD), ("rg_b", KD), ("b_a", KD), ("b_x", KD), ("lam", KD), ("ml_w", 4 * KD),
       ("ml_b", KD), ("head_g", KD), ("b_if", 1), ("w_if", 24 * 2 * HL))


def _columns(spec):
    at, out = 0, {}
    for name, n in spec:
        out[name] = (at, n)
        at += n
    return out, at


C1, NP1 = _columns(_C1)
C2, NP2 = _columns(_C2)

NORMS = [(KD, True), (KD, True), (KQ, True), (KKV, True), (KD, False), (KD, True), (KD, False),
         (KD, True), (KD, True), (KD, False)]
N_MEM, N_X, N_CQ, N_CKV, N_MIX, N_FFN, N_FFN_OUT, N_LAYER, N_FINAL = 0, 1, 2, 3, 4, 5, 6, 7, 9
SPLIT_BEFORE = [sum(k for k, s in NORMS[:n] if s) for n in range(len(NORMS) + 1)]
SQUARES_BEFORE = [sum((k + 1) // 2 for k, _ in NORMS[:n]) for n in range(len(NORMS) + 1)]
PAIRS = KD // 2

FIRST_UNITS = [LAYER0 + lay * PER_LAYER + m for lay in range(LAYERS + 1) for m in range(3)]

ADA_BETWEEN = ((0, 1), (2,), (3, 4), (5,))

JOBS_DIL, JOBS_MLA, JOBS_MEM = range(0, HD), range(HD, HD + HM), range(HD + HM, 2 * HD + HM)


def affine(need, limit):
    for d in {b - a for a, b in zip(need, need[1:])} | {0}:
        a = max(x - d * i for i, x in enumerate(need))
        if all(a + d * i <= y for i, y in enumerate(limit)):
            return a, d
    raise ValueError(f"no line between {need} and {limit}")


def program(nc, w_units, w_ada, x_in, mem_in, pos_in, c_in, par1_in, par2_in, out):
    ctx = ExitStack()
    with ctx:
        def sb(name, shape, dt=F32):
            return ctx.enter_context(nc.sbuf_tensor(name, shape, dt))

        def sem(name):
            return ctx.enter_context(nc.semaphore(name))

        raw = sb("raw", [P, SLOTS, UNIT])
        w_hi = sb("w_hi", [P, SLOTS, UNIT], F32R)
        w_lo = sb("w_lo", [P, SLOTS, UNIT], F32R)
        act = sb("act", [P, 24, 2, S], F32R)
        x = sb("x", [P, KD, S])
        ar_d = sb("ar_d", [P, 36, S])
        ar_g = sb("ar_g", [P, 24, S])
        ar_m = sb("ar_m", [P, 12, S])
        ar_p = sb("ar_p", [P, 3456])
        dist = sb("dist", [P, GROUPS, 384])
        causal = sb("causal", [P, 384])
        causal_t = sb("causal_t", [P, 384])
        ident = sb("ident", [P, P])
        ones = sb("ones", [P, P])
        std_rstd = sb("std_rstd", [P, 2, S])
        std, rstd = std_rstd[:, 0, :], std_rstd[:, 1, :]
        par1 = sb("par1", [P, NP1])
        par2 = sb("par2", [P, NP2])
        mod = sb("mod", [P, 24 * LAYERS])
        small = sb("small", [P, 64])
        tiny = sb("tiny", [P, 24])
        psum = ctx.enter_context(nc.psum_tensor("psum", [P, 8, 512], F32))
        eps = tiny[:, 0:1]

        def c1(name, j=0, n=1):
            at = C1[name][0]
            if isinstance(j, int):
                return par1[:, at + j:at + j + n]
            return par1[:, bass.ds(j + at, n)]

        def c2(name, j=0, n=1):
            at = C2[name][0]
            return par2[:, at + j:at + j + n]

        def flat(ap):
            return ap.rearrange("p a b -> p (a b)")

        memx = ar_d[:, 0:8, :]
        latent = ar_g[:, 0:5, :]
        qk_d = ar_d[:, 0:24, :]
        v_d = ar_d[:, 24:36, :].rearrange("p a b -> p (a b)").rearrange("p (s n) -> p s n", s=2)
        q_mla = ar_g[:, 0:8, :]
        k_mla = ar_g[:, 8:16, :]
        v_mla = flat(ar_g[:, 16:20, :]).rearrange("p (s n) -> p s n", s=2)
        cos_t = ar_g[:, 20, :]
        sin_t = ar_g[:, 21, :]
        rope_tmp = ar_g[:, 22:24, :]
        k_mem = ar_m[:, 0:4, :]
        v_mem = flat(ar_m[:, 4:8, :]).rearrange("p (s n) -> p s n", s=2)
        q_mem = ar_m[:, 8:12, :]
        cact = flat(q_mem)
        ada = ar_p[:, 0:3072].rearrange("p (r n) -> p r n", r=3)
        s_sb = ar_p[:, 0:2304].rearrange("p (r n) -> p r n", r=2)
        pt_sb = ar_p[:, 2304:3456]
        gates = ar_d[:, 0:24, :]
        merged = ar_d[:, 24:32, :]
        branch_y = ar_d[:, 32:36, :]
        sq = ar_d[:, 16:24, :]
        tn = ar_d[:, 24:32, :]
        late = ar_g[:, 0:6, :]
        z_up = ar_p[:, 0:1024].rearrange("p (r n) -> p r n", r=4)
        u_rg = ar_d[:, 0:8, :]
        xc = ar_d[:, 8:16, :]
        xm = ar_d[:, 16:24, :]
        so = ar_d[:, 24:32, :]
        zy = ar_g[:, 0:16, :]
        k_ml = ar_g[:, 16:24, :]
        q_ml = ar_m[:, 0:8, :]
        rg_r = so
        rg_sq = xc
        rg_t = ar_p[:, 0:2048].rearrange("p (a b) -> p a b", b=S)
        rg_i = (ar_m[:, 8:12, :], ar_d[:, 32:36, :])
        v_ml = u_rg
        v_tok = flat(xm).rearrange("p (s n) -> p s n", s=2)
        sq_ml = xc
        row = [ar_p[0:HL, 2048 + S * i:2048 + S * (i + 1)] for i in range(5)]
        gate_rows = ar_p[0:2 * HL, 2048:2048 + S]
        neg_row = flat(std_rstd[0:HL, :, :])
        c_col = small[:, 16:24].rearrange("p (s h) -> p s h", s=2)
        w_ml = flat(xc)[:, 0:768].rearrange("p (r n) -> p r n", r=2)
        sw_ml = flat(xc)[:, 768:1536].rearrange("p (r n) -> p r n", r=2)
        floor_ml = xc[:, 6:8, :]
        den_ml = ar_p[:, 1792:2048]
        soft = tiny[:, 8:16]
        nsoft = tiny[:, 16:24]
        gain2 = small[:, 24:32]
        t8 = [small[:, 32 + 8 * i:40 + 8 * i] for i in range(4)]

        def bank(b):
            return psum[:, b, :]

        def half(b, m):
            return psum[:, b, m * S:(m + 1) * S]

        def stat(j, q, k):
            at = (j % 2) * 8 + k * 2
            return small[:, at:at + 2] if q is None else small[:, at + q:at + q + 1]

        def score_views(j):
            s = s_sb[:, j % 2, :]
            if j in JOBS_MLA:
                views = [s[:, 0:128], s[:, 128:384]]
            elif j in JOBS_DIL:
                s = s.rearrange("p (g n) -> p g n", g=3)
                views = [s[:, :, 0:128], s[:, :, 128:384]]
            else:
                return [(psum[:, j % 2, q * S:(q + 1) * S], s[:, q * S:(q + 1) * S]) for q in range(2)]
            return [(v, v) for v in views]

        def head_rows(j):
            if j in JOBS_MLA:
                h = j - JOBS_MLA[0]
                return 64 * (h % 2), 64 * (h % 2) + 64, 8 + h // 2
            return 0, P, j if j in JOBS_DIL else HD + j - JOBS_MEM[0]

        def side_unit(j, second):
            return U["uq"] + 2 * j + second

        def out_bank(j):
            return 6 if j in JOBS_DIL else 6 + j % 2

        def gate_unit(j, second):
            return U["gates"] + 2 * (j - JOBS_MLA[0]) + second

        def gate_bank(n):
            return half((2, 5)[n % 2], 0)

        raw_in = [sem(f"raw_in{r}") for r in range(SLOTS)]
        ada_in = [sem(f"ada_in{r}") for r in range(3)]
        c_in_s, x_in_s, mem_in_s, par_in, par2_in_s, pos_in_s, out_s = (sem(n) for n in (
            "c_landed", "x_landed", "mem_landed", "par1_landed", "par2_landed", "pos_landed", "out_landed"))
        hi_done, lo_done, unit_used = sem("hi_done"), sem("lo_done"), sem("unit_used")
        taken = {"a": sem("taken_act"), "v": sem("taken_dve")}
        ada_used, mod_done, cact_done = sem("ada_used"), sem("mod_done"), sem("cact_done")
        sq_done, ss_done, std_done, rstd_done = (sem(n) for n in ("sq_done", "ss_done", "std_done", "rstd_done"))
        tn_done, nh_done, nl_done, res_done = (sem(n) for n in ("tn_done", "nh_done", "nl_done", "res_done"))
        masks_done, tables_done, rope_done, k_pe_done = (sem(n) for n in (
            "masks_done", "tables_done", "rope_done", "k_pe_done"))
        angle_done, sine_done = sem("angle_done"), sem("sine_done")
        s_ready, m_ready, e_ready, p_ready, pt_ready, pt_copied, o_ready, oh_ready, ol_ready = (
            sem(n) for n in ("s_ready", "m_ready", "e_ready", "p_ready", "pt_ready", "pt_copied", "o_ready",
                             "oh_ready", "ol_ready"))
        merge_done, mh_done, merged_lo = sem("merge_done"), sem("mh_done"), sem("merged_lo")
        gates_done = sem("gates_done")
        q_nope = sem("q_nope")
        warmed, z_init, z_free, silu_done, prod_done, ah_done, al_done = (sem(n) for n in (
            "warmed", "z_init", "z_free", "silu_done", "prod_done", "ah_done", "al_done"))
        (xc_silu, xs_hi, xs_lo, rg_tanh, rg_exp, rg_arg, rg_sqrt, yr_done, yh_done, yl_done, sp_exp, sp_done,
         vt_ready, vt_copied, gt_ready, gt_done, gr_ready, f_abs, f_exp, rows_done, cc_ready, cc_done,
         mb_ready, wm_ready, we_ready, floor_ready, st_ready, sw_ready, num_ready, cell_done, hsq_done, hss_done,
         hstd_done) = (sem(n) for n in (
             "xc_silu", "xs_hi", "xs_lo", "rg_tanh", "rg_exp", "rg_arg", "rg_sqrt", "y_done", "yh_done",
             "yl_done", "sp_exp", "sp_done", "vt_ready", "vt_copied", "gt_ready", "gt_done", "gr_ready",
             "f_abs", "f_exp", "rows_done", "cc_ready", "cc_done", "mb_ready", "wm_ready", "we_ready",
             "floor_ready", "st_ready", "sw_ready", "num_ready", "cell_done", "hsq_done", "hss_done", "hstd_done"))
        dve_step, act_step, pool_step = sem("dve_step"), sem("act_step"), sem("pool_step")

        block = ctx.enter_context(nc.Block())

        class Step:

            def __init__(self, eng, semaphore):
                self.eng, self.sem, self.n, self.off = eng, semaphore, 0, 0

            def link(self, ins):
                self.n += 1
                ins.then_inc(self.sem, 1)
                self.eng.wait_ge(self.sem, self.off + self.n)

            @contextmanager
            def turns(self, reg, n, per):
                start, off = self.n, self.off
                self.off = reg * per + off
                yield
                assert self.n - start == per, (self.n - start, per)
                self.n, self.off = start + n * per, off

        def taken_at(eng, n, loops=()):
            for e in "av":
                points = [0]
                for _, step, turns in loops:
                    points = [o + step * i for o in points for i in range(turns)]
                need = [TAKEN[e][n + o] for o in points]
                if need[-1] == 0:
                    continue
                value = None
                if not loops:
                    value = need[0]
                elif len(loops) == 1:
                    a, d = affine(need, need)
                    value = loops[0][0] * d + a if d else a
                else:
                    (lay, step, n0), (reg, _, n1) = loops
                    delta = TAKEN[e][n + step + loops[1][1] * (n1 - 1)] - TAKEN[e][n + loops[1][1] * (n1 - 1)]
                    need = [max(need[i + n1 * j] - delta * j for j in range(n0)) for i in range(n1)]
                    a, d = affine(need, need)
                    value = reg * d + lay * delta + a if d else lay * delta + a
                if isinstance(value, int) and value <= 0:
                    continue
                eng.wait_ge(taken[e], value)

        def ring_free(eng, n, loops, start):
            turns, step = loops[-1][2], loops[-1][1]
            for e in "av":
                need = [TAKEN[e][n - 3 + step * i] for i in range(1, turns)]
                if need[-1] <= TAKEN[e][start - 1]:
                    continue
                most = [TAKEN[e][n - 1 + step * i] for i in range(1, turns)]
                a, d = affine(need, most)
                assert 0 < a - d <= TAKEN[e][n - 1]
                value = loops[-1][0] * d + (a - d)
                if len(loops) == 2:
                    value = loops[0][0] * (TAKEN[e][n + loops[0][1]] - TAKEN[e][n]) + value
                eng.wait_ge(taken[e], value)

        def unit_of(n, loops=()):
            for reg, step, _ in loops:
                n = reg * step + n
            return n

        def landed(n, loops=()):
            v = 16 * (n // SLOTS + 1)
            for reg, step, _ in loops:
                v = reg * (16 * step // SLOTS) + v
            return v

        @block.sync
        def _(sp):
            sp.dma_start(memx, mem_in).then_inc(mem_in_s, 16)
            sp.dma_start(x[:], x_in).then_inc(x_in_s, 16)
            for r in range(SLOTS):
                sp.dma_start(raw[:, r, :], w_units[r]).then_inc(raw_in[r], 16)
            for s in range(3):
                sp.dma_start(ada[:, s, :], w_ada[s]).then_inc(ada_in[s], 16)

            def weights(i, group, r):
                at = i * SLOTS + (group * SLOTS + r + 1)
                sp.wait_ge(lo_done, at)
                sp.dma_start(raw[:, r, :], w_units[bass.ds(at + (SLOTS - 1), 1)].rearrange("a p n -> p (a n)"))\
                    .then_inc(raw_in[r], 16)

            def modulation(k, slot):
                sp.wait_ge(ada_used, k + (-2))
                sp.dma_start(ada[:, slot, :], w_ada[bass.ds(k, 1)].rearrange("a p n -> p (a n)"))\
                    .then_inc(ada_in[slot], 16)

            with sp.Fori(0, 4) as i:
                for r in range(SLOTS):
                    weights(i, 0, r)
            for s in range(3):
                sp.wait_ge(ada_used, s + 1)
                sp.dma_start(ada[:, s, :], w_ada[3 + s]).then_inc(ada_in[s], 16)
            with sp.Fori(0, 6) as i:
                for r in range(SLOTS):
                    weights(i, 4, r)
                    for s in ADA_BETWEEN[r]:
                        modulation(i * 6 + (6 + s), s % 3)
            with sp.Fori(0, 2) as i:
                for r in range(SLOTS):
                    weights(i, 10, r)
                    if r < 3:
                        modulation(i * 3 + (42 + r), r)
            with sp.Fori(0, NU // SLOTS - 1 - 12) as i:
                for r in range(SLOTS):
                    weights(i, 12, r)
            for n in range(NU // SLOTS * SLOTS, NU):
                sp.wait_ge(lo_done, n - SLOTS + 1)
                sp.dma_start(raw[:, n % SLOTS, :], w_units[n]).then_inc(raw_in[n % SLOTS], 16)
            sp.wait_ge(tn_done, SPLIT_BEFORE[-1] + KD)
            sp.dma_start(out, tn[:]).then_inc(out_s, 16)
            sp.wait_ge(out_s, 16)

        @block.gpsimd
        def _(pool):
            step = Step(pool, pool_step)
            link = step.link
            g = nc.gpsimd
            link(g.memset(ident[:], 0.0))
            link(g.affine_select(out=ident[:], in_=ident[:], compare_op=ALU.not_equal, fill=1.0, base=0,
                                 pattern=[[-1, P]], channel_multiplier=1))
            link(g.memset(causal[:], 0.0))
            link(g.memset(causal_t[:], 0.0))
            link(g.affine_select(out=causal[:, 0:128], in_=causal[:, 0:128], compare_op=ALU.is_ge, fill=NEG,
                                 base=0, pattern=[[-1, 128]], channel_multiplier=1))
            link(g.affine_select(out=causal[:, 128:384], in_=causal[:, 128:384], compare_op=ALU.is_ge, fill=NEG,
                                 base=128, pattern=[[-1, 256]], channel_multiplier=1))
            for a in (0, 256):
                link(g.affine_select(out=causal_t[:, a:a + 128], in_=causal_t[:, a:a + 128], compare_op=ALU.is_ge,
                                     fill=NEG, base=0, pattern=[[1, 128]], channel_multiplier=-1))
            di = dist[:, 0, :].bitcast(I32)
            link(g.iota(di[:, 0:128], pattern=[[-1, 128]], base=0, channel_multiplier=1))
            link(g.iota(di[:, 128:384], pattern=[[-1, 256]], base=128, channel_multiplier=1))
            g.memset(ones[:], 1.0).then_inc(masks_done, 1)
            for lay in range(LAYERS):
                if lay:
                    pool.wait_ge(res_done, (2 + lay) * PAIRS)
                pool.dma_start(par2[:], par2_in[lay]).then_inc(par2_in_s, 16)

        @block.scalar
        def _(a):
            step = Step(a, act_step)
            link = step.link
            hold_reg = a.alloc_register("act_hold")
            a.reg_mov(hold_reg, 0)

            def wait(semaphore, value):
                a.wait_ge(semaphore, value)
                if not isinstance(value, int):
                    a.reg_add(hold_reg, hold_reg, 0)

            def hi(n, loops=()):
                a.wait_ge(raw_in[n % SLOTS], landed(n, loops))
                if n >= SLOTS:
                    a.wait_ge(unit_used, unit_of(n - SLOTS + 1, loops))
                a.activation(w_hi[:, n % SLOTS, :], raw[:, n % SLOTS, :], ACT.Copy).then_inc(hi_done, 1)

            def ahead(n, loops=()):
                if n + 3 not in FIRST_UNITS:
                    hi(n + 3, loops)

            def product(n, loops=()):
                wait(unit_used, unit_of(n + 1, loops))

            def norm_square(n, src, dst, k):
                if n:
                    a.wait_ge(ss_done, n)
                for j in range(0, k, 2):
                    a.activation(dst[:, j:min(j + 2, k), :], src[:, j:min(j + 2, k), :], ACT.Square)\
                        .then_inc(sq_done, 1)

            def residual_square(norms, residuals):
                a.wait_ge(ss_done, norms)
                for c in range(PAIRS):
                    a.wait_ge(res_done, residuals * PAIRS + (c + 1))
                    a.activation(sq[:, 2 * c:2 * c + 2, :], x[:, 2 * c:2 * c + 2, :], ACT.Square)\
                        .then_inc(sq_done, 1)

            def norm_std(n, k, lay=0, at=4):
                a.wait_ge(ss_done, lay + (n + 1))
                if n:
                    a.wait_ge(rstd_done, lay + n)
                a.activation(std, half(at, 0), ACT.Sqrt, bias=eps, scale=1.0 / (k * P)).then_inc(std_done, 1)

            def norm_hi(n, k, slot, src):
                for j in range(k):
                    a.wait_ge(tn_done, SPLIT_BEFORE[n] + j + 1)
                    a.activation(act[:, slot + j, 0, :], src[:, j, :], ACT.Copy).then_inc(nh_done, 1)

            a.dma_start(par1[:], par1_in).then_inc(par_in, 16)
            a.dma_start(cact, c_in).then_inc(c_in_s, 16)
            a.dma_start(ar_g[:, 20, :].bitcast(I32), pos_in).then_inc(pos_in_s, 16)
            a.wait_ge(mem_in_s, 16)
            norm_square(N_MEM, memx, sq, KD)
            a.wait_ge(x_in_s, 16)
            for j in range(0, KD, 2):
                a.activation(ar_g[:, j:j + 2, :], x[:, j:j + 2, :], ACT.Square).then_inc(sq_done, 1)
            a.wait_ge(tables_done, 1)
            norm_std(N_MEM, KD)
            hi(0)
            norm_std(N_X, KD, at=5)
            norm_hi(N_MEM, KD, 0, tn)
            hi(1)
            hi(2)
            ahead(U["memk"])
            norm_hi(N_X, KD, 16, ar_g[:, 8:16, :])
            ahead(U["memk"] + 1)
            ahead(U["memk"] + 2)
            for m in range(4):
                n = U["memk"] + m
                product(n)
                if m == 1:
                    ahead(U["memk"] + 3)
                elif m == 2:
                    a.wait_ge(angle_done, 1)
                    a.activation(cos_t[64:96, :], rope_tmp[64:96, 0, :], ACT.Sin, scale=0.5).then_inc(sine_done, 1)
                    a.activation(sin_t[96:128, :], rope_tmp[96:128, 0, :], ACT.Sin).then_inc(sine_done, 1)
                a.activation(k_mem[:, m, :], half(n % 4, 0), ACT.Copy).then_inc(taken["a"], 1)
            for m in range(2):
                n = U["memv"] + 2 * m
                ahead(n)
                ahead(n + 1)
                product(n + 1)
                a.activation(v_mem[:, :, m * S:(m + 1) * S], bank(n % 4).rearrange("p (s n) -> p s n", s=2),
                             ACT.Copy).then_inc(taken["a"], 1)
            a.wait_ge(c_in_s, 16)
            a.activation(cact, cact, ACT.Silu).then_inc(cact_done, 1)
            for m in range(5):
                n = U["latent"] + m
                ahead(n)
                product(n)
                if m == 0:
                    a.wait_ge(nl_done, 2 * KD)
                ins = a.activation(latent[:, m, :], half(n % 4, 0), ACT.Copy).then_inc(taken["a"], 1)
                if m == KQ - 1:
                    a.wait_ge(taken["a"], TAKEN["a"][n])
                    norm_square(N_CQ, latent[:, 0:KQ, :], ar_g[:, 5:8, :], KQ)
            a.wait_ge(taken["a"], TAKEN["a"][U["latent"] + 4])
            norm_square(N_CKV, latent[:, KQ:5, :], ar_g[:, 8:10, :], KKV)
            ahead(U["latent"] + 5)
            norm_std(N_CQ, KQ)
            norm_std(N_CKV, KKV)
            norm_hi(N_CQ, KQ, 8, ar_g[:, 10:13, :])
            norm_hi(N_CKV, KKV, 11, ar_g[:, 13:15, :])

            with a.Fori(0, 6) as i:
                loops = ((i, 4, 6),)
                for r in range(4):
                    n = U["qk"] + r
                    ahead(n, loops)
                    product(n, loops)
                    a.activation(qk_d[:, bass.ds(i * 4 + r, 1), :].rearrange("p a n -> p (a n)"), half(n % 4, 0),
                                 ACT.Copy).then_inc(taken["a"], 1)
            with a.Fori(0, 3) as i:
                loops = ((i, 4, 3),)
                for r in range(0, 4, 2):
                    n = U["v"] + r
                    ahead(n, loops)
                    ahead(n + 1, loops)
                    product(n + 1, loops)
                    a.activation(v_d[:, :, bass.ds(i * 2 * S + r // 2 * S, S)],
                                 bank(n % 4).rearrange("p (s n) -> p s n", s=2), ACT.Copy).then_inc(taken["a"], 1)

            a.wait_ge(nl_done, SPLIT_BEFORE[N_CKV + 1])
            n = U["ukvk"]
            ahead(n)
            product(n)
            for m in range(4):
                for hh in range(2):
                    ins = a.activation(k_mla[0:64, 2 * m + hh, :], psum[64 * hh:64 * hh + 64, 4 + m // 2,
                                                                      (m % 2) * S:(m % 2 + 1) * S], ACT.Copy)
            ins.then_inc(taken["a"], 1)
            n = U["ukvv"]
            ahead(n)
            product(n)
            a.wait_ge(k_pe_done, 1)
            for blk in range(2):
                ins = a.activation(v_mla[:, blk, :], bank(6 + blk), ACT.Copy)
            ins.then_inc(taken["a"], 1)
            a.wait_ge(mod_done, 1)

            def side_out(j, second):
                n = side_unit(j, second)
                ahead(n)
                product(n)
                m = n - U["uq"]
                if m < 4:
                    a.activation(q_mla[0:64, 2 * m:2 * m + 2, :], psum[0:64, 7, :].rearrange("p (h t) -> p h t", h=2),
                                 ACT.Copy).then_inc(q_nope, 1)
                else:
                    a.activation(q_mem[:, m - 4, :], half(7, 0), ACT.Copy).then_inc(taken["a"], 1)

            def exps(j):
                a.wait_ge(m_ready, j + 1)
                scale = (NOPE + ROPE) ** -0.5 if j in JOBS_MLA else DH ** -0.5
                for q, (src, dst) in enumerate(score_views(j)):
                    ins = a.activation(dst, src, ACT.Exp, bias=stat(j, q, 2), scale=scale, accum_out=stat(j, q, 3))
                ins.then_inc(e_ready, 1)

            def copy_pt(j):
                a.wait_ge(pt_ready, j + 1)
                if 0 < j <= JOBS_MLA[0]:
                    a.wait_ge(o_ready, j)
                elif j:
                    a.wait_ge(o_ready, j - 1)
                if j in JOBS_DIL:
                    a.activation(pt_sb.rearrange("p (g n) -> p g n", g=3), psum[:, 3:6, 0:384], ACT.Copy)\
                        .then_inc(pt_copied, 1)
                else:
                    n = 384 if j in JOBS_MLA else 512
                    a.activation(pt_sb[:, 512 * (j % 2):512 * (j % 2) + n], psum[:, 3 + j % 2, 0:n], ACT.Copy)\
                        .then_inc(pt_copied, 1)

            def out_hi(j):
                a.wait_ge(o_ready, j + 1)
                lo_p, hi_p, slot = head_rows(j)
                a.activation(act[lo_p:hi_p, slot, 0, :], psum[lo_p:hi_p, out_bank(j), 0:S], ACT.Copy)\
                    .then_inc(oh_ready, 1)

            def gate_out(j, second):
                n = gate_unit(j, second)
                ahead(n)
                product(n)
                m = n - U["gates"]
                a.activation(gates[:, m, :], gate_bank(n), ACT.Identity, bias=c1("b_gate", m))\
                    .then_inc(taken["a"], 1)

            exps(0)
            for j in range(JOBS_MEM[-1] + 1):
                if j in JOBS_DIL:
                    side_out(j, 0)
                    copy_pt(j)
                if j < JOBS_MEM[-1]:
                    exps(j + 1)
                if j in JOBS_DIL:
                    side_out(j, 1)
                else:
                    gate_out(j, 0)
                    copy_pt(j)
                    gate_out(j, 1)
                out_hi(j)
                if (j - JOBS_MLA[0]) % 4 == 3 and j not in JOBS_DIL:
                    n = gate_unit(j, 1)
                    m = n - U["gates"] + 1
                    a.wait_ge(taken["a"], TAKEN["a"][n])
                    a.activation(gates[:, m - KD:m, :], gates[:, m - KD:m, :], ACT.Sigmoid).then_inc(gates_done, 1)
            for m in range(12):
                ahead(U["branch"] + m)
                if m >= 8:
                    j = 2 * (m - 8)
                    a.wait_ge(merge_done, m - 7)
                    a.activation(act[:, 16 + j:18 + j, 0, :], merged[:, j:j + 2, :], ACT.Copy).then_inc(mh_done, 1)

            def k_major(name, count, norm):
                for m in range(count):
                    ahead(U[name] + m)
                product(U[name] + count - 1)
                for b in range(4):
                    a.activation(sq[:, 2 * b:2 * b + 2, :], bank(4 + b).rearrange("p (h t) -> p h t", h=2),
                                 ACT.Square).then_inc(sq_done, 1)
                norm_std(norm, KD, at=0)

            k_major("wo", 8, N_MIX)
            residual_square(N_FFN, 0)
            norm_std(N_FFN, KD)
            norm_hi(N_FFN, KD, 16, tn)

            def warm(turn):
                a.wait_ge(warmed, turn)
                a.activation(tiny[:, 6:7], eps, ACT.Silu).then_inc(warmed, 1)

            def up_turn(i, turns, first, direct):
                loops = ((i, 4, turns),)
                warm(i + (first + 1))

                def high(p):
                    wait(prod_done, i * 2 + (2 * first + p + 1))
                    dst = act[:, bass.ds(i * 2 + (2 * first + p), 1), 0, :] if direct else \
                        late[:, bass.ds(i * 2 + (2 * first - 16 + p), 1), :]
                    a.activation(dst.rearrange("p a n -> p (a n)"), z_up[:, 2 * p + 1, :], ACT.Copy)\
                        .then_inc(ah_done, 1)

                for r in range(4):
                    n = U["up"] + 4 * first + r
                    if r < 3:
                        ahead(n, loops)
                    product(n, loops)
                    if r % 2 == 0 and direct:
                        wait(z_free, i * 2 + (1 + r // 2))
                    elif r % 2 == 0:
                        wait(ah_done, i * 2 + (2 * first - 1 + r // 2))
                    a.activation(z_up[:, r, :], half(n % 4, 0), ACT.Identity,
                                 bias=c1("conv_b", i * 4 + (4 * first + r)),
                                 scale=c1("conv_w", i * 4 + (4 * first + r + 2 * 2 * KF))).then_inc(z_init, 1)
                    if r % 2:
                        taken_at(a, n - 1, loops)
                        a.activation(z_up[:, r - 1, :], z_up[:, r - 1, :], ACT.Silu).then_inc(silu_done, 1)
                    if r == 2:
                        high(0)
                ahead(n, loops)
                high(1)

            a.activation(tiny[:, 6:7], eps, ACT.Silu).then_inc(warmed, 1)
            with a.Fori(0, 8) as i:
                up_turn(i, 8, 0, True)
            a.wait_ge(z_free, 2 + 16)
            with a.Fori(0, 3) as i:
                up_turn(i, 3, 8, False)
            a.wait_ge(unit_used, U["down"])
            a.wait_ge(ah_done, KF)
            for t in range(3):
                a.activation(act[:, 16 + 2 * t:18 + 2 * t, 0, :], late[:, 2 * t:2 * t + 2, :], ACT.Copy)\
                    .then_inc(ah_done, 1)
            k_major("down", KF, N_FFN_OUT)

            with a.Fori(0, LAYERS) as lay:
                L = (lay, PER_LAYER, LAYERS)
                for m in range(3):
                    hi(LAYER0 + m, (L,))
                residual_square(lay + N_LAYER, lay + 1)
                norm_std(N_LAYER, KD, lay)
                for j in range(KD):
                    wait(tn_done, lay * KD + (SPLIT_BEFORE[N_LAYER] + j + 1))
                    a.activation(act[:, 16 + j, 0, :], tn[:, j, :], ACT.Identity,
                                 bias=mod[:, bass.ds(lay * 24 + j, 1)]).then_inc(nh_done, 1)
                a.wait_ge(par2_in_s, lay * 16 + 16)
                a.wait_ge(sp_done, lay * 2 + 1)
                a.activation(t8[0], t8[0], ACT.Exp, scale=-1.0).then_inc(sp_exp, 1)
                with a.Fori(0, 2) as i:
                    loops = (L, (i, 4, 2))
                    for r in range(4):
                        n = U["conv"] + r
                        ahead(n, loops)
                        product(n, loops)
                        a.activation(u_rg[:, bass.ds(i * 4 + r, 1), :].rearrange("p a n -> p (a n)"),
                                     half(n % 4, 0), ACT.Identity,
                                     bias=par2[:, bass.ds(i * 4 + (C2["rg_b"][0] + r), 1)],
                                     scale=par2[:, bass.ds(i * 4 + (C2["rg_w"][0] + 3 * KD + r), 1)])\
                            .then_inc(z_init, 1)
                a.wait_ge(nl_done, lay * KD + SPLIT_BEFORE[N_LAYER + 1])
                with a.Fori(0, 2) as i:
                    loops = (L, (i, 4, 2))
                    for r in range(4):
                        n = U["conv"] + 8 + r
                        ahead(n, loops)
                        product(n, loops)
                        a.activation(xm[:, bass.ds(i * 4 + r, 1), :].rearrange("p a n -> p (a n)"),
                                     half(n % 4, 0), ACT.Copy)
                        a.activation(xc[:, bass.ds(i * 4 + r, 1), :].rearrange("p a n -> p (a n)"),
                                     half(n % 4, 0), ACT.Identity,
                                     bias=par2[:, bass.ds(i * 4 + (C2["ml_b"][0] + r), 1)],
                                     scale=par2[:, bass.ds(i * 4 + (C2["ml_w"][0] + 3 * KD + r), 1)])\
                            .then_inc(z_init, 1)
                def rg_gate(name, dst, bias):
                    product(U[name], (L,))
                    for h in range(HR):
                        ins = a.activation(dst(h), half(4 + h // 2, h % 2), ACT.Sigmoid, bias=c2(bias, h))
                    ins.then_inc(taken["a"], 1)

                def split_high(slot, src, h):
                    a.activation(act[:, slot + 4 * h:slot + 4 * h + 4, 0, :], src[:, 4 * h:4 * h + 4, :], ACT.Copy)\
                        .then_inc(xs_hi, 1)

                def z_tile(m):
                    n = Z_UNITS[m]
                    ahead(n, (L,))
                    product(n, (L,))
                    a.activation(zy[:, m, :], half(n % 4, 0), ACT.Silu).then_inc(taken["a"], 1)

                taken_at(a, U["conv"] + 7, (L,))
                split_high(8, u_rg, 0)
                z_tile(0)
                split_high(8, u_rg, 1)
                taken_at(a, U["conv"] + 15, (L,))
                z_tile(1)
                split_high(0, xm, 0)
                z_tile(2)
                split_high(0, xm, 1)
                a.activation(xc[:], xc[:], ACT.Silu).then_inc(xc_silu, 1)
                z_tile(3)
                ahead(U["rg_i"], (L,))
                rg_gate("rg_i", lambda h: rg_i[h // 4][:, h % 4, :], "b_x")
                z_tile(4)
                ahead(U["rg_r"], (L,))
                rg_gate("rg_r", lambda h: rg_r[:, h, :], "b_a")
                a.wait_ge(xc_silu, lay + 1)
                split_high(8, xc, 0)
                z_tile(5)
                split_high(8, xc, 1)
                z_tile(6)
                z_tile(7)
                a.wait_ge(taken["a"], lay * LAYER_A + TAKEN["a"][U["rg_r"]])
                a.wait_ge(sp_done, lay * 2 + 2)
                for h in range(HR):
                    ins = a.activation(rg_t[:, h, :], rg_r[:, h, :], ACT.Tanh, scale=soft[:, h:h + 1])
                ins.then_inc(rg_tanh, 1)
                a.wait_ge(rg_tanh, lay + 1)
                for q in range(2):
                    n = U["mlq"] + q
                    ahead(n, (L,))
                    product(n, (L,))
                    for b in range(2):
                        ins = a.activation(q_ml[:, 4 * q + 2 * b:4 * q + 2 * b + 2, :],
                                           bank(4 + 2 * q + b).rearrange("p (h t) -> p h t", h=2), ACT.Copy)
                    ins.then_inc(taken["a"], 1)
                for h in range(HR):
                    ins = a.activation(rg_r[:, h, :], rg_r[:, h, :], ACT.Exp, scale=nsoft[:, h:h + 1])
                ins.then_inc(rg_exp, 1)
                for q in range(2):
                    ahead(U["mlk"] + q, (L,))
                for q in range(2):
                    n = U["mlv"] + q
                    ahead(n, (L,))
                    product(n, (L,))
                    if q == 0:
                        a.wait_ge(rg_arg, lay * 2 + 1)
                    for b in range(2):
                        ins = a.activation(v_ml[:, 4 * q + 2 * b:4 * q + 2 * b + 2, :],
                                           bank(4 + 2 * q + b).rearrange("p (h t) -> p h t", h=2), ACT.Copy)
                    ins.then_inc(taken["a"], 1)

                def late_tile(m):
                    n = U["late"] + m
                    tile = LATE_TILES[m]
                    ahead(n, (L,))
                    product(n, (L,))
                    if tile < KD:
                        ins = a.activation(zy[:, KD + tile, :], half(n % 4, 0), ACT.Silu)
                    else:
                        ins = a.activation(so[:, tile - KD, :], half(n % 4, 0), ACT.Sigmoid)
                    ins.then_inc(taken["a"], 1)

                def v_tokens(*which):
                    for q in which:
                        a.wait_ge(vt_ready, lay * 4 + (q + 1))
                        a.activation(v_tok[:, q // 2, (q % 2) * 512:(q % 2 + 1) * 512], bank(4 + q % 2), ACT.Copy)\
                            .then_inc(vt_copied, 1)

                late_tile(0)
                a.wait_ge(f_abs, lay + 1)
                a.activation(row[2], row[2], ACT.Exp, scale=-1.0).then_inc(f_exp, 1)
                v_tokens(0, 1)
                a.wait_ge(rg_arg, lay * 2 + 2)
                a.activation(rg_t[:], rg_t[:], ACT.Sqrt).then_inc(rg_sqrt, 1)
                late_tile(1)
                v_tokens(2, 3)
                late_tile(2)
                late_tile(3)

                def weigh(h):
                    a.wait_ge(wm_ready, lay * HL + (h + 1))
                    a.activation(w_ml[:, h % 2, 0:256], w_ml[:, h % 2, 0:256], ACT.Exp, bias=c_col[:, 0, h:h + 1])
                    a.activation(w_ml[:, h % 2, 256:384], w_ml[:, h % 2, 256:384], ACT.Exp,
                                 bias=c_col[:, 1, h:h + 1]).then_inc(we_ready, 1)
                    if h > 1:
                        a.wait_ge(cell_done, lay * HL + (h - 1))
                    a.activation(floor_ml[:, h % 2, :], half(5, 1), ACT.Exp).then_inc(floor_ready, 1)

                weigh(0)
                late_tile(4)
                a.wait_ge(yr_done, lay * 5 + 1)
                for h in range(2):
                    a.activation(act[:, 8 + 4 * h:12 + 4 * h, 0, :], zy[:, 4 * h:4 * h + 4, :], ACT.Copy)\
                        .then_inc(yh_done, 1)
                for h in range(HL):
                    late_tile(5 + 3 * h)
                    late_tile(6 + 3 * h)
                    if h + 1 < HL:
                        weigh(h + 1)
                        late_tile(7 + 3 * h)
                a.wait_ge(cell_done, lay * HL + HL)
                for h in range(HL):
                    a.activation(sq_ml[:, 2 * h:2 * h + 2, :], so[:, 2 * h:2 * h + 2, :], ACT.Square)\
                        .then_inc(hsq_done, 1)
                for m in range(3):
                    ahead(U["out"] + m, (L,))
                for h in range(HL):
                    a.wait_ge(hss_done, lay * HL + (h + 1))
                    a.activation(sq_ml[:, 2 * h, :], half(4 + h, 0), ACT.Sqrt, bias=eps, scale=1.0 / 256)\
                        .then_inc(hstd_done, 1)
                for h in range(HL):
                    a.wait_ge(yr_done, lay * 5 + (h + 2))
                    a.activation(act[:, 2 * h:2 * h + 2, 0, :], zy[:, 8 + 2 * h:10 + 2 * h, :], ACT.Copy)\
                        .then_inc(yh_done, 1)
                    ahead(U["out"] + 3 + h, (L,))
                for m in range(7, 13):
                    ahead(U["out"] + m, (L,))
            residual_square(N_FINAL, LAYERS + 1)
            norm_std(N_FINAL, KD)

        @block.vector
        def _(v):
            step = Step(v, dve_step)
            link = step.link

            def lo(n, loops=()):
                v.wait_ge(hi_done, unit_of(n + 1, loops))
                r = n % SLOTS
                v.tensor_tensor(w_lo[:, r, :], raw[:, r, :], w_hi[:, r, :].bitcast(F32), ALU.subtract)\
                    .then_inc(lo_done, 1)

            def ahead(n, loops=()):
                if n + 3 not in FIRST_UNITS:
                    lo(n + 3, loops)

            def act_lo(slot, src, count=1):
                return v.tensor_tensor(act[:, slot:slot + count, 1, :], src,
                                       act[:, slot:slot + count, 0, :].bitcast(F32), ALU.subtract)

            def norm_rstd(n):
                v.wait_ge(std_done, n + 1)
                ins = v.reciprocal(rstd, std)
                ins.then_inc(rstd_done, 1)
                v.wait_ge(rstd_done, n + 1)

            def norm_split(n, k, src, gain, dst, slot, between=None):
                norm_rstd(n)
                if between:
                    between()
                for j in range(k + 1):
                    if j < k:
                        v.scalar_tensor_tensor(out=dst[:, j, :], in0=src[:, j, :], scalar=gain(j), in1=rstd,
                                               op0=ALU.mult, op1=ALU.mult).then_inc(tn_done, 1)
                    if j:
                        v.wait_ge(nh_done, SPLIT_BEFORE[n] + j)
                        act_lo(slot + j - 1, dst[:, j - 1:j, :]).then_inc(nl_done, 1)

            def norm_add(n, gain):
                norm_rstd(n)
                for c in range(PAIRS + 1):
                    if c < PAIRS:
                        for j in (2 * c, 2 * c + 1):
                            ins = v.scalar_tensor_tensor(out=tn[:, j, :], in0=half(4 + c, j % 2), scalar=gain(j),
                                                         in1=rstd, op0=ALU.mult, op1=ALU.mult)
                        ins.then_inc(dve_step, 1)
                        step.n += 1
                    if c:
                        v.wait_ge(dve_step, step.n - (c < PAIRS))
                        v.tensor_tensor(x[:, 2 * c - 2:2 * c, :], x[:, 2 * c - 2:2 * c, :], tn[:, 2 * c - 2:2 * c, :],
                                        ALU.add).then_inc(res_done, 1)

            link(v.memset(tiny[:], 0.0))
            v.memset(eps, EPS).then_inc(tables_done, 1)
            v.wait_ge(par_in, 16)
            norm_split(N_MEM, KD, memx, lambda j: c1("g_mem", j), tn, 0, between=lambda: lo(0))
            lo(1)
            lo(2)
            ahead(U["memk"])
            norm_split(N_X, KD, x, lambda j: c1("g_pre_mix", j), ar_g[:, 8:16, :], 16)
            ahead(U["memk"] + 1)
            ahead(U["memk"] + 2)

            two_pi = 2 * np.pi
            part1 = 6.28125
            part2 = float(np.float32(round((two_pi - part1) * 2 ** 22) / 2 ** 22))
            part3 = two_pi - part1 - part2
            magic = 1.5 * 2 ** 23
            ang, turn = rope_tmp[:, 0, :], rope_tmp[:, 1, :]
            v.wait_ge(pos_in_s, 16)
            link(v.tensor_scalar(ang, ar_g[:, 20, :].bitcast(I32), c1("freq"), None, ALU.mult))
            link(v.tensor_scalar(turn, ang, 1.0 / two_pi, magic, ALU.mult, ALU.add))
            link(v.tensor_scalar(turn, turn, magic, None, ALU.subtract))
            for part in (part1, part2, part3):
                link(v.scalar_tensor_tensor(out=ang, in0=turn, scalar=-part, in1=ang, op0=ALU.mult, op1=ALU.add))
            v.tensor_scalar(ang, ang, 3.1415925, -3.1415925, ALU.min, ALU.max).then_inc(angle_done, 1)

            ahead(U["memk"] + 3)
            ahead(U["memv"])
            v.wait_ge(masks_done, 1)
            di = dist[:, 0, :].bitcast(I32)
            tmp = flat(ar_d[:, 32:34, :])[:, 0:384]
            for g in (1, 2):
                dg = dist[:, g, :]
                link(v.tensor_scalar(dg.bitcast(I32), di, DILATION[g] - 1, None, ALU.bitwise_and))
                link(v.tensor_scalar(dg, dg.bitcast(I32), 0.0, 1.0, ALU.is_equal, ALU.subtract))
                link(v.scalar_tensor_tensor(out=dg, in0=dg, scalar=-300 * NEG, in1=di, op0=ALU.mult,
                                            op1=ALU.subtract))
                link(v.tensor_tensor(dg, dg, causal[:], ALU.add))
                ahead(U["memv"] + g)
            link(v.tensor_scalar(tmp, di, float(SPAN), 300 * NEG, ALU.is_gt, ALU.mult))
            link(v.scalar_tensor_tensor(out=tmp, in0=di, scalar=-1.0, in1=tmp, op0=ALU.mult, op1=ALU.add))
            link(v.tensor_tensor(dist[:, 0, :], tmp, causal[:], ALU.add))
            v.wait_ge(sine_done, 2)
            link(v.tensor_tensor(cos_t[64:96, :], cos_t[64:96, :], cos_t[64:96, :], ALU.mult))
            link(v.tensor_scalar(cos_t[64:96, :], cos_t[64:96, :], -2.0, 1.0, ALU.mult, ALU.add))
            link(v.tensor_scalar(sin_t[96:128, :], sin_t[96:128, :], par1[96:128, C1["sign"][0]:C1["sign"][0] + 1],
                                 None, ALU.mult))

            def modulation(k, slot, value):
                v.wait_ge(ada_in[slot], value)
                v.scalar_tensor_tensor(out=ada[:, slot, :], in0=ada[:, slot, :], scalar=1.0, in1=cact,
                                       op0=ALU.mult, op1=ALU.mult,
                                       accum_out=mod[:, k:k + 1] if isinstance(k, int) else mod[:, bass.ds(k, 1)])\
                    .then_inc(ada_used, 1)

            ahead(U["memv"] + 3)
            v.wait_ge(cact_done, 1)
            for n in range(U["latent"], U["latent"] + 6):
                ahead(n)
                if n - U["latent"] in range(3):
                    modulation(n - U["latent"], n - U["latent"], 16)

            def rotate(dst, src_bank, m):
                link(v.tensor_tensor(rope_tmp[64:96, m, :], psum[96:128, src_bank, m * S:(m + 1) * S],
                                     sin_t[96:128, :], ALU.mult))
                ins = v.tensor_tensor(dst, psum[64:96, src_bank, m * S:(m + 1) * S], cos_t[64:96, :], ALU.mult)
                return ins

            n = U["latent"] + 5
            v.wait_ge(unit_used, n + 1)
            k_rot = ar_g[64:96, 16, :]
            rotate(k_rot, n % 4, 0).then_inc(taken["v"], 1)
            v.wait_ge(taken["v"], TAKEN["v"][n])
            link(v.tensor_tensor(k_rot, k_rot, rope_tmp[64:96, 0, :], ALU.add))
            norm_split(N_CQ, KQ, latent[:, 0:KQ, :], lambda j: c1("q_norm", j), ar_g[:, 10:13, :], 8)
            norm_split(N_CKV, KKV, latent[:, KQ:5, :], lambda j: c1("kv_norm", j), ar_g[:, 13:15, :], 11)

            with v.Fori(0, 6) as i:
                for r in range(4):
                    ahead(U["qk"] + r, ((i, 4, 6),))
                    for s in ADA_BETWEEN[r]:
                        modulation(i * 6 + (3 + s), s % 3, i * 32 + 16 * (s // 3 + 2))
            with v.Fori(0, 3) as i:
                for r in range(4):
                    ahead(U["v"] + r, ((i, 4, 3),))
                    if r < 3:
                        modulation(i * 3 + (39 + r), r, i * 16 + (13 * 16 + 16))
            v.wait_ge(ada_used, 24 * LAYERS)
            v.tensor_tensor(mod[:], mod[:], c1("b_ada", 0, 24 * LAYERS), ALU.add).then_inc(mod_done, 1)
            v.tensor_copy(k_mla[64:96, :, :], k_rot.unsqueeze(1).to_broadcast([32, 8, S])).then_inc(k_pe_done, 1)
            ahead(U["ukvk"])
            ahead(U["ukvv"])

            def side(j, second):
                n = side_unit(j, second)
                ahead(n)
                m = n - U["uq"]
                if m >= 4:
                    return
                v.wait_ge(q_nope, m + 1)
                for h in range(2):
                    dst = q_mla[64:96, 2 * m + h, :]
                    ins = rotate(dst, 7, h)
                    if h:
                        ins.then_inc(taken["v"], 1)
                        v.wait_ge(taken["v"], TAKEN["v"][n])
                    else:
                        link(ins)
                    ins = v.tensor_tensor(dst, dst, rope_tmp[64:96, h, :], ALU.add)
                ins.then_inc(rope_done, 1)

            def maxima(j):
                v.wait_ge(s_ready, j + 1)
                s = s_sb[:, j % 2, :]
                scale = (NOPE + ROPE) ** -0.5 if j in JOBS_MLA else DH ** -0.5
                if j in JOBS_MLA:
                    link(v.tensor_tensor(s[:, 0:384], psum[:, j % 2, 0:384], causal[:], ALU.add))
                elif j in JOBS_DIL:
                    for g in range(GROUPS):
                        slope = 2.0 ** (-8.0 * (j * GROUPS + g + 1) / (GROUPS * HD))
                        ins = v.scalar_tensor_tensor(out=s[:, 384 * g:384 * g + 384], in0=dist[:, g, :],
                                                     scalar=slope / scale, in1=psum[:, g, 0:384], op0=ALU.mult,
                                                     op1=ALU.add)
                    link(ins)
                for q, (src, _) in enumerate(score_views(j)):
                    ins = v.tensor_reduce(stat(j, q, 0), src, AX.XY if j in JOBS_DIL else AX.X, ALU.max,
                                          negate=True)
                link(ins)
                v.tensor_scalar(stat(j, None, 2), stat(j, None, 0), scale, None, ALU.mult).then_inc(m_ready, 1)

            def normalise(j):
                v.wait_ge(e_ready, j + 1)
                link(v.reciprocal(stat(j, None, 1), stat(j, None, 3)))
                for q, (_, p) in enumerate(score_views(j)):
                    ins = v.tensor_scalar(p, p, stat(j, q, 1), None, ALU.mult)
                ins.then_inc(p_ready, 1)

            def out_lo(j):
                v.wait_ge(oh_ready, j + 1)
                lo_p, hi_p, slot = head_rows(j)
                v.tensor_tensor(act[lo_p:hi_p, slot, 1, :], psum[lo_p:hi_p, out_bank(j), 0:S],
                                act[lo_p:hi_p, slot, 0, :].bitcast(F32), ALU.subtract).then_inc(ol_ready, 1)

            maxima(0)
            for j in range(JOBS_MEM[-1] + 1):
                normalise(j)
                if j in JOBS_DIL:
                    side(j, 0)
                if j < JOBS_MEM[-1]:
                    maxima(j + 1)
                if j in JOBS_DIL:
                    side(j, 1)
                else:
                    ahead(gate_unit(j, 0))
                    ahead(gate_unit(j, 1))
                out_lo(j)

            for b in range(3):
                for q in range(4):
                    n = U["branch"] + 4 * b + q
                    ahead(n)
                    v.wait_ge(unit_used, n + 1)
                    y = bank(n % 4).rearrange("p (h t) -> p h t", h=2)
                    g = gates[:, 8 * b + 2 * q:8 * b + 2 * q + 2, :]
                    m = merged[:, 2 * q:2 * q + 2, :]
                    dst = m if b == 0 else branch_y[:, 2 * (q % 2):2 * (q % 2) + 2, :]
                    if q == 0:
                        v.wait_ge(gates_done, b + 1)
                    v.tensor_tensor(dst, y, g, ALU.mult).then_inc(taken["v"], 1)
                    if b:
                        v.wait_ge(taken["v"], TAKEN["v"][n])
                        ins = v.tensor_tensor(m, m, dst, ALU.add)
                        if b == 1:
                            ins.then_inc(dve_step, 1)
                            step.n += 1
                        else:
                            ins.then_inc(merge_done, 1)
                            v.wait_ge(mh_done, q + 1)
                            act_lo(16 + 2 * q, m, 2).then_inc(merged_lo, 1)
                if b == 1:
                    v.wait_ge(dve_step, step.n)
            for m in range(8):
                ahead(U["wo"] + m)
            norm_add(N_MIX, lambda j: c1("g_post_mix", j))
            v.wait_ge(res_done, PAIRS)
            norm_split(N_FFN, KD, x, lambda j: c1("g_pre_ffn", j), tn, 16)

            def up_turn(i, turns, first, direct):
                loops = ((i, 4, turns),)

                def taps(r):
                    n = U["up"] + 4 * first + r
                    v.wait_ge(z_init, i * 4 + (4 * first + r + 1))
                    for tap, shift in ((1, 1), (0, 2)):
                        ins = v.scalar_tensor_tensor(
                            out=z_up[:, r, shift:S], in0=psum[:, n % 4, 0:S - shift],
                            scalar=c1("conv_w", i * 4 + (4 * first + r + tap * 2 * KF)),
                            in1=z_up[:, r, shift:S], op0=ALU.mult, op1=ALU.add)
                        if tap:
                            link(ins)
                        else:
                            ins.then_inc(taken["v"], 1)

                def gated(p):
                    v.wait_ge(silu_done, i * 2 + (2 * first + p + 1))
                    taken_at(v, U["up"] + 4 * first + 2 * p + 1, loops)
                    v.tensor_tensor(z_up[:, 2 * p + 1, :], z_up[:, 2 * p, :], z_up[:, 2 * p + 1, :], ALU.mult)\
                        .then_inc(prod_done, 1)

                def low(p):
                    if direct:
                        v.wait_ge(ah_done, i * 2 + (2 * first + p + 1))
                        slot = bass.ds(i * 2 + (2 * first + p), 1)
                        v.tensor_tensor(act[:, slot, 1, :].rearrange("p a n -> p (a n)"), z_up[:, 2 * p + 1, :],
                                        act[:, slot, 0, :].rearrange("p a n -> p (a n)").bitcast(F32),
                                        ALU.subtract).then_inc(z_free, 1)

                def split(r):
                    ahead(U["up"] + 4 * first + r, loops)

                with step.turns(i, turns, 4):
                    split(0)
                    taps(0)
                    split(1)
                    taps(1)
                    split(2)
                    gated(0)
                    taps(2)
                    low(0)
                    taps(3)
                    gated(1)
                    split(3)
                    low(1)

            v.memset(tiny[:, 5:6], 0.0).then_inc(z_free, 2)
            with v.Fori(0, 8) as i:
                up_turn(i, 8, 0, True)
            with v.Fori(0, 3) as i:
                up_turn(i, 3, 8, False)
            for t in range(3):
                v.wait_ge(ah_done, KF + t + 1)
                act_lo(16 + 2 * t, late[:, 2 * t:2 * t + 2, :], 2).then_inc(al_done, 1)
            for m in range(KF):
                ahead(U["down"] + m)
            norm_add(N_FFN_OUT, lambda j: c1("g_post_ffn", j))

            def log1p(dst, e, t, q, poly):
                link(v.tensor_scalar(t, e, 2.0, None, ALU.add))
                link(v.reciprocal(t, t))
                link(v.tensor_tensor(e, e, t, ALU.mult))
                link(v.tensor_tensor(q, e, e, ALU.mult))
                link(v.tensor_scalar(poly, q, 1.0 / 17, None, ALU.mult))
                for d in (15, 13, 11, 9, 7, 5, 3):
                    link(v.scalar_tensor_tensor(out=poly, in0=poly, scalar=1.0 / d, in1=q, op0=ALU.add,
                                                op1=ALU.mult))
                link(v.tensor_scalar(poly, poly, 1.0, 2.0, ALU.add, ALU.mult))
                link(v.tensor_tensor(dst, poly, e, ALU.mult))

            LINKS = 97
            with v.Fori(0, LAYERS) as lay, step.turns(lay, LAYERS, LINKS):
                L = (lay, PER_LAYER, LAYERS)
                for m in range(3):
                    lo(LAYER0 + m, (L,))
                v.wait_ge(par2_in_s, lay * 16 + 16)
                v.scalar_tensor_tensor(out=t8[0], in0=c2("lam", 0, KD), scalar=-1.0, in1=c2("lam", 0, KD),
                                       op0=ALU.mult, op1=ALU.max).then_inc(sp_done, 1)
                at = lay * 24 + KD
                v.wait_ge(res_done, lay * PAIRS + 2 * PAIRS)
                v.scalar_tensor_tensor(out=gain2, in0=mod[:, bass.ds(at, KD)], scalar=1.0,
                                       in1=c2("norm_g", 0, KD), op0=ALU.add, op1=ALU.mult).then_inc(dve_step, 1)
                step.n += 1
                v.wait_ge(std_done, lay + (N_LAYER + 1))
                v.reciprocal(rstd, std).then_inc(rstd_done, 1)
                v.wait_ge(rstd_done, lay + (N_LAYER + 1))
                for j in range(KD + 1):
                    if j < KD:
                        v.scalar_tensor_tensor(out=tn[:, j, :], in0=x[:, j, :], scalar=gain2[:, j:j + 1],
                                               in1=rstd, op0=ALU.mult, op1=ALU.mult).then_inc(tn_done, 1)
                    if j:
                        v.wait_ge(nh_done, lay * KD + (SPLIT_BEFORE[N_LAYER] + j))
                        v.scalar_tensor_tensor(out=act[:, 16 + j - 1, 1, :], in0=tn[:, j - 1, :],
                                               scalar=mod[:, bass.ds(lay * 24 + (j - 1), 1)],
                                               in1=act[:, 16 + j - 1, 0, :].bitcast(F32), op0=ALU.add,
                                               op1=ALU.subtract).then_inc(nl_done, 1)
                def split(which, slot, src, halves=(0, 1)):
                    for h in halves:
                        v.wait_ge(xs_hi, lay * 6 + (2 * which + h + 1))
                        act_lo(slot + 4 * h, src[:, 4 * h:4 * h + 4, :], 4).then_inc(xs_lo, 1)

                for part, (dst, w) in enumerate(((u_rg, "rg_w"), (xc, "ml_w"))):
                    with v.Fori(0, 2) as i, step.turns(i, 2, 8):
                        loops = (L, (i, 4, 2))
                        for r in range(4):
                            n = U["conv"] + 8 * part + r
                            ahead(n, loops)
                            v.wait_ge(z_init, lay * 16 + (i * 4 + (2 * KF + 8 * part + r + 1)))
                            for shift in (1, 2, 3):
                                at = i * 4 + (C2[w][0] + (3 - shift) * KD + r)
                                tile = dst[:, bass.ds(i * 4 + r, 1), shift:S].rearrange("p a n -> p (a n)")
                                ins = v.scalar_tensor_tensor(out=tile, in0=psum[:, n % 4, 0:S - shift],
                                                             scalar=par2[:, bass.ds(at, 1)], in1=tile,
                                                             op0=ALU.mult, op1=ALU.add)
                                if shift < 3:
                                    link(ins)
                                else:
                                    ins.then_inc(taken["v"], 1)

                def z_ahead(m):
                    ahead(Z_UNITS[m], (L,))

                split(0, 8, u_rg, (0,))
                z_ahead(0)
                split(0, 8, u_rg, (1,))
                z_ahead(1)
                split(1, 0, xm, (0,))
                z_ahead(2)
                split(1, 0, xm, (1,))
                z_ahead(3)
                ahead(U["rg_i"], (L,))
                z_ahead(4)
                v.wait_ge(taken["a"], lay * LAYER_A + TAKEN["a"][U["rg_i"]])
                for h in range(2):
                    ins = v.tensor_tensor(rg_i[h], rg_i[h], u_rg[:, 4 * h:4 * h + 4, :], ALU.mult)
                ins.then_inc(rg_arg, 1)
                ahead(U["rg_r"], (L,))
                split(2, 8, xc, (0,))
                z_ahead(5)
                split(2, 8, xc, (1,))
                z_ahead(6)
                v.wait_ge(sp_exp, lay + 1)
                log1p(t8[1], t8[0], t8[2], t8[3], t8[1])
                link(v.tensor_scalar(t8[2], c2("lam", 0, KD), -1.0, 0.0, ALU.mult, ALU.max))
                link(v.tensor_tensor(t8[1], t8[1], t8[2], ALU.add))
                link(v.tensor_scalar(soft, t8[1], RG_C, None, ALU.mult))
                v.tensor_scalar(nsoft, t8[1], -RG_C, None, ALU.mult).then_inc(sp_done, 1)
                z_ahead(7)
                for q in range(2):
                    ahead(U["mlq"] + q, (L,))
                for q in range(2):
                    n = U["mlk"] + q
                    ahead(n, (L,))
                    v.wait_ge(unit_used, unit_of(n + 1, (L,)))
                    for b in range(2):
                        ins = v.tensor_copy(k_ml[:, 4 * q + 2 * b:4 * q + 2 * b + 2, :],
                                            bank(2 * q + b).rearrange("p (h t) -> p h t", h=2))
                    ins.then_inc(taken["v"], 1)
                for q in range(2):
                    ahead(U["mlv"] + q, (L,))
                v.wait_ge(rg_exp, lay + 1)
                link(v.tensor_tensor(rg_sq[:], rg_r[:], rg_r[:], ALU.mult))
                v.scalar_tensor_tensor(out=flat(rg_t), in0=flat(rg_sq), scalar=1.0, in1=flat(rg_t), op0=ALU.add,
                                       op1=ALU.mult).then_inc(rg_arg, 1)
                def late_ahead(m):
                    ahead(U["late"] + m, (L,))

                v.wait_ge(gt_ready, lay + 1)
                v.tensor_scalar(gate_rows, psum[0:2 * HL, GATE_ROWS_BANK, 0:S], c2("b_if")[0:2 * HL, :], None, ALU.add)\
                    .then_inc(gt_done, 1)
                late_ahead(0)
                li, f, e, t, q = row
                v.wait_ge(gr_ready, lay + 1)
                link(v.tensor_copy(f, psum[0:HL, 6, 0:S]))
                v.scalar_tensor_tensor(out=e, in0=f, scalar=-1.0, in1=f, op0=ALU.mult, op1=ALU.max)\
                    .then_inc(f_abs, 1)
                v.wait_ge(f_exp, lay + 1)
                poly = neg_row[:, 0:S]
                log1p(e, e, t, q, poly)
                late_ahead(1)
                link(v.scalar_tensor_tensor(out=f, in0=f, scalar=0.0, in1=e, op0=ALU.min, op1=ALU.subtract))
                link(v.memset(t, 1.0))
                link(v.tensor_tensor_scan(q, t, f, 0.0, ALU.mult, ALU.add))
                link(v.tensor_tensor(li, li, q, ALU.subtract))
                link(v.tensor_tensor_scan(f, t, li, 0.0, ALU.mult, ALU.max))
                v.tensor_scalar(neg_row[:, 0:S], f, -1.0, None, ALU.mult)
                v.scalar_tensor_tensor(out=neg_row[:, S:2 * S], in0=f, scalar=-1.0, in1=q, op0=ALU.mult,
                                       op1=ALU.subtract).then_inc(rows_done, 1)
                def decay(h):
                    v.wait_ge(mb_ready, lay * HL + (h + 1))
                    v.tensor_tensor(w_ml[:, h % 2, 0:256], half(5, 0), causal_t[:, 0:256], ALU.add)
                    v.tensor_tensor(w_ml[:, h % 2, 256:384], psum[:, 5, 128:256], causal_t[:, 256:384],
                                    ALU.add).then_inc(wm_ready, 1)

                late_ahead(2)
                v.wait_ge(rg_sqrt, lay + 1)
                for h in range(2):
                    ins = v.tensor_tensor(rg_i[h], rg_i[h], rg_t[:, 4 * h:4 * h + 4, :], ALU.mult)
                link(ins)
                v.wait_ge(cc_ready, lay + 1)
                v.tensor_copy(small[:, 16:24], psum[:, 7, 0:8]).then_inc(cc_done, 1)
                decay(0)
                late_ahead(3)

                def decayed_scores(h):
                    v.wait_ge(st_ready, lay * HL + (h + 1))
                    v.wait_ge(we_ready, lay * HL + (h + 1))
                    v.scalar_tensor_tensor(out=sw_ml[:, h % 2, :], in0=psum[:, 4, 0:384], scalar=256 ** -0.5,
                                           in1=w_ml[:, h % 2, :], op0=ALU.mult, op1=ALU.mult)\
                        .then_inc(sw_ready, 1)

                decayed_scores(0)
                for h in range(HR):
                    ins = v.tensor_tensor_scan(rg_t[:, h, :], rg_r[:, h, :], rg_i[h // 4][:, h % 4, :], 0.0,
                                               ALU.mult, ALU.add)
                link(ins)
                v.tensor_tensor(zy[:, 0:8, :], zy[:, 0:8, :], rg_t[:], ALU.mult).then_inc(yr_done, 1)

                late_ahead(4)
                for h in range(HL):
                    late_ahead(5 + 3 * h)
                    if h:
                        decayed_scores(h)
                    if h + 1 < HL:
                        decay(h + 1)
                    late_ahead(6 + 3 * h)
                    if h == 0:
                        for half_y in range(2):
                            v.wait_ge(yh_done, lay * 6 + (half_y + 1))
                            act_lo(8 + 4 * half_y, zy[:, 4 * half_y:4 * half_y + 4, :], 4).then_inc(yl_done, 1)
                    v.wait_ge(num_ready, lay * HL + (h + 1))
                    v.wait_ge(floor_ready, lay * HL + (h + 1))
                    link(v.tensor_tensor(den_ml, half(7, 0), floor_ml[:, h % 2, :], ALU.max))
                    link(v.scalar_tensor_tensor(out=den_ml, in0=half(7, 0), scalar=-1.0,
                                                in1=den_ml, op0=ALU.mult, op1=ALU.max))
                    link(v.reciprocal(den_ml, den_ml))
                    for dv in range(2):
                        ins = v.tensor_tensor(ar_m[:, 10 + dv, :], half(6, dv), den_ml, ALU.mult)
                    link(ins)
                    taken_at(v, U["late"] + 6 + 3 * h, (L,))
                    v.tensor_tensor(so[:, 2 * h:2 * h + 2, :], so[:, 2 * h:2 * h + 2, :], ar_m[:, 10:12, :],
                                    ALU.mult).then_inc(cell_done, 1)
                    if h < 3:
                        late_ahead(7 + 3 * h)
                for m in range(3):
                    ahead(U["out"] + m, (L,))
                v.wait_ge(cell_done, lay * HL + HL)
                for h in range(HL + 1):
                    if h < HL:
                        v.wait_ge(hstd_done, lay * HL + (h + 1))
                        link(v.reciprocal(den_ml, sq_ml[:, 2 * h, :]))
                        for dv in range(2):
                            m = 2 * h + dv
                            ins = v.scalar_tensor_tensor(out=so[:, m, :], in0=so[:, m, :], scalar=c2("head_g", m),
                                                         in1=den_ml, op0=ALU.mult, op1=ALU.mult)
                        link(ins)
                        zh = zy[:, 8 + 2 * h:10 + 2 * h, :]
                        v.tensor_tensor(zh, zh, so[:, 2 * h:2 * h + 2, :], ALU.mult).then_inc(yr_done, 1)
                    if h:
                        v.wait_ge(yh_done, lay * 6 + (h + 2))
                        act_lo(2 * h - 2, zy[:, 6 + 2 * h:8 + 2 * h, :], 2).then_inc(yl_done, 1)
                        ahead(U["out"] + 2 + h, (L,))
                for m in range(7, 13):
                    ahead(U["out"] + m, (L,))
                v.wait_ge(unit_used, unit_of(U["out"] + 16, (L,)))
                for m in range(KD):
                    ins = v.scalar_tensor_tensor(out=x[:, m, :], in0=half(m // 2, m % 2),
                                                 scalar=mod[:, bass.ds(lay * 24 + (16 + m), 1)], in1=x[:, m, :],
                                                 op0=ALU.mult, op1=ALU.add)
                    if m % 2:
                        ins.then_inc(res_done, 1)
            v.wait_ge(std_done, N_FINAL + 1)
            v.reciprocal(rstd, std).then_inc(rstd_done, 1)
            v.wait_ge(rstd_done, N_FINAL + 1)
            for j in range(KD):
                v.scalar_tensor_tensor(out=tn[:, j, :], in0=x[:, j, :], scalar=c1("final_g", j), in1=rstd,
                                       op0=ALU.mult, op1=ALU.mult).then_inc(tn_done, 1)

        @block.tensor
        def _(t):
            def mm3(out_ap, wh, wl, rh, rl, start, stop):
                t.matmul(out_ap, wh, rh, start=start, stop=False, skip_group_check=True)
                t.matmul(out_ap, wh, rl, start=False, stop=False, skip_group_check=True)
                return t.matmul(out_ap, wl, rh, start=False, stop=stop, skip_group_check=True)

            def unit(n, loops=()):
                t.wait_ge(lo_done, unit_of(n + 1, loops))

            def wide(n, loops=()):
                r = n % SLOTS
                return (w_hi[:, r, :].rearrange("p (k m) -> p k m", k=8),
                        w_lo[:, r, :].rearrange("p (k m) -> p k m", k=8))

            def tile_product(n, slot, loops=(), ready=None, out_ap=None):
                unit(n, loops)
                wh, wl = wide(n)
                for k in range(KD):
                    if ready:
                        ready(k)
                    ins = mm3(out_ap or half(n % 4, 0), wh[:, k, :], wl[:, k, :], act[:, slot + k, 0, :],
                              act[:, slot + k, 1, :], k == 0, k == KD - 1)
                ins.then_inc(unit_used, 1)

            def value_pair(n, slot, loops=()):
                for u in range(2):
                    unit(n + u, loops)
                    r = (n + u) % SLOTS
                    wh = w_hi[:, r, :].rearrange("p (k m) -> p k m", k=4)
                    wl = w_lo[:, r, :].rearrange("p (k m) -> p k m", k=4)
                    for k in range(4):
                        for blk in range(2):
                            cut = slice(blk * P, blk * P + P)
                            ins = mm3(half(n % 4, blk), act[:, slot + 4 * u + k, 0, cut],
                                      act[:, slot + 4 * u + k, 1, cut], wh[:, k, :], wl[:, k, :],
                                      u == 0 and k == 0 and blk == 0, u == 1 and k == 3)
                    ins.then_inc(unit_used, 1)

            def k_product(name, count, slot, ready):
                for k in range(count):
                    n = U[name] + k
                    unit(n)
                    ready(k)
                    wh, wl = wide(n)
                    for m in range(KD):
                        ins = mm3(half(4 + m // 2, m % 2), wh[:, m, :], wl[:, m, :], act[:, slot(k), 0, :],
                                  act[:, slot(k), 1, :], k == 0 and m % 2 == 0, k == count - 1)
                    ins.then_inc(unit_used, 1)

            def norm_sum(n, tiles, k, lay=0, at=4):
                if n > N_X:
                    t.wait_ge(std_done, lay + n)
                for j in range(k):
                    if j % 2 == 0:
                        t.wait_ge(sq_done, lay * PAIRS + (SQUARES_BEFORE[n] + j // 2 + 1))
                    ins = t.matmul(half(at, 0), ones[:], tiles[:, j, :], start=j == 0, stop=j == k - 1)
                ins.then_inc(ss_done, 1)

            def split_tile(n, lay=0):
                return lambda k: t.wait_ge(nl_done, lay * KD + (SPLIT_BEFORE[n] + k + 1))

            t.wait_ge(masks_done, 1)
            norm_sum(N_MEM, sq, KD)
            norm_sum(N_X, ar_g[:, 0:8, :], KD, at=5)
            for m in range(4):
                tile_product(U["memk"] + m, 0, ready=split_tile(N_MEM) if m == 0 else None)
            for m in range(2):
                taken_at(t, U["memv"] + 2 * m - 4 + 1)
                value_pair(U["memv"] + 2 * m, 0)
            t.wait_ge(nl_done, 2 * KD)
            for m in range(6):
                taken_at(t, U["latent"] + m - 3)
                tile_product(U["latent"] + m, 16)
            norm_sum(N_CQ, ar_g[:, 5:8, :], KQ)
            norm_sum(N_CKV, ar_g[:, 8:10, :], KKV)

            taken_at(t, U["qk"] - 1)
            with t.Fori(0, 6) as i:
                loops = ((i, 4, 6),)
                for r in range(4):
                    n = U["qk"] + r
                    ring_free(t, n, loops, U["qk"])
                    tile_product(n, 16, loops)
            taken_at(t, U["v"] - 1)
            with t.Fori(0, 3) as i:
                loops = ((i, 4, 3),)
                for r in range(0, 4, 2):
                    n = U["v"] + r
                    ring_free(t, n, loops, U["v"])
                    value_pair(n, 16, loops)
            t.wait_ge(nl_done, SPLIT_BEFORE[N_CKV + 1])
            n = U["ukvk"]
            unit(n)
            wh, wl = (w[:, n % SLOTS, :].rearrange("p (k h m) -> p k h m", k=KKV, h=4) for w in (w_hi, w_lo))
            for m in range(4):
                for k in range(KKV):
                    ins = mm3(half(4 + m // 2, m % 2), wh[:, k, m, :], wl[:, k, m, :], act[:, 11 + k, 0, :],
                              act[:, 11 + k, 1, :], k == 0, k == KKV - 1)
            ins.then_inc(unit_used, 1)
            n = U["ukvv"]
            unit(n)
            wh, wl = (w[:, n % SLOTS, :].rearrange("p (k m) -> p k m", k=KKV) for w in (w_hi, w_lo))
            for blk in range(2):
                cut = slice(blk * P, blk * P + P)
                for k in range(KKV):
                    ins = mm3(bank(6 + blk), act[:, 11 + k, 0, cut], act[:, 11 + k, 1, cut], wh[:, k, :],
                              wl[:, k, :], k == 0, k == KKV - 1)
            ins.then_inc(unit_used, 1)

            def side_product(j, second):
                n = side_unit(j, second)
                taken_at(t, n - 1)
                if n >= U["memq"]:
                    tile_product(n, 16, out_ap=half(7, 0))
                    return
                unit(n)
                wh, wl = (w[:, n % SLOTS, 0:768].rearrange("p (k h m) -> p k h m", k=KQ, h=2) for w in (w_hi, w_lo))
                for h in range(2):
                    for k in range(KQ):
                        ins = mm3(half(7, h), wh[:, k, h, :], wl[:, k, h, :], act[:, 8 + k, 0, :],
                                  act[:, 8 + k, 1, :], k == 0, k == KQ - 1)
                ins.then_inc(unit_used, 1)

            def scores(j):
                if j in JOBS_MEM[2:]:
                    t.wait_ge(e_ready, j - 1)
                elif 0 < j <= JOBS_MLA[0]:
                    t.wait_ge(m_ready, j)
                elif j:
                    t.wait_ge(m_ready, j - 1)
                if j in JOBS_MLA:
                    h = j - JOBS_MLA[0]
                    q, k, b = q_mla[0:96, h, :], k_mla[0:96, h, :], j % 2
                    t.matmul(psum[:, b, 0:128], q[:, 0:128], k[:, 0:128], start=True, stop=True)
                    ins = t.matmul(psum[:, b, 128:384], q[:, 128:256], k, start=True, stop=True)
                elif j in JOBS_DIL:
                    for g in range(GROUPS):
                        h = g * HD + j
                        q, k = qk_d[:, h, :], qk_d[:, 12 + h, :]
                        t.matmul(psum[:, g, 0:128], q[:, 0:128], k[:, 0:128], start=True, stop=True)
                        ins = t.matmul(psum[:, g, 128:384], q[:, 128:256], k, start=True, stop=True)
                else:
                    h = j - JOBS_MEM[0]
                    for blk in range(2):
                        ins = t.matmul(half(j % 2, blk), q_mem[:, h, blk * P:blk * P + P], k_mem[:, h, :],
                                       start=True, stop=True)
                ins.then_inc(s_ready, 1)

            def transposes(j):
                t.wait_ge(p_ready, j + 1)
                if 0 < j <= JOBS_MLA[0]:
                    t.wait_ge(pt_copied, j)
                elif j:
                    t.wait_ge(pt_copied, j - 1)
                s = s_sb[:, j % 2, :]
                if j in JOBS_MEM:
                    for q in range(2):
                        for k in range(2):
                            ins = t.transpose(psum[:, 3 + j % 2, k * S + q * P:k * S + q * P + P],
                                              s[:, q * S + k * P:q * S + k * P + P], ident[:])
                else:
                    for g in range(GROUPS if j in JOBS_DIL else 1):
                        b = 3 + g if j in JOBS_DIL else 3 + j % 2
                        for c in range(3):
                            ins = t.transpose(psum[:, b, c * P:c * P + P],
                                              s[:, 384 * g + c * P:384 * g + c * P + P], ident[:])
                ins.then_inc(pt_ready, 1)

            def weighted(j):
                t.wait_ge(pt_copied, j + 1)
                if 0 < j <= JOBS_MLA[0]:
                    t.wait_ge(ol_ready, j)
                elif j:
                    t.wait_ge(ol_ready, j - 1)
                b = out_bank(j)
                if j in JOBS_MLA:
                    p = pt_sb[:, 512 * (j % 2):512 * (j % 2) + 384]
                    h = j - JOBS_MLA[0]
                    rows = slice(64 * (h % 2), 64 * (h % 2) + 64)
                    t.matmul(psum[rows, b, 0:256], v_mla[:, 0, 64 * h:64 * h + 64], p[:, 0:256], start=True,
                             stop=False, skip_group_check=True)
                    ins = t.matmul(psum[rows, b, 128:256], v_mla[:, 1, 64 * h:64 * h + 64], p[:, 256:384],
                                   start=False, stop=True, skip_group_check=True)
                elif j in JOBS_DIL:
                    for g in range(GROUPS):
                        h = g * HD + j
                        p = pt_sb[:, 384 * g:384 * g + 384]
                        t.matmul(psum[:, b, 0:256], v_d[:, 0, P * h:P * h + P], p[:, 0:256], start=g == 0,
                                 stop=False, skip_group_check=True)
                        ins = t.matmul(psum[:, b, 128:256], v_d[:, 1, P * h:P * h + P], p[:, 256:384],
                                       start=False, stop=g == GROUPS - 1, skip_group_check=True)
                else:
                    h = j - JOBS_MEM[0]
                    for k in range(2):
                        ins = t.matmul(psum[:, b, 0:256], v_mem[:, k, P * h:P * h + P],
                                       pt_sb[:, 512 * (j % 2) + k * S:512 * (j % 2) + k * S + S], start=k == 0,
                                       stop=k == 1)
                ins.then_inc(o_ready, 1)

            def gate_product(j, second):
                n = gate_unit(j, second)
                if j == JOBS_MLA[0]:
                    t.wait_ge(pt_copied if second else m_ready, HD)
                taken_at(t, n - 2)
                tile_product(n, 16, out_ap=gate_bank(n))

            taken_at(t, U["v"] + 11)
            scores(0)
            for j in range(JOBS_MEM[-1] + 1):
                if j in JOBS_DIL:
                    side_product(j, 0)
                if j + 1 == JOBS_MLA[0]:
                    t.wait_ge(rope_done, 4)
                elif j + 1 == JOBS_MEM[0]:
                    taken_at(t, U["memq"] + 3)
                if j < JOBS_MEM[-1]:
                    scores(j + 1)
                if j in JOBS_DIL:
                    transposes(j)
                    side_product(j, 1)
                else:
                    gate_product(j, 0)
                    transposes(j)
                    gate_product(j, 1)
                if j == JOBS_MLA[1]:
                    taken_at(t, U["memq"] + 3)
                weighted(j)
            taken_at(t, U["gates"] + 23)
            t.wait_ge(ol_ready, JOBS_MEM[-1] + 1)
            for b in range(3):
                for q in range(4):
                    n = U["branch"] + 4 * b + q
                    taken_at(t, n - 3)
                    unit(n)
                    wh, wl = (w[:, n % SLOTS, :].rearrange("p (k h m) -> p k h m", k=4, h=2) for w in (w_hi, w_lo))
                    slot = (8, 0, 4)[b]
                    for h in range(2):
                        for k in range(4):
                            ins = mm3(half(n % 4, h), wh[:, k, h, :], wl[:, k, h, :], act[:, slot + k, 0, :],
                                      act[:, slot + k, 1, :], k == 0, k == 3)
                    ins.then_inc(unit_used, 1)
            k_product("wo", 8, lambda k: 16 + k, lambda k: t.wait_ge(merged_lo, k // 2 + 1))
            norm_sum(N_MIX, sq, KD, at=0)
            norm_sum(N_FFN, sq, KD)
            with t.Fori(0, 11) as i:
                loops = ((i, 4, 11),)
                for r in range(4):
                    n = U["up"] + r
                    ring_free(t, n, loops, U["up"])
                    tile_product(n, 16, loops, split_tile(N_FFN) if r == 0 else None)
            t.wait_ge(z_free, 2 + 16)
            k_product("down", KF, lambda k: k, lambda k: k >= 16 and t.wait_ge(al_done, (k - 16) // 2 + 1))
            norm_sum(N_FFN_OUT, sq, KD, at=0)

            with t.Fori(0, LAYERS) as lay:
                L = (lay, PER_LAYER, LAYERS)
                norm_sum(N_LAYER, sq, KD, lay)
                with t.Fori(0, 4) as i:
                    loops = (L, (i, 4, 4))
                    for r in range(4):
                        n = U["conv"] + r
                        ring_free(t, n, loops, U["conv"])
                        tile_product(n, 16, loops, split_tile(N_LAYER, lay) if r == 0 else None)
                def gate_tile(n):
                    taken_at(t, n - 3, (L,))
                    tile_product(n, 16, (L,))

                def rg_gate(name):
                    n = U[name]
                    unit(n, (L,))
                    if name == "rg_i":
                        t.wait_ge(xs_lo, lay * 6 + 2)
                    else:
                        taken_at(t, U["rg_i"], (L,))
                    wh, wl = wide(n)
                    for h in range(HR):
                        ins = mm3(half(4 + h // 2, h % 2), wh[:, h, :], wl[:, h, :], act[:, 8 + h, 0, :],
                                  act[:, 8 + h, 1, :], True, True)
                    ins.then_inc(unit_used, 1)

                for n in Z_UNITS[0:4]:
                    gate_tile(n)
                rg_gate("rg_i")
                gate_tile(Z_UNITS[4])
                rg_gate("rg_r")
                for n in Z_UNITS[5:8]:
                    gate_tile(n)
                for name, slot, first in (("mlq", 8, 4), ("mlk", 8, 0), ("mlv", 0, 4)):
                    for u in range(2):
                        n = U[name] + u
                        unit(n, (L,))
                        if name == "mlq":
                            taken_at(t, U["rg_r"], (L,))
                            t.wait_ge(xs_lo, lay * 6 + 6)
                        elif name == "mlk":
                            taken_at(t, Z_UNITS[7], (L,))
                        else:
                            taken_at(t, U["mlq"] + u, (L,))
                        wh, wl = (w[:, n % SLOTS, :].rearrange("p (h k m) -> p h k m", h=2, k=2)
                                  for w in (w_hi, w_lo))
                        for h in range(2):
                            for m in range(2):
                                for k in range(2):
                                    s = slot + 4 * u + 2 * h + k
                                    ins = mm3(half(first + 2 * u + h, m), wh[:, h, k, m * P:m * P + P],
                                              wl[:, h, k, m * P:m * P + P], act[:, s, 0, :], act[:, s, 1, :],
                                              k == 0, k == 1)
                        ins.then_inc(unit_used, 1)

                def late(*which):
                    for m in which:
                        gate_tile(U["late"] + m)

                taken_at(t, U["mlk"] + 1, (L,))
                for c in range(24):
                    if c == 16:
                        taken_at(t, U["mlv"] + 1, (L,))
                    src = (q_ml, k_ml, v_ml)[c // 8]
                    ins = t.matmul(psum[0:2 * HL, GATE_ROWS_BANK, 0:S], c2("w_if", 8 * c, 8), src[:, c % 8, :],
                                   start=c == 0, stop=c == 23)
                ins.then_inc(gt_ready, 1)
                late(0)
                t.wait_ge(gt_done, lay + 1)
                t.matmul(psum[0:64, 6, 0:S], ident[0:2 * HL, HL:HL + 64], gate_rows, start=True, stop=True)\
                    .then_inc(gr_ready, 1)
                for q in range(4):
                    if q == 2:
                        late(1)
                    if q >= 2:
                        t.wait_ge(vt_copied, lay * 4 + (q - 1))
                    for c in range(4):
                        ins = t.transpose(psum[:, 4 + q % 2, c * P:c * P + P],
                                          v_ml[:, 4 * (q % 2) + c, (q // 2) * P:(q // 2) * P + P], ident[:])
                    ins.then_inc(vt_ready, 1)

                def ml_scores(h):
                    if h:
                        t.wait_ge(sw_ready, lay * HL + h)
                    for k in range(2):
                        m = 2 * h + k
                        t.matmul(psum[:, 4, 0:256], k_ml[:, m, 0:128], q_ml[:, m, :], start=k == 0,
                                 stop=False, skip_group_check=True)
                    for k in range(2):
                        m = 2 * h + k
                        ins = t.matmul(psum[:, 4, 256:384], k_ml[:, m, 128:256], q_ml[:, m, 128:256],
                                       start=False, stop=k == 1, skip_group_check=True)
                    ins.then_inc(st_ready, 1)

                def spread(h):
                    if h:
                        t.wait_ge(floor_ready, lay * HL + h)
                    t.matmul(bank(5), ident[0:HL, h:h + 1].to_broadcast([HL, P]), neg_row, start=True,
                             stop=True).then_inc(mb_ready, 1)

                late(2)
                t.wait_ge(vt_copied, lay * 4 + 4)
                ml_scores(0)
                late(3)
                t.wait_ge(rows_done, lay + 1)
                for blk in range(2):
                    ins = t.matmul(psum[:, 7, 4 * blk:4 * blk + 4], row[0][:, blk * P:blk * P + P],
                                   ident[0:HL, 0:HL], start=True, stop=True, skip_group_check=True)
                ins.then_inc(cc_ready, 1)
                spread(0)
                late(4)
                for h in range(HL):
                    late(5 + 3 * h)
                    if h + 1 < HL:
                        spread(h + 1)
                    late(6 + 3 * h)
                    t.wait_ge(sw_ready, lay * HL + (h + 1))
                    if h:
                        t.wait_ge(cell_done, lay * HL + h)
                    else:
                        t.wait_ge(cc_done, lay + 1)
                    sw = sw_ml[:, h % 2, :]
                    for dv in range(2):
                        c = 256 * h + 128 * dv
                        t.matmul(half(6, dv), v_tok[:, 0, c:c + P], sw[:, 0:256], start=dv == 0, stop=False,
                                 skip_group_check=True)
                        t.matmul(psum[:, 6, dv * S + 128:dv * S + 256], v_tok[:, 1, c:c + P],
                                 sw[:, 256:384], start=False, stop=True, skip_group_check=True)
                    t.matmul(psum[:, 7, 0:256], ones[:], sw[:, 0:256], start=True, stop=False,
                             skip_group_check=True)
                    t.matmul(psum[:, 7, 128:256], ones[:], sw[:, 256:384], start=False, stop=True,
                             skip_group_check=True).then_inc(num_ready, 1)
                    if h + 1 < HL:
                        ml_scores(h + 1)
                        late(7 + 3 * h)
                for k in range(16):
                    n = U["out"] + k
                    if k == 0:
                        taken_at(t, U["late"] + 15, (L,))
                    if k == 2:
                        t.wait_ge(cell_done, lay * HL + HL)
                        for h in range(HL):
                            t.wait_ge(hsq_done, lay * HL + (h + 1))
                            for kk in range(2):
                                ins = t.matmul(half(4 + h, 0), ones[:], sq_ml[:, 2 * h + kk, :], start=kk == 0,
                                               stop=kk == 1)
                            ins.then_inc(hss_done, 1)
                    unit(n, (L,))
                    if k in (0, 4):
                        t.wait_ge(yl_done, lay * 6 + (k // 4 + 1))
                    elif k >= 8 and k % 2 == 0:
                        t.wait_ge(yl_done, lay * 6 + (2 + (k - 8) // 2 + 1))
                    slot = (k + 8) % 16
                    wh, wl = wide(n)
                    for m in range(KD):
                        ins = mm3(half(m // 2, m % 2), wh[:, m, :], wl[:, m, :], act[:, slot, 0, :],
                                  act[:, slot, 1, :], k == 0 and m % 2 == 0, k == 15)
                    ins.then_inc(unit_used, 1)
            norm_sum(N_FINAL, sq, KD)


def _tile_columns(w):
    k, n = w.shape
    return w.reshape(k // P, P, n // P, P).transpose(2, 1, 0, 3).reshape(n // P, P, k)


def _pack_units(i):
    w_in = i["w_in"][0]
    off_kr = 640
    off_dil, off_memq, off_gate = 672, 5280, 5792
    units = []

    def put(a):
        units.append(np.ascontiguousarray(a, np.float32))

    def value_units(w):
        n = w.shape[1] // S
        put(w.reshape(2, 4, P, n, S).transpose(3, 0, 2, 1, 4).reshape(2 * n, P, UNIT))

    w_mem = i["w_mem_kv"][0]
    put(_tile_columns(w_mem[:, :512]))
    value_units(w_mem[:, 512:])
    put(_tile_columns(w_in[:, :off_kr]))
    kr = w_in[:, off_kr:off_dil]
    last = np.zeros((D, P), np.float32)
    last[:, 64:96] = kr
    last[:, 96:112] = kr[:, 16:]
    last[:, 112:128] = kr[:, :16]
    put(_tile_columns(last))
    dil = w_in[:, off_dil:off_memq]
    put(_tile_columns(dil[:, :3072]))
    value_units(dil[:, 3072:])
    uq = i["w_uq"][0].reshape(KQ, P, HM, NOPE + ROPE)
    full = np.zeros((KQ, P, HM, P), np.float32)
    full[..., :96] = uq
    full[..., 96:112] = uq[..., 80:96]
    full[..., 112:128] = uq[..., 64:80]
    uq_units = np.zeros((4, P, UNIT), np.float32)
    uq_units[:, :, :768] = full.reshape(KQ, P, 4, 2, P).transpose(2, 1, 0, 3, 4).reshape(4, P, 768)
    ukv = i["w_ukv"][0].reshape(KKV, P, HM, NOPE + VM)
    put(ukv[..., :NOPE].transpose(1, 0, 2, 3).reshape(1, P, UNIT))
    put(ukv[..., NOPE:].transpose(1, 0, 2, 3).reshape(1, P, UNIT))
    put(uq_units)
    put(_tile_columns(w_in[:, off_memq:off_gate]))
    put(_tile_columns(w_in[:, off_gate:]))
    for name in ("w_br_mla", "w_br_dil", "w_br_mem"):
        w = i[name][0]
        put(w.reshape(4, P, 4, 2, P).transpose(2, 1, 0, 3, 4).reshape(4, P, UNIT))
    put(i["w_o"][0].reshape(KD, P, D))
    up = i["w_ffn_up"][0]
    g, v = _tile_columns(up[:, :FF]), _tile_columns(up[:, FF:])
    put(np.stack([g, v], 1).reshape(2 * KF, P, UNIT))
    put(i["w_ffn_down"][0].reshape(KF, P, D))
    for lay in range(LAYERS):
        w = i["w_in_2"][lay]
        tiles = [_tile_columns(w[:, a * D:(a + 1) * D]) for a in range(5)]
        put(tiles[0])
        put(tiles[2])
        put(tiles[1][0:4])
        put(i["rg_w_x_2"][lay].transpose(1, 0, 2).reshape(1, P, UNIT))
        put(tiles[1][4:5])
        put(i["rg_w_a_2"][lay].transpose(1, 0, 2).reshape(1, P, UNIT))
        put(tiles[1][5:8])
        for name in ("ml_w_q_2", "ml_w_k_2", "ml_w_v_2"):
            put(i[name][lay].reshape(2, 2, 2, P, 256).transpose(0, 3, 1, 2, 4).reshape(2, P, UNIT))
        put(np.concatenate([tiles[4], tiles[3]])[LATE_TILES])
        put(i["w_out_2"][lay].reshape(16, P, D))
    out = np.concatenate(units)
    assert out.shape == (NU, P, UNIT), out.shape
    return out


def _col(a):
    return np.ascontiguousarray(a.reshape(-1, P).T)


def _pack_params(i):
    par1 = np.zeros((P, NP1), np.float32)

    def put(par, cols, name, a):
        at, n = cols[name]
        assert a.shape == (P, n), (name, a.shape, n)
        par[:, at:at + n] = a

    for name, key in (("g_pre_mix", "g_pre_mix"), ("g_mem", "g_mem"), ("q_norm", "mla_q_norm"),
                      ("kv_norm", "mla_kv_norm"), ("b_gate", "b_gate"), ("g_post_mix", "g_post_mix"),
                      ("g_pre_ffn", "g_pre_ffn"), ("g_post_ffn", "g_post_ffn"),
                      ("b_ada", "b_ada_2"), ("final_g", "final_g_2")):
        put(par1, C1, name, _col(i[key]))
    w = i["conv_w"][0].reshape(3, 2, KF, P).transpose(0, 2, 1, 3)
    put(par1, C1, "conv_w", _col(w))
    put(par1, C1, "conv_b", _col(i["conv_b"][0].reshape(2, KF, P).transpose(1, 0, 2)))
    half_dim = ROPE // 2
    freq = np.float32(10000.0) ** (-np.arange(half_dim, dtype=np.float32) / np.float32(half_dim))
    put(par1, C1, "freq", np.tile(freq.astype(np.float32), P // half_dim)[:, None])
    put(par1, C1, "sign", np.tile(np.repeat([-1.0, 1.0], half_dim), P // ROPE)[:, None])
    par2 = np.zeros((LAYERS, P, NP2), np.float32)
    for lay in range(LAYERS):
        for name, key in (("norm_g", "norm_g_2"), ("rg_w", "rg_conv_w_2"), ("rg_b", "rg_conv_b_2"),
                          ("b_a", "rg_b_a_2"), ("b_x", "rg_b_x_2"), ("lam", "rg_lambda_2"),
                          ("ml_w", "ml_conv_w_2"), ("ml_b", "ml_conv_b_2"), ("head_g", "ml_norm_g_2")):
            put(par2[lay], C2, name, _col(i[key][lay]))
        par2[lay, 0:2 * HL, C2["b_if"][0]] = i["ml_b_if_2"][lay]
        put(par2[lay], C2, "w_if", i["ml_w_if_2"][lay].reshape(24, P, 2 * HL).transpose(1, 0, 2).reshape(P, -1))
    return par1, par2


def kernel(**inputs):
    import concourse.bacc as bacc
    from concourse.bass_utils import run_bass_kernel_spmd

    i = {k: np.asarray(v) for k, v in inputs.items()}

    def features(a):
        return np.ascontiguousarray(a[0].T.reshape(KD, P, S).transpose(1, 0, 2))

    par1, par2 = _pack_params(i)
    arrays = {
        "w_units": _pack_units(i),
        "w_ada": np.ascontiguousarray(i["w_ada_2"].transpose(0, 2, 1).reshape(24 * LAYERS, P, D)),
        "x_in": features(i["x"]),
        "mem_in": features(i["mem"]),
        "pos_in": np.ascontiguousarray(np.broadcast_to(i["positions"].astype(np.int32), (P, S))),
        "c_in": np.ascontiguousarray(np.broadcast_to(i["c_2"], (P, D))),
        "par1_in": par1,
        "par2_in": par2,
    }
    nc = bacc.Bacc("TRN2", target_bir_lowering=False, num_devices=1)
    args = {n: nc.dram_tensor(n, a.shape, mybir.dt.from_np(a.dtype), kind="ExternalInput").ap()
            for n, a in arrays.items()}
    out = nc.dram_tensor("out", (P, KD, S), F32, kind="ExternalOutput").ap()
    program(nc, out=out, **args)
    r = run_bass_kernel_spmd(nc, [arrays], core_ids=[0])
    y = r.results[0]["out"]
    return np.ascontiguousarray(y.transpose(1, 0, 2).reshape(D, S).T)[None]
```
